# Optimizing a Trainium2 kernel written in Bass

```python
import math
import jax, jax.numpy as jnp
from jax import lax
import numpy as np

D_MODEL = 1024
BATCH = 1
SEQ = 256
DEPTH = 1

N_META = 16
A_HEADS = 4
A_DK = 64
A_DV = 2 * A_DK
B_HEADS = 4
B_DQ = 128
B_DC = 256
B_DV = 128
IDX_HEADS = 8
IDX_DIM = 64
IDX_TOPK_MAX = 256
REL_BUCKETS = 32
REL_MAX_DIST = 128
N_BIAS_HEADS = A_HEADS + B_HEADS
D_FF = 2816
Q_BLOCK = 128
EPS = 1e-6
A_SCALE = A_DK ** -0.5
B_SCALE = B_DC ** -0.5

IN_SIZES = (
    A_HEADS * 2 * A_DK,
    A_HEADS * 2 * A_DK,
    A_HEADS * A_DV,
    B_HEADS * B_DQ,
    B_DC,
    IDX_HEADS * IDX_DIM,
    IDX_DIM,
    IDX_HEADS,
)
N_IN = sum(IN_SIZES)
IN_SPLITS = [int(v) for v in np.cumsum(IN_SIZES)[:-1]]
D_MIX = A_HEADS * A_DV + B_HEADS * B_DV


def rmsnorm(x, g):
    xf = x.astype(jnp.float32)
    y = xf * lax.rsqrt(jnp.mean(xf * xf, axis=-1, keepdims=True) + EPS)
    return (y * g.astype(jnp.float32)).astype(x.dtype)

def swiglu(x, w_gate, w_up, w_down):
    return (jax.nn.silu(x @ w_gate) * (x @ w_up)) @ w_down

def rel_bucket(q_pos, k_pos):
    max_exact = REL_BUCKETS // 2
    n = jnp.maximum(q_pos - k_pos, 0)
    nf = jnp.maximum(n, 1).astype(jnp.float32)
    large = max_exact + (jnp.log(nf / max_exact) / math.log(REL_MAX_DIST / max_exact)
                         * (REL_BUCKETS - max_exact)).astype(jnp.int32)
    large = jnp.minimum(large, REL_BUCKETS - 1)
    return jnp.where(n < max_exact, n, large)

def diff_attention(q, k, v, lam, bias_a, subln_g, lam_init):
    bsz, length = q.shape[0], q.shape[1]
    outs = []
    for start in range(0, length, Q_BLOCK):
        stop = min(start + Q_BLOCK, length)
        q_pos = jnp.arange(start, stop)
        k_pos = jnp.arange(stop)
        bias = bias_a[rel_bucket(q_pos[:, None], k_pos[None, :])].transpose(2, 0, 1)
        s = jnp.einsum('bqhmd,bkhmd->bhmqk', q[:, start:stop], k[:, :stop]).astype(jnp.float32)
        s = s * A_SCALE + bias[None, :, None].astype(jnp.float32)
        s = jnp.where(k_pos[None, :] <= q_pos[:, None], s, -jnp.inf)
        p = jax.nn.softmax(s, axis=-1)
        a = p[:, :, 0] - lam * p[:, :, 1]
        outs.append(jnp.einsum('bhqk,bkhd->bqhd', a.astype(v.dtype), v[:, :stop]))
    o = jnp.concatenate(outs, axis=1)
    o = rmsnorm(o, subln_g) * (1.0 - lam_init)
    return o.reshape(bsz, length, A_HEADS * A_DV)

def dsa_attention(q_lat, c, iq, ik, iw, w_uv, bias_b, topk):
    bsz, length = q_lat.shape[0], q_lat.shape[1]
    gather = jax.vmap(lambda cb, ib: cb[ib])
    outs = []
    for start in range(0, length, Q_BLOCK):
        stop = min(start + Q_BLOCK, length)
        q_pos = jnp.arange(start, stop)
        k_pos = jnp.arange(stop)
        dots = jnp.einsum('bqhd,bkd->bqhk', iq[:, start:stop], ik[:, :stop]).astype(jnp.float32)
        w = iw[:, start:stop].astype(jnp.float32) * (IDX_HEADS ** -0.5)
        score = jnp.einsum('bqh,bqhk->bqk', w, jax.nn.relu(dots * (IDX_DIM ** -0.5)))
        score = jnp.where(k_pos[None, None, :] <= q_pos[None, :, None], score, -jnp.inf)
        _, sel = lax.top_k(score, min(topk, stop))
        valid = sel <= q_pos[None, :, None]
        g = gather(c, sel)
        bias = bias_b[rel_bucket(q_pos[None, :, None], sel)].transpose(0, 3, 1, 2)
        s = jnp.einsum('bqhc,bqkc->bhqk', q_lat[:, start:stop], g).astype(jnp.float32)
        s = s * B_SCALE + bias.astype(jnp.float32)
        s = jnp.where(valid[:, None], s, -jnp.inf)
        p = jax.nn.softmax(s, axis=-1)
        o_lat = jnp.einsum('bhqk,bqkc->bqhc', p.astype(g.dtype), g)
        outs.append(jnp.einsum('bqhc,hcd->bqhd', o_lat, w_uv))
    o = jnp.concatenate(outs, axis=1)
    return o.reshape(bsz, length, B_HEADS * B_DV)

def first_inputs(seed: int = 0) -> dict:
    key = jax.random.key(seed)
    ks = jax.random.split(key, 32)
    f32 = jnp.float32

    def nrm(k, shape, scale):
        return jax.random.normal(k, shape, f32) * scale

    def gain(k, shape):
        return 1.0 + 0.02 * jax.random.normal(k, shape, f32)

    L = DEPTH
    return {
        'x': nrm(ks[0], (BATCH, SEQ, D_MODEL), 1.0),
        'meta_tokens': nrm(ks[1], (N_META, D_MODEL), 1.0),
        'rel_bias': nrm(ks[2], (REL_BUCKETS, N_BIAS_HEADS), 0.1),
        'ffn1_norm': gain(ks[3], (L, D_MODEL)),
        'ffn1_w_gate': nrm(ks[4], (L, D_MODEL, D_FF), D_MODEL ** -0.5),
        'ffn1_w_up': nrm(ks[5], (L, D_MODEL, D_FF), D_MODEL ** -0.5),
        'ffn1_w_down': nrm(ks[6], (L, D_FF, D_MODEL), D_FF ** -0.5),
        'mix_norm': gain(ks[7], (L, D_MODEL)),
        'w_in': nrm(ks[8], (L, D_MODEL, N_IN), D_MODEL ** -0.5),
        'a_q_norm': gain(ks[9], (L, A_DK)),
        'a_k_norm': gain(ks[10], (L, A_DK)),
        'a_lambda_q1': nrm(ks[11], (L, A_DK), 0.1),
        'a_lambda_k1': nrm(ks[12], (L, A_DK), 0.1),
        'a_lambda_q2': nrm(ks[13], (L, A_DK), 0.1),
        'a_lambda_k2': nrm(ks[14], (L, A_DK), 0.1),
        'a_subln': gain(ks[15], (L, A_DV)),
        'b_kv_norm': gain(ks[16], (L, B_DC)),
        'b_w_uk': nrm(ks[17], (L, B_HEADS, B_DQ, B_DC), B_DQ ** -0.5),
        'b_q_norm': gain(ks[18], (L, B_DC)),
        'b_w_uv': nrm(ks[19], (L, B_HEADS, B_DC, B_DV), B_DC ** -0.5),
        'w_out': nrm(ks[20], (L, D_MIX, D_MODEL), D_MIX ** -0.5),
        'ffn2_norm': gain(ks[21], (L, D_MODEL)),
        'ffn2_w_gate': nrm(ks[22], (L, D_MODEL, D_FF), D_MODEL ** -0.5),
        'ffn2_w_up': nrm(ks[23], (L, D_MODEL, D_FF), D_MODEL ** -0.5),
        'ffn2_w_down': nrm(ks[24], (L, D_FF, D_MODEL), D_FF ** -0.5),
    }

def first_block(x, meta_tokens, rel_bias, ffn1_norm, ffn1_w_gate, ffn1_w_up, ffn1_w_down,
              mix_norm, w_in, a_q_norm, a_k_norm, a_lambda_q1, a_lambda_k1, a_lambda_q2,
              a_lambda_k2, a_subln, b_kv_norm, b_w_uk, b_q_norm, b_w_uv, w_out,
              ffn2_norm, ffn2_w_gate, ffn2_w_up, ffn2_w_down):
    bsz, seq = x.shape[0], x.shape[1]
    topk = min(IDX_TOPK_MAX, seq // 4)
    meta = jnp.broadcast_to(meta_tokens.astype(x.dtype)[None], (bsz, N_META, D_MODEL))
    h = jnp.concatenate([meta, x], axis=1)
    length = h.shape[1]
    bias_a = rel_bias[:, :A_HEADS]
    bias_b = rel_bias[:, A_HEADS:]

    for l in range(DEPTH):
        h = h + 0.5 * swiglu(rmsnorm(h, ffn1_norm[l]), ffn1_w_gate[l], ffn1_w_up[l], ffn1_w_down[l])

        u = rmsnorm(h, mix_norm[l]) @ w_in[l]
        qa, ka, va, qb, ckv, iq, ik, iw = jnp.split(u, IN_SPLITS, axis=-1)

        qa = rmsnorm(qa.reshape(bsz, length, A_HEADS, 2, A_DK), a_q_norm[l])
        ka = rmsnorm(ka.reshape(bsz, length, A_HEADS, 2, A_DK), a_k_norm[l])
        va = va.reshape(bsz, length, A_HEADS, A_DV)
        lam_init = 0.8 - 0.6 * math.exp(-0.3 * l)
        lam = (jnp.exp(jnp.sum(a_lambda_q1[l].astype(jnp.float32) * a_lambda_k1[l].astype(jnp.float32)))
               - jnp.exp(jnp.sum(a_lambda_q2[l].astype(jnp.float32) * a_lambda_k2[l].astype(jnp.float32)))
               + lam_init)
        o_a = diff_attention(qa, ka, va, lam, bias_a, a_subln[l], lam_init)

        qb = qb.reshape(bsz, length, B_HEADS, B_DQ)
        q_lat = rmsnorm(jnp.einsum('blhd,hdc->blhc', qb, b_w_uk[l]), b_q_norm[l])
        c = rmsnorm(ckv, b_kv_norm[l])
        iq = iq.reshape(bsz, length, IDX_HEADS, IDX_DIM)
        o_b = dsa_attention(q_lat, c, iq, ik, iw, b_w_uv[l], bias_b, topk)

        h = h + jnp.concatenate([o_a, o_b], axis=-1) @ w_out[l]

        h = h + 0.5 * swiglu(rmsnorm(h, ffn2_norm[l]), ffn2_w_gate[l], ffn2_w_up[l], ffn2_w_down[l])

    return h[:, N_META:]


DEPTH_2 = 2

CHUNK = 64

A_HEADS_2 = 8
A_NOPE = 64
A_ROPE = 32
A_VDIM = 64
A_QLORA = 256
A_KVLORA = 128
ROPE_THETA = 10000.0

B_DIM = 64

POOL_WINDOWS = (2, 4, 8, 16)
POOL_CH = 64

A_WIDTH = A_HEADS_2 * A_VDIM
B_WIDTH = B_HEADS * B_DIM
C_WIDTH = len(POOL_WINDOWS) * POOL_CH
D_MIX_2 = A_WIDTH + B_WIDTH + C_WIDTH

A_IN = A_QLORA + A_KVLORA + A_ROPE
B_IN = 3 * B_WIDTH
D_IN = A_IN + B_IN + C_WIDTH

N_GROUPS = 4
EXPERTS_PER_GROUP = 8
TOP_K_INNER = 2
D_EXPERT = 256


def rms_norm(x, g):
    xf = x.astype(jnp.float32)
    y = xf * lax.rsqrt(jnp.mean(xf * xf, axis=-1, keepdims=True) + EPS)
    return (y * g.astype(jnp.float32)).astype(x.dtype)

def rope_tables(seq):
    pos = jnp.arange(seq, dtype=jnp.float32)
    inv = ROPE_THETA ** (-jnp.arange(0, A_ROPE, 2, dtype=jnp.float32) / A_ROPE)
    ang = pos[:, None] * inv[None, :]
    return jnp.cos(ang), jnp.sin(ang)

def apply_rope(x, cos, sin):
    half = x.shape[-1] // 2
    x1 = x[..., :half].astype(jnp.float32)
    x2 = x[..., half:].astype(jnp.float32)
    out = jnp.concatenate([x1 * cos - x2 * sin, x2 * cos + x1 * sin], axis=-1)
    return out.astype(x.dtype)

def mla_mixer(c_q, c_kv, k_r, q_norm_g, w_uq, kv_norm_g, w_ukv):
    B, S, _ = c_q.shape
    cos, sin = rope_tables(S)
    q = jnp.einsum('bsr,rf->bsf', rms_norm(c_q, q_norm_g), w_uq).reshape(B, S, A_HEADS_2, A_NOPE + A_ROPE)
    q = jnp.concatenate([q[..., :A_NOPE], apply_rope(q[..., A_NOPE:], cos[None, :, None], sin[None, :, None])], axis=-1)
    kv = jnp.einsum('bsr,rf->bsf', rms_norm(c_kv, kv_norm_g), w_ukv).reshape(B, S, A_HEADS_2, A_NOPE + A_VDIM)
    k_rope = apply_rope(k_r, cos[None], sin[None])
    k = jnp.concatenate([kv[..., :A_NOPE], jnp.broadcast_to(k_rope[:, :, None, :], (B, S, A_HEADS_2, A_ROPE))], axis=-1)
    v = kv[..., A_NOPE:]
    scale = (A_NOPE + A_ROPE) ** -0.5
    chunk_id = jnp.arange(S) // CHUNK
    outs = []
    for i in range(S // Q_BLOCK):
        q0, q1 = i * Q_BLOCK, (i + 1) * Q_BLOCK
        s = jnp.einsum('bqhd,bkhd->bhqk', q[:, q0:q1], k[:, :q1]).astype(jnp.float32) * scale
        allowed = chunk_id[:q1][None, :] <= chunk_id[q0:q1][:, None]
        s = jnp.where(allowed, s, -1e30)
        p = jax.nn.softmax(s, axis=-1).astype(v.dtype)
        outs.append(jnp.einsum('bhqk,bkhd->bqhd', p, v[:, :q1]))
    return jnp.concatenate(outs, axis=1).reshape(B, S, A_WIDTH)

def stick_breaking_mixer(q, k, v):
    B, S = q.shape[0], q.shape[1]
    pos = jnp.arange(S)
    scale = B_DIM ** -0.5
    outs = []
    for i in range(S // Q_BLOCK):
        q0, q1 = i * Q_BLOCK, (i + 1) * Q_BLOCK
        z = jnp.einsum('bqhd,bkhd->bhqk', q[:, q0:q1], k[:, :q1]).astype(jnp.float32) * scale
        strict = pos[:q1][None, :] < pos[q0:q1][:, None]
        log_1m_beta = jnp.where(strict, -jax.nn.softplus(z), 0.0)
        between = lax.cumsum(log_1m_beta, axis=3, reverse=True) - log_1m_beta
        a = jnp.where(strict, jnp.exp(jax.nn.log_sigmoid(z) + between), 0.0).astype(v.dtype)
        outs.append(jnp.einsum('bhqk,bkhd->bqhd', a, v[:, :q1]))
    return jnp.concatenate(outs, axis=1).reshape(B, S, B_WIDTH)

def pool_mixer(u, pool_w, pool_scale):
    B, S, _ = u.shape
    uf = u.astype(jnp.float32)
    cs = jnp.concatenate([jnp.zeros((B, 1, C_WIDTH), jnp.float32), jnp.cumsum(uf, axis=1)], axis=1)
    pos = jnp.arange(S, dtype=jnp.float32)
    groups = []
    for g, w in enumerate(POOL_WINDOWS):
        c = cs[..., g * POOL_CH:(g + 1) * POOL_CH]
        lag = jnp.pad(c[:, :S - w + 1], ((0, 0), (w - 1, 0), (0, 0)))
        count = jnp.minimum(pos + 1.0, float(w))[None, :, None]
        mean = (c[:, 1:] - lag) / count
        groups.append(mean - uf[..., g * POOL_CH:(g + 1) * POOL_CH])
    d = jnp.stack(groups, axis=2).astype(u.dtype)
    y = jnp.einsum('bsgc,gcd->bsgd', d, pool_w).reshape(B, S, C_WIDTH)
    return y * pool_scale

def hier_moe(h, w_group, b_group, w_expert, b_expert, w_gate, w_up, w_down):
    B, S, D = h.shape
    t = h.reshape(B * S, D)
    g_prob = jax.nn.softmax((t @ w_group + b_group).astype(jnp.float32), axis=-1)
    p_sel, g_idx = lax.top_k(g_prob, 1)
    p_sel, g_idx = p_sel[:, 0], g_idx[:, 0]
    e_logits = (t @ w_expert + b_expert).astype(jnp.float32).reshape(B * S, N_GROUPS, EXPERTS_PER_GROUP)
    e_in = jnp.take_along_axis(e_logits, g_idx[:, None, None], axis=1)[:, 0]
    e_prob = jax.nn.softmax(e_in, axis=-1)
    w_k, i_k = lax.top_k(e_prob, TOP_K_INNER)
    w_k = w_k / jnp.sum(w_k, axis=-1, keepdims=True)
    inner = jnp.sum(jax.nn.one_hot(i_k, EXPERTS_PER_GROUP, dtype=jnp.float32) * w_k[..., None], axis=1)
    combine = (p_sel[:, None, None] * jax.nn.one_hot(g_idx, N_GROUPS, dtype=jnp.float32)[:, :, None]
               * inner[:, None, :]).astype(t.dtype)
    y = jnp.zeros_like(t)
    for g in range(N_GROUPS):
        a = jnp.einsum('nd,edf->nef', t, w_gate[g])
        b = jnp.einsum('nd,edf->nef', t, w_up[g])
        hid = jax.nn.silu(a) * b * combine[:, g, :, None]
        y = y + jnp.einsum('nef,efd->nd', hid, w_down[g])
    return y.reshape(B, S, D)

def hybrid_layer(x, norm1_g, w_in, q_norm_g, w_uq, kv_norm_g, w_ukv, pool_w, pool_scale, w_out,
                 norm2_g, w_group, b_group, w_expert, b_expert, w_gate, w_up, w_down):
    B, S, _ = x.shape
    hn = rms_norm(x, norm1_g)
    proj = jnp.einsum('bsd,df->bsf', hn, w_in)
    o1 = A_QLORA
    o2 = o1 + A_KVLORA
    o3 = o2 + A_ROPE
    o4 = o3 + B_IN
    ya = mla_mixer(proj[..., :o1], proj[..., o1:o2], proj[..., o2:o3], q_norm_g, w_uq, kv_norm_g, w_ukv)
    qkv_b = proj[..., o3:o4].reshape(B, S, 3, B_HEADS, B_DIM)
    yb = stick_breaking_mixer(qkv_b[:, :, 0], qkv_b[:, :, 1], qkv_b[:, :, 2])
    yc = pool_mixer(proj[..., o4:], pool_w, pool_scale)
    mixed = jnp.concatenate([ya, yb, yc], axis=-1)
    x = x + jnp.einsum('bsm,md->bsd', mixed, w_out)
    x = x + hier_moe(rms_norm(x, norm2_g), w_group, b_group, w_expert, b_expert, w_gate, w_up, w_down)
    return x

def second_inputs(seed: int = 0) -> dict:
    key = jax.random.key(seed)
    ks = jax.random.split(key, 20)
    L, D = DEPTH_2, D_MODEL

    def nrm(k, shape, fan_in):
        return jax.random.normal(k, shape, jnp.float32) * (fan_in ** -0.5)

    def gain(k, shape):
        return 1.0 + 0.02 * jax.random.normal(k, shape, jnp.float32)

    return {
        'x': jax.random.normal(ks[0], (BATCH, SEQ, D), jnp.float32),
        'norm1_g': gain(ks[1], (L, D)),
        'w_in': nrm(ks[2], (L, D, D_IN), D),
        'q_norm_g': gain(ks[3], (L, A_QLORA)),
        'w_uq': nrm(ks[4], (L, A_QLORA, A_HEADS_2 * (A_NOPE + A_ROPE)), A_QLORA),
        'kv_norm_g': gain(ks[5], (L, A_KVLORA)),
        'w_ukv': nrm(ks[6], (L, A_KVLORA, A_HEADS_2 * (A_NOPE + A_VDIM)), A_KVLORA),
        'pool_w': nrm(ks[7], (L, len(POOL_WINDOWS), POOL_CH, POOL_CH), POOL_CH),
        'pool_scale': gain(ks[8], (L, C_WIDTH)),
        'w_out': nrm(ks[9], (L, D_MIX_2, D), D_MIX_2),
        'norm2_g': gain(ks[10], (L, D)),
        'w_group': nrm(ks[11], (L, D, N_GROUPS), D),
        'b_group': 0.01 * jax.random.normal(ks[12], (L, N_GROUPS), jnp.float32),
        'w_expert': nrm(ks[13], (L, D, N_GROUPS * EXPERTS_PER_GROUP), D),
        'b_expert': 0.01 * jax.random.normal(ks[14], (L, N_GROUPS * EXPERTS_PER_GROUP), jnp.float32),
        'w_gate': nrm(ks[15], (L, N_GROUPS, EXPERTS_PER_GROUP, D, D_EXPERT), D),
        'w_up': nrm(ks[16], (L, N_GROUPS, EXPERTS_PER_GROUP, D, D_EXPERT), D),
        'w_down': nrm(ks[17], (L, N_GROUPS, EXPERTS_PER_GROUP, D_EXPERT, D), D_EXPERT),
        'final_g': gain(ks[18], (D,)),
    }

def second_block(x, norm1_g, w_in, q_norm_g, w_uq, kv_norm_g, w_ukv, pool_w, pool_scale, w_out,
              norm2_g, w_group, b_group, w_expert, b_expert, w_gate, w_up, w_down, final_g):
    for l in range(DEPTH_2):
        x = hybrid_layer(x, norm1_g[l], w_in[l], q_norm_g[l], w_uq[l], kv_norm_g[l], w_ukv[l],
                         pool_w[l], pool_scale[l], w_out[l], norm2_g[l], w_group[l], b_group[l],
                         w_expert[l], b_expert[l], w_gate[l], w_up[l], w_down[l])
    return rms_norm(x, final_g)


def setup_inputs(seed=0):
    out = dict(first_inputs(seed))
    for name, value in second_inputs(seed + 1).items():
        if name != "x":
            out[name + "_2"] = value
    return out


def reference(
    x, meta_tokens, rel_bias, ffn1_norm, ffn1_w_gate, ffn1_w_up, ffn1_w_down, mix_norm, w_in,
    a_q_norm, a_k_norm, a_lambda_q1, a_lambda_k1, a_lambda_q2, a_lambda_k2, a_subln, b_kv_norm,
    b_w_uk, b_q_norm, b_w_uv, w_out, ffn2_norm, ffn2_w_gate, ffn2_w_up, ffn2_w_down, norm1_g_2,
    w_in_2, q_norm_g_2, w_uq_2, kv_norm_g_2, w_ukv_2, pool_w_2, pool_scale_2, w_out_2,
    norm2_g_2, w_group_2, b_group_2, w_expert_2, b_expert_2, w_gate_2, w_up_2, w_down_2,
    final_g_2,
):
    x = first_block(
        x, meta_tokens, rel_bias, ffn1_norm, ffn1_w_gate, ffn1_w_up, ffn1_w_down, mix_norm,
        w_in, a_q_norm, a_k_norm, a_lambda_q1, a_lambda_k1, a_lambda_q2, a_lambda_k2, a_subln,
        b_kv_norm, b_w_uk, b_q_norm, b_w_uv, w_out, ffn2_norm, ffn2_w_gate, ffn2_w_up,
        ffn2_w_down,
    )
    return second_block(
        x, norm1_g_2, w_in_2, q_norm_g_2, w_uq_2, kv_norm_g_2, w_ukv_2, pool_w_2, pool_scale_2,
        w_out_2, norm2_g_2, w_group_2, b_group_2, w_expert_2, b_expert_2, w_gate_2, w_up_2,
        w_down_2, final_g_2,
    )


_drawn_inputs = setup_inputs


def setup_inputs(seed=0):
    import zlib

    import numpy as np

    out = dict(_drawn_inputs(seed))
    spreads = {}
    factors = {'b_kv_norm': 6.527,
     'b_q_norm': 4.509,
     'ffn2_norm': 2.79,
     'norm1_g_2': 3.168,
     'q_norm_g_2': 5.958,
     'kv_norm_g_2': 3.924,
     'pool_scale_2': 3.251,
     'b_group_2': 23.12,
     'b_expert_2': 23.821,
     'final_g_2': 7.846,
     'a_q_norm': 3.691,
     'a_k_norm': 3.504,
     'a_subln': 3.77,
     'norm2_g_2': 6.884}
    for name, (base, spread) in spreads.items():
        noise = np.random.default_rng([zlib.crc32(name.encode()), seed]).standard_normal(out[name].shape)
        drawn = base * np.exp(spread * noise) if base else spread * noise
        out[name] = __import__('jax').numpy.asarray(drawn.astype(out[name].dtype))
    for name, factor in factors.items():
        out[name] = (out[name] * factor).astype(out[name].dtype)
    return out
```

```python
from contextlib import ExitStack
import math

import numpy as np

import concourse.bass as bass
from concourse import mybir

F32 = mybir.dt.float32
BF16 = mybir.dt.bfloat16
ALU = mybir.AluOpType
ACT = mybir.ActivationFunctionType
AX_X = mybir.AxisListType.X

P = 128
D = 1024
KT = D // P
NMETA, SEQ = 16, 256
T1 = NMETA + SEQ
T2 = SEQ
D_FF = 2816
FT = D_FF // P
FC = FT // 2
CH = KT * 256
AH, ADK, ADV = 4, 64, 128
BH, BDC = 4, 256
IH, TOPK = 8, 64
BLOCKS1 = [(0, 128), (128, 128), (256, T1 - 256)]
BLOCKS2 = [(0, 128), (128, 128)]
MH = 8
SH = 4
NE = 32
LAYERS = 2
NEG = -1e30
TAKEN = -3e38
EPS = 1e-6
LAM0 = 0.8 - 0.6 * math.exp(0.0)
GX = 384
ROW = 512
NS = 6

G_NORM = 0
G_AQ, G_AK, G_BKV, G_BQ, G_SUB = 64, 65, 66, 68, 70
G_QN, G_KVN, G_PS = 71, 75, 77
G_LAM = 81
G_RB = G_LAM + 4 * ADK
G_EPS = G_RB + LAYERS * 36
EPS_AT = {1024: 0, 64: 1, 256: 2, 128: 3}
G_ALL = G_EPS + len(EPS_AT)

C_ID, C_ONE, C_BD, C_UP = 0, 128, 256, 384
C_CM = 512
C_M2 = C_CM + GX
C_NM = C_M2 + 256
C_COS = C_NM + 384
C_IC = C_COS + 4 * T2
C_FO = C_IC + 2 * T2
C_OH = C_FO + 32
C_OM = C_OH + ROW
C_ALL = C_OM + ROW

NORM_D = {"first_in": 12, "second_in": 6}


def spread(ap, axis, n):
    shape = list(ap.shape)
    shape[axis] = n
    return ap.broadcast_to(shape)


def constants():
    c = np.zeros((P, C_ALL), np.float32)
    p = np.arange(P)
    c[:, C_ID:C_ID + P] = np.eye(P)
    c[:, C_ONE:C_ONE + P] = 1.0
    c[:, C_BD:C_BD + P] = (p[:, None] // 64) == (p[None, :] // 64)
    c[:, C_UP:C_UP + P] = p[:, None] >= p[None, :]
    x = np.arange(GX)
    c[:, C_CM:C_CM + GX] = np.where(p[:, None] + 256 - x[None, :] >= 0, 0.0, NEG)
    c[:64, C_M2 + 192:C_M2 + 256] = NEG
    q = np.arange(T2)
    c[:, C_NM:C_NM + T2] = np.where(p[:, None] < q[None, :], 0.0, NEG)
    c[:, C_NM + T2:C_NM + 384] = np.where(p[:, None] < p[None, :], 0.0, NEG)
    inv = (np.float32(10000.0) ** (-np.arange(0, 32, 2, dtype=np.float32) / np.float32(32))).astype(np.float32)
    ang = np.arange(T2, dtype=np.float32)[:, None] * inv[None, :]
    cos, sin = np.cos(ang).T, np.sin(ang).T
    cos2, sin2 = np.concatenate([cos, cos]), np.concatenate([-sin, sin])
    s = 96.0 ** -0.5
    for j, t in enumerate((cos2 * s, sin2 * s, cos2, sin2)):
        c[64:96, C_COS + j * T2:C_COS + (j + 1) * T2] = t
    for g, w in enumerate((2, 4, 8, 16)):
        r = slice(64 * (g % 2), 64 * (g % 2) + 64)
        c[r, C_IC + (g // 2) * T2:C_IC + (g // 2 + 1) * T2] = 1.0 / np.minimum(q + 1.0, w)
    c[:, C_FO:C_FO + 32] = 32 - np.arange(32)
    n = 383 - np.arange(ROW)
    nf = np.maximum(n, 1).astype(np.float32)
    large = 16 + (np.log(nf / np.float32(16)) / np.float32(math.log(8)) * np.float32(16)).astype(np.int32)
    bucket = np.where(np.maximum(n, 0) < 16, np.maximum(n, 0), np.minimum(large, 31))
    c[:32, C_OH:C_OH + ROW] = np.arange(32)[:, None] == bucket[None, :]
    c[:, C_OM:C_OM + ROW] = np.where(n >= 0, 0.0, NEG)
    return c


def build(nc, stream, gains, consts, x_tok, rel_bias, wuk, wuv, small2, out):
    with ExitStack() as ctx:
        sems = {}

        def S(name):
            if name not in sems:
                sems[name] = ctx.enter_context(nc.semaphore(name))
            return sems[name]

        def sb(name, shape, dt=F32):
            return ctx.enter_context(nc.sbuf_tensor(name, shape, dt))

        ring = sb("ring", [P, NS, CH])
        hT = sb("hT", [P, KT, T1])
        xn = sb("xn", [P, KT, T1])
        sq = sb("sq", [P, 10, T1])
        root = sb("root", [P, 2, T1])
        rstd = sb("rstd", [P, 2, T1])
        mixT = sb("mixT", [P, KT, T1])
        G = sb("G", [P, 8, GX])
        cst = sb("cst", [P, C_ALL])
        gn = sb("gn", [P, G_ALL])
        w_uk = sb("w_uk", [P, 4, 256])
        w_uv = sb("w_uv", [P, 4, 2, P])
        SM = 1536 + 1024 + 256 + 288
        sm = sb("sm", [P, SM])
        w_uq = sm[:, 0:1536].rearrange("p (k n) -> p k n", k=2)
        w_ukv = sm[:, 1536:2560].rearrange("p (h n) -> p h n", h=MH)
        w_pool = sm[:, 2560:2816].rearrange("p (t n) -> p t n", t=2)
        w_rt = sm[:, 2816:3104].rearrange("p (k n) -> p k n", k=KT)
        rb = sb("rb", [32, 8])
        zb = sb("zb", [P, 512], BF16)
        arena = sb("arena", [P, 17000])

        at = {}

        def carve(name, off, *shape):
            n = int(np.prod(shape))
            at[name] = off + n
            assert off + n <= 17000, (name, off + n)
            v = arena[:, off:off + n]
            if len(shape) == 2:
                v = v.rearrange("p (a b) -> p a b", a=shape[0])
            if len(shape) == 3:
                v = v.rearrange("p (a b c) -> p a b c", a=shape[0], b=shape[1])
            return v

        xtok = carve("xtok", 0, 3, D)
        hid = carve("hid", 0, FT, T1)
        sil = carve("sil", at["hid"], 2, T1)
        uT = carve("uT", 0, 18, T1)
        va = carve("va", at["uT"], 3, 512)
        ikT = carve("ikT", at["va"], T1)
        iw = carve("iw", at["ikT"], 3, IH)
        qlT = carve("qlT", at["iw"], 8, T1)
        ctok = carve("ctok", at["qlT"], 3, BDC)
        selb = carve("selb", at["ctok"], 3, T1)
        olT = carve("olT", at["selb"], 8, T1)
        W0 = at["olT"]
        s_sb = carve("s_sb", W0, 2, 2, 272)
        a_sb = carve("a_sb", at["s_sb"], 2, 272)
        aT = carve("aT", at["a_sb"], 2, 384)
        gb = carve("gb", at["aT"], 2, 272)
        score = carve("score", W0, 272)
        rel = carve("rel", W0 + 272, 4, 272)
        score2 = carve("score2", W0 + 272 * 5, 272)
        qcat = carve("qcat", 0, MH, T2)
        kcat = carve("kcat", at["qcat"], MH, T2)
        vm = carve("vm", at["kcat"], 2, 512)
        qbT = carve("qbT", at["vm"], 2, T2)
        kbT = carve("kbT", at["qbT"], 2, T2)
        vb = carve("vb", at["kbT"], 2, T2)
        cq = carve("cq", at["vb"], 2, T2)
        ckv = carve("ckv", at["cq"], 1, T2)
        wuqs = carve("wuqs", at["ckv"], 2, MH, 32)
        wkrs = carve("wkrs", at["wuqs"], KT, 32)
        rt1 = carve("rt1", at["wkrs"], 2, T2)
        rt2 = carve("rt2", at["rt1"], 2, T2)
        PO = at["rt2"]
        upad = carve("upad", PO, 2, 272)
        ps2 = carve("ps2", at["upad"], 2, 272)
        ps4 = carve("ps4", at["ps2"], 2, 272)
        pd = carve("pd", at["ps4"], 2, T2)
        assert at["pd"] <= W0, (at["pd"], W0)
        zm = carve("zm", W0, SH, 384)
        ln = carve("ln", at["zm"], SH, 384)
        comb_bc = carve("comb_bc", 0, NE, T2)
        silm = carve("silm", at["comb_bc"], 2, 512)
        um = carve("um", at["silm"], 512)
        hm = carve("hm", at["um"], 2, 512)
        rl = carve("rl", at["hm"], 2, 36)
        comb = carve("comb", at["rl"], 2, NE)
        combT = carve("combT", at["comb"], T2)
        e8 = carve("e8", at["combT"], 2, 8)
        t48 = carve("t48", at["e8"], 2, NE)
        small = carve("small", at["t48"], 160)
        otok = carve("otok", 0, 2, D)
        mx = sb("mx", [P, 2, 2])
        nmx = sb("nmx", [P, 2, 2])
        sums = sb("sums", [P, 2, 2])
        rs = sb("rs", [P, 2, 2])
        top8 = sb("top8", [P, 8])
        lamb = sb("lamb", [P, 8])
        lprod = sb("lprod", [P, ADK])
        btab = carve("btab", at["sil"], ROW)[0:8, :]

        bank = [ctx.enter_context(nc.psum_tensor(f"bank{i}", [P, 512], F32)) for i in range(8)]
        bias_rows = nc.dram_tensor("bias_rows", (8, ROW), F32).ap()
        bias_skew = nc.dram_tensor("bias_skew", (P, 8 * ROW), F32).ap()
        comb_dram = nc.dram_tensor("comb_dram", (LAYERS, NE, T2), F32).ap()

        ident, ones = cst[:, C_ID:C_ID + P], cst[:, C_ONE:C_ONE + P]
        bd64, upper = cst[:, C_BD:C_BD + P], cst[:, C_UP:C_UP + P]

        def gain(c):
            return gn[:, c:c + 1]

        span = [(0, T1)] * 3 + [(NMETA, T2)] * 5

        freed = []
        down_first = []
        used = 0
        units = 0
        MOE_AT = []
        STARTS = []

        def plan_ffn(f, k):
            nonlocal used
            for c in range(FC):
                freed.append(("gate_ready", 2 * FC * f + 2 * c + 2))
                freed.append(("up_ready", 2 * FC * f + 2 * c + 2))
            plan_down(k, FC)

        def plan_down(k, n):
            nonlocal used
            for c in range(n - 1):
                used += 1
                freed.append(("down_used", used))
            freed.append(("y_ready", 8 * (k + 1)))

        def plan_proj(per_chunk):
            nonlocal units
            for n in per_chunk:
                units += n
                freed.append(("proj_ready", units))

        A_FFN1 = len(freed)
        plan_ffn(0, 0)
        A_IN1 = len(freed)
        PER1 = [2, 2, 2, 2, 3, 3, 2, 2, 2, 2, 2, 2]
        plan_proj(PER1)
        A_OUT1 = len(freed)
        plan_down(1, 4)
        A_FFN2 = len(freed)
        plan_ffn(1, 2)
        A_IN2, A_OUT2 = [], []
        PER2 = [2, 3, 2, 2, 1, 2]
        for l in range(LAYERS):
            A_IN2.append(len(freed))
            plan_proj(PER2)
            A_OUT2.append(len(freed))
            plan_down(3 + l, 4)
            MOE_AT.append(len(freed))
            for e in range(NE):
                for s in ("moe_gate_ready", "moe_up_ready", "moe_down_used"):
                    freed.append((s, NE * l + e + 1))
        NCHUNK = len(freed)
        U1, U2 = sum(PER1), sum(PER2)
        SAVED2 = U2 - 2

        def chunk(n):
            return ring[:, n % NS, :]

        def up_view(n):
            return chunk(n).rearrange("p (k n) -> p k n", k=KT)

        def down_view(n):
            return chunk(n).rearrange("p (f n) -> p f n", f=2)

        def slot_sem(n):
            return S(f"slot{n % NS}_loaded")

        def loaded(eng, n):
            eng.wait_ge(slot_sem(n), 16 * (n // NS + 1))

        units_all = []

        def seg(make):
            at0 = len(units_all)
            units_all.extend(make)
            return at0, len(units_all)

        def block_bias(h, i, nq, L):
            x0 = P * (2 - i)
            return G[0:nq, h, x0:x0 + L]

        def unit_a(i, h):
            q0, nq = BLOCKS1[i]
            L = q0 + nq
            return dict(
                maps=2, nq=nq, L=L, q0=q0, kind="a", h=h, i=i,
                score=[[(uT[64 * m:64 * m + 64, h, q0:q0 + nq], uT[64 * m:64 * m + 64, 4 + h, 0:L])] for m in range(2)],
                bias=block_bias(h, i, nq, L),
                v=[lambda k, nk: va[0:nk, k, P * h:P * h + P]], base=0, M=P,
                out=mixT[:, h, q0:q0 + nq])

        def unit_b(i, h):
            q0, nq = BLOCKS1[i]
            L = q0 + nq
            return dict(
                maps=1, nq=nq, L=L, q0=q0, kind="b", h=h, i=i,
                score=[[(qlT[:, 2 * h + c, q0:q0 + nq], uT[:, 12 + c, 0:L]) for c in range(2)]],
                bias=None,
                v=[lambda k, nk, c=c: ctok[0:nk, k, P * c:P * c + P] for c in range(2)], base=0, M=P,
                out=olT[:, 2 * h:2 * h + 2, q0:q0 + nq])

        def unit_m(i, h):
            q0, nq = BLOCKS2[i]
            L = q0 + nq
            b = 64 * (h % 2)
            return dict(
                maps=1, nq=nq, L=L, q0=q0, kind="m", h=h, i=i,
                score=[[(qcat[0:96, h, q0:q0 + nq], kcat[0:96, h, 0:L])]],
                bias=cst[:, C_M2 + P * (1 - i):C_M2 + 256],
                v=[lambda k, nk: vm[0:nk, k, 64 * h:64 * h + 64]], base=b, M=64,
                out=mixT[b:b + 64, h // 2, q0:q0 + nq])

        SEG_A = seg([unit_a(i, h) for i in range(3) for h in range(AH)])
        SEG_B = seg([unit_b(i, h) for i in range(3) for h in range(BH)])
        SEG_M = [seg([unit_m(i, h) for i in range(2) for h in range(MH)]) for l in range(LAYERS)]

        def key_tiles(u):
            return [(k, min(P, u["L"] - P * k)) for k in range((u["L"] + P - 1) // P)]

        def steps(segment, *stages):
            a, b = segment
            for s in range(a, b + len(stages) - 1):
                for j, stage in enumerate(stages):
                    if a <= s - j < b:
                        stage(s - j)

        def qcols(i):
            q0, nq = BLOCKS1[i]
            return q0, nq, q0 + nq

        block = ctx.enter_context(nc.Block())

        @block.sync
        def _(sp):
            def load(n):
                if n >= NS:
                    name, v = freed[n - NS]
                    sp.wait_ge(S(name), v)
                sp.dma_start(chunk(n), stream[n]).then_inc(slot_sem(n), 16)

            n = 0
            for l in range(LAYERS):
                while n < MOE_AT[l] + 6:
                    load(n)
                    n += 1
                with sp.Fori(1, NE // 2) as i:
                    for j in range(6):
                        m = MOE_AT[l] + j
                        name = ("moe_gate_ready", "moe_up_ready", "moe_down_used")[j % 3]
                        sp.wait_ge(S(name), i * 2 + (NE * l - 1 + j // 3))
                        sp.dma_start(chunk(m), stream[bass.ds(i * 6 + m, 1)].rearrange("a p n -> p (a n)")
                                     ).then_inc(slot_sem(m), 16)
                n = MOE_AT[l] + 3 * NE
            for t in range(2):
                sp.wait_ge(S("out_ready"), 4 * (t + 1))
                sp.dma_start(out[0, P * t:P * t + P, :], otok[:, t, :]).then_inc(S("out_written"), 16)
            sp.wait_ge(S("out_written"), 32)

        @block.gpsimd
        def _(pool):
            n_chain = 0

            def link(ins):
                nonlocal n_chain
                n_chain += 1
                ins.then_inc(S("pool_chain"), 1)
                pool.wait_ge(S("pool_chain"), n_chain)

            nc.gpsimd.memset(zb[:], 0.0).then_inc(S("zeros_ready"), 1)
            pool.wait_ge(S("bias_rows_ready"), 1)
            pool.dma_start(bias_rows, btab[:, :]).then_inc(S("bias_rows_written"), 16)
            pool.wait_ge(S("bias_rows_written"), 16)
            src = spread(bias_rows.rearrange("(a h) n -> a (h n)", a=1), 0, P)
            pool.dma_start(bias_skew, src).then_inc(S("bias_skew_written"), 16)
            pool.wait_ge(S("bias_skew_written"), 16)
            for h in range(8):
                src = bass.AP(bias_skew.tensor, 127 + ROW * h, [[8 * ROW - 1, P], [1, GX]])
                pool.dma_start(G[:, h, :], src).then_inc(S("G_loaded"), 16)

            for g in range(*SEG_B):
                u = units_all[g]
                pool.wait_ge(S("G_loaded"), 16 * 8)
                pool.wait_ge(S("selected"), u["i"] + 1)
                if g - SEG_B[0] >= 2:
                    pool.wait_ge(S("scores_taken"), g - 1)
                else:
                    pool.wait_ge(S("subln_done"), AH)
                nc.gpsimd.tensor_tensor(gb[0:u["nq"], g % 2, 0:u["L"]], block_bias(4 + u["h"], u["i"], u["nq"], u["L"]),
                                        selb[0:u["nq"], u["i"], 0:u["L"]], ALU.add).then_inc(S("bias_ready"), 1)

            for l in range(LAYERS):
                pool.wait_ge(S("small2_loaded"), 16 * (l + 1))
                if l == 0:
                    pool.wait_ge(S("residual_ready"), 8 * 3)
                else:
                    pool.wait_ge(S("residual_ready"), 8 * 5)
                wq = w_uq.rearrange("p k (h n) -> p k h n", h=MH)
                for k in range(2):
                    link(nc.gpsimd.tensor_copy(wuqs[:, k, :, 0:16], wq[:, k, :, 80:96]))
                    link(nc.gpsimd.tensor_copy(wuqs[:, k, :, 16:32], wq[:, k, :, 64:80]))
                pool.wait_ge(slot_sem(A_IN2[l] + 1), 16 * ((A_IN2[l] + 1) // NS + 1))
                wk = up_view(A_IN2[l] + 1)
                link(nc.gpsimd.tensor_copy(wkrs[:, :, 0:16], wk[:, :, 144:160]))
                nc.gpsimd.tensor_copy(wkrs[:, :, 16:32], wk[:, :, 128:144]).then_inc(S("swapped_ready"), 1)
                nc.gpsimd.memset(upad[:, :, 0:16], 0.0).then_inc(S("pad_ready"), 1)
                pool.wait_ge(S("pad_ready"), l + 1)
                pool.wait_ge(S("proj_saved"), U1 + SAVED2 * (l + 1))
                link(nc.gpsimd.tensor_tensor(ps2[:, :, 1:272], upad[:, :, 1:272], upad[:, :, 0:271], ALU.add))
                link(nc.gpsimd.tensor_tensor(ps4[:, :, 3:272], ps2[:, :, 3:272], ps2[:, :, 1:270], ALU.add))
                ic = cst[:, C_IC:C_IC + 2 * T2].rearrange("p (t n) -> p t n", t=2)
                link(nc.gpsimd.tensor_tensor(pd[0:64, 0, :], ps2[0:64, 0, 16:272], ic[0:64, 0, :], ALU.mult))
                link(nc.gpsimd.tensor_tensor(pd[64:128, 0, :], ps4[64:128, 0, 16:272], ic[64:128, 0, :], ALU.mult))
                link(nc.gpsimd.tensor_tensor(ps2[:, 1, 7:272], ps4[:, 1, 7:272], ps4[:, 1, 3:268], ALU.add))
                link(nc.gpsimd.tensor_tensor(pd[0:64, 1, :], ps2[0:64, 1, 16:272], ic[0:64, 1, :], ALU.mult))
                link(nc.gpsimd.tensor_tensor(ps4[:, 1, 15:272], ps2[:, 1, 15:272], ps2[:, 1, 7:264], ALU.add))
                link(nc.gpsimd.tensor_tensor(pd[64:128, 1, :], ps4[64:128, 1, 16:272], ic[64:128, 1, :], ALU.mult))
                nc.gpsimd.tensor_tensor(pd[:, :, :], pd[:, :, :], upad[:, :, 16:272], ALU.subtract
                                        ).then_inc(S("pool_d_ready"), 1)
                pool.wait_ge(S("combT_ready"), l + 1)
                pool.dma_start(comb_dram[l], combT[0:NE, :]).then_inc(S("comb_written"), 16)
                pool.wait_ge(S("comb_written"), 16 * (l + 1))
                src = spread(comb_dram[l].rearrange("(a e) n -> a (e n)", a=1), 0, P)
                pool.dma_start(comb_bc.rearrange("p e n -> p (e n)"), src).then_inc(S("comb_loaded"), 16)
            pool.wait_ge(S("comb_loaded"), 32)
            pool.wait_ge(S("G_loaded"), 16 * 8)

        @block.scalar
        def _(act):
            n_chain = 0

            def link(ins):
                nonlocal n_chain
                n_chain += 1
                ins.then_inc(S("act_chain"), 1)
                act.wait_ge(S("act_chain"), n_chain)

            copy = nc.scalar.activation

            act.dma_start(cst[:], consts).then_inc(S("consts_loaded"), 16)
            act.dma_start(xtok[:, 0:2, :], x_tok[0:256].rearrange("(t p) n -> p t n", p=P)).then_inc(S("x_loaded"), 16)
            act.dma_start(xtok[0:16, 2, :], x_tok[256:272]).then_inc(S("x_loaded"), 16)
            act.dma_start(gn[:], gains).then_inc(S("gains_loaded"), 16)
            act.dma_start(rb[:], rel_bias).then_inc(S("rb_loaded"), 16)
            act.dma_start(w_uk[:], wuk).then_inc(S("wuk_loaded"), 16)
            act.dma_start(w_uv[:], wuv).then_inc(S("wuv_loaded"), 16)
            act.dma_start(sm[:], small2[0]).then_inc(S("small2_loaded"), 16)

            for d in range(KT):
                act.wait_ge(S("xT_ready"), d + 1)
                copy(hT[:, d, :], bank[d][:, 0:T1], ACT.Copy).then_inc(S("input_saved"), 1)
            act.wait_ge(S("lam_sums_ready"), 1)
            copy(lamb[:, 2:4], lamb[:, 0:2], ACT.Exp).then_inc(S("lam_exp_ready"), 1)

            n_root = 0

            def take_root(src, width, ready, v):
                nonlocal n_root
                act.wait_ge(S(ready), v)
                if n_root >= 2:
                    act.wait_ge(S("root_used"), n_root - 1)
                nc.scalar.activation(root[:, n_root % 2, 0:src.shape[1]], src, ACT.Sqrt, bias=gain(G_EPS + EPS_AT[width])
                                     ).then_inc(S("root_ready"), 1)
                n_root += 1

            def squares(n):
                off, T = span[n]
                for half in range(2):
                    if n == 0:
                        act.wait_ge(S("input_saved"), 4 * (half + 1))
                    else:
                        act.wait_ge(S("residual_ready"), 8 * (n - 1) + 4 * (half + 1))
                    copy(sq[:, 4 * half:4 * half + 4, 0:T], hT[:, 4 * half:4 * half + 4, off:off + T], ACT.Square
                         ).then_inc(S("squares_ready"), 1)
                if n == 0:
                    act.wait_ge(S("gains_loaded"), 16)
                take_root(bank[0][:, 0:T], D, "sumsq_ready", n + 1)

            def ffn(f):
                for i in range(FT):
                    g = FT * f + i
                    act.wait_ge(S("gate_ready"), g + 1)
                    if i >= 2:
                        act.wait_ge(S("hid_ready"), g - 1)
                    copy(sil[:, i % 2, :], bank[2 * (i % 4)][:, 0:T1], ACT.Silu).then_inc(S("silu_ready"), 1)

            def save(u, *ops):
                act.wait_ge(S("proj_ready"), u + 1)
                for op in ops[:-1]:
                    link(op())
                ops[-1]().then_inc(S("proj_saved"), 1)

            def exps(g):
                u = units_all[g]
                act.wait_ge(S("max_ready"), g + 1)
                for m in range(u["maps"]):
                    s = s_sb[0:u["nq"], g % 2, m, 0:u["L"]]
                    ins = nc.scalar.activation(s, s, ACT.Exp, bias=nmx[0:u["nq"], g % 2, m:m + 1],
                                               accum_out=sums[0:u["nq"], g % 2, m:m + 1])
                ins.then_inc(S("exps_ready"), 1)

            def save_T(g):
                u = units_all[g]
                act.wait_ge(S("aT_ready"), g + 1)
                if g >= 2:
                    act.wait_ge(S("o_ready"), g - 1)
                kts = key_tiles(u)
                nq = u["nq"]
                full = [k for k, nk in kts if nk == P]
                ops = []
                if full:
                    w = nq * len(full)
                    ops.append((aT[:, g % 2, 0:w], bank[4 + g % 2][:, 0:w]))
                if kts[-1][1] < P:
                    k, nk = kts[-1]
                    ops.append((aT[0:nk, g % 2, nq * k:nq * k + nq], bank[4 + g % 2][0:nk, nq * k:nq * k + nq]))
                for o, i in ops[:-1]:
                    link(copy(o, i, ACT.Copy))
                copy(ops[-1][0], ops[-1][1], ACT.Copy).then_inc(S("aT_saved"), 1)

            def save_o(g):
                u = units_all[g]
                act.wait_ge(S("o_ready"), g + 1)
                b, M, nq = u["base"], u["M"], u["nq"]
                src = bank[6 + g % 2][b:b + M, 0:nq * len(u["v"])]
                if len(u["v"]) == 2:
                    src = src.rearrange("p (c n) -> p c n", c=2)
                if u["kind"] == "a":
                    link(copy(u["out"], src, ACT.Copy))
                    copy(sq[:, u["h"], u["q0"]:u["q0"] + nq], src, ACT.Square).then_inc(S("o_saved"), 1)
                else:
                    copy(u["out"], src, ACT.Copy).then_inc(S("o_saved"), 1)

            squares(0)
            ffn(0)
            squares(1)
            act.wait_ge(S("bias_rows_written"), 16)
            u = 0
            for t in range(8):
                save(u, lambda: copy(uT[:, t, :], bank[u % 8][:, 0:T1], ACT.Copy),
                     lambda: copy(sq[:, t, :], bank[u % 8][:, 0:T1], ACT.Square))
                u += 1
            for c in range(2):
                for t, (q0, nq) in enumerate(BLOCKS1):
                    save(u, lambda: copy(va[0:nq, t, 256 * c:256 * c + 256], bank[u % 8][0:nq, 0:256], ACT.Copy))
                    u += 1
            for t in range(4):
                save(u, lambda: copy(uT[:, 8 + t, :], bank[u % 8][:, 0:T1], ACT.Copy))
                u += 1
            for t in range(2):
                save(u, lambda: copy(uT[:, 12 + t, :], bank[u % 8][:, 0:T1], ACT.Copy),
                     lambda: copy(sq[:, 8 + t, :], bank[u % 8][:, 0:T1], ACT.Square))
                u += 1
            for t in range(4):
                save(u, lambda: copy(uT[:, 14 + t, :], bank[u % 8][:, 0:T1], ACT.Copy))
                u += 1
            save(u, lambda: copy(ikT[:, :], bank[u % 8][:, 0:T1], ACT.Copy))
            u += 1
            iwb = bank[u % 8][:, 0:24].rearrange("p (t n) -> p t n", t=3)
            save(u, lambda: nc.scalar.activation(iw[:, 0:2, :], iwb[:, 0:2, :], ACT.Copy, scale=IH ** -0.5),
                 lambda: nc.scalar.activation(iw[0:16, 2, :], iwb[0:16, 2, :], ACT.Copy, scale=IH ** -0.5))
            for t in range(8):
                take_root(bank[t][:, 0:T1], ADK, "norm1_psum", t + 1)
            take_root(bank[0][:, 0:T1], BDC, "normc_psum", 1)
            for t in range(8):
                act.wait_ge(S("qlat_ready"), t + 1)
                link(copy(qlT[:, t, :], bank[t][:, 0:T1], ACT.Copy))
                copy(sq[:, t, :], bank[t][:, 0:T1], ACT.Square).then_inc(S("qlat_saved"), 1)
            for h in range(BH):
                take_root(bank[h][:, 0:T1], BDC, "normq_psum", h + 1)
            for t, (q0, nq) in enumerate(BLOCKS1):
                act.wait_ge(S("ctok_ready"), t + 1)
                copy(ctok[0:nq, t, :], bank[4 + t][0:nq, 0:BDC], ACT.Copy).then_inc(S("ctok_saved"), 1)
            for i in range(3):
                q0, nq, L = qcols(i)
                for h in range(IH):
                    n = IH * i + h
                    act.wait_ge(S("dots_ready"), n + 1)
                    if n >= 4:
                        act.wait_ge(S("score_added"), n - 3)
                    nc.scalar.activation(rel[0:nq, n % 4, 0:L], bank[n % 4][0:nq, 0:L], ACT.Relu, scale=0.125
                                         ).then_inc(S("relu_ready"), 1)
            steps(SEG_A, exps, save_T, save_o)
            for h in range(AH):
                take_root(bank[h][:, 0:T1], ADV, "subln_psum", h + 1)
            steps(SEG_B, exps, save_T, save_o)
            for h in range(BH):
                act.wait_ge(S("ob_ready"), h + 1)
                copy(mixT[:, 4 + h, :], bank[h][:, 0:T1], ACT.Copy).then_inc(S("ob_saved"), 1)
            squares(2)
            ffn(1)

            for l in range(LAYERS):
                squares(3 + 2 * l)
                u = U1 + U2 * l
                v = lambda b: bank[b % 8][:, 0:T2]
                for t in range(2):
                    save(u, lambda: copy(cq[:, t, :], v(u), ACT.Copy), lambda: copy(sq[:, t, 0:T2], v(u), ACT.Square))
                    u += 1
                save(u, lambda: copy(ckv[:, 0, :], v(u), ACT.Copy), lambda: copy(sq[:, 2, 0:T2], v(u), ACT.Square))
                u += 1
                u += 2
                for dst in (qbT, kbT):
                    for t in range(2):
                        save(u, lambda: copy(dst[:, t, :], v(u), ACT.Copy))
                        u += 1
                save(u, lambda: copy(vb.rearrange("p t n -> p (t n)"), bank[u % 8][:, :], ACT.Copy))
                u += 1
                act.wait_ge(S("pad_ready"), l + 1)
                for t in range(2):
                    save(u, lambda: copy(upad[:, t, 16:272], v(u), ACT.Copy))
                    u += 1
                take_root(bank[0][:, 0:T2], 256, "norm_lat_psum", 2 * l + 1)
                take_root(bank[1][:, 0:T2], 128, "norm_lat_psum", 2 * l + 2)
                for n in range(4):
                    act.wait_ge(S("q_up_ready"), 4 * l + n + 1)
                    nc.scalar.activation(qcat[0:64, 2 * n:2 * n + 2, :],
                                         bank[2 * (n % 2)][0:64, :].rearrange("p (h n) -> p h n", h=2),
                                         ACT.Copy, scale=96.0 ** -0.5).then_inc(S("q_nope_saved"), 1)
                for n in range(4):
                    act.wait_ge(S("k_up_ready"), 4 * l + n + 1)
                    copy(kcat[0:64, 2 * n:2 * n + 2, :], bank[4 + n % 2][0:64, :].rearrange("p (h n) -> p h n", h=2),
                         ACT.Copy).then_inc(S("k_nope_saved"), 1)
                for t in range(2):
                    act.wait_ge(S("v_up_ready"), 2 * l + t + 1)
                    copy(vm[:, t, :], bank[6 + t][:, :], ACT.Copy).then_inc(S("vm_saved"), 1)
                steps(SEG_M[l], exps, save_T, save_o)
                for h in range(SH):
                    act.wait_ge(S("nabs_ready"), SH * l + h + 1)
                    link(copy(ln[:, h, :], ln[:, h, :], ACT.Exp))
                for h in range(SH):
                    nc.scalar.activation(ln[:, h, :], ln[:, h, :], ACT.Ln, bias=1.0).then_inc(S("ln_ready"), 1)
                for h in range(SH):
                    act.wait_ge(S("stick_log_ready"), SH * l + h + 1)
                    copy(ln[:, h, :], zm[:, h, :], ACT.Exp).then_inc(S("stick_ready"), 1)
                for h in range(SH):
                    b = 64 * (h % 2)
                    act.wait_ge(S("stick_o_ready"), SH * l + h + 1)
                    copy(mixT[b:b + 64, 4 + h // 2, 0:T2], bank[4 + h][b:b + 64, 0:T2], ACT.Copy
                         ).then_inc(S("stick_saved"), 1)
                for t in range(2):
                    act.wait_ge(S("pool_y_ready"), l + 1)
                    nc.scalar.activation(mixT[:, 6 + t, 0:T2], bank[0][:, T2 * t:T2 * t + T2], ACT.Copy,
                                         scale=gain(G_PS + 2 * l + t)).then_inc(S("pool_saved"), 1)
                squares(4 + 2 * l)
                act.wait_ge(S("router_shifted"), l + 1)
                copy(small[:, 16:24], small[:, 8:16], ACT.Exp).then_inc(S("router_exp1"), 1)
                act.wait_ge(S("router_gap"), l + 1)
                copy(small[:, 44:46], small[:, 40:42], ACT.Exp).then_inc(S("router_exp2"), 1)
                act.wait_ge(S("combT_psum"), l + 1)
                copy(combT[0:NE, :], bank[1][0:NE, 0:T2], ACT.Copy).then_inc(S("combT_ready"), 1)
                if l + 1 < LAYERS:
                    act.wait_ge(S("router_ready"), l + 1)
                    act.dma_start(sm[:], small2[l + 1]).then_inc(S("small2_loaded"), 16)

                def silu(e, p, first):
                    act.wait_ge(S("moe_gate_ready"), e + 1)
                    if not first:
                        act.wait_ge(S("moe_hid_ready"), e - 1)
                    copy(silm[:, p, :], bank[4 + 2 * p][:, :], ACT.Silu).then_inc(S("moe_silu_ready"), 1)
                silu(NE * l, 0, True)
                silu(NE * l + 1, 1, True)
                with act.Fori(1, NE // 2) as i:
                    for p in range(2):
                        silu(i * 2 + (NE * l + p), p, False)
            squares(7)
            for t in range(2):
                for j in range(4):
                    n = 4 * t + j
                    act.wait_ge(S("outT_ready"), n + 1)
                    copy(otok[:, t, 256 * j:256 * j + 256], bank[1 + n % 4][:, 0:256], ACT.Copy).then_inc(S("out_ready"), 1)

        @block.tensor
        def _(pe):
            mm = nc.tensor.matmul

            def token_sum(dst, lhs, tiles, T):
                for j, t in enumerate(tiles):
                    ins = mm(dst, lhs, sq[:, t, 0:T], start=(j == 0), stop=(j == len(tiles) - 1))
                return ins

            def norm(n):
                off, T = span[n]
                pe.wait_ge(S("squares_ready"), 2 * n + 1)
                token_sum(bank[0][:, 0:T], ones, range(4), T) if False else None
                for t in range(KT):
                    if t == 4:
                        pe.wait_ge(S("squares_ready"), 2 * n + 2)
                    ins = mm(bank[0][:, 0:T], ones, sq[:, t, 0:T], start=(t == 0), stop=(t == KT - 1))
                ins.then_inc(S("sumsq_ready"), 1)

            def ffn(f, at, n):
                for i in range(FT):
                    g, c, ft = FT * f + i, i // 2, i % 2
                    if i >= 4:
                        pe.wait_ge(S("hid_ready"), g - 3)
                    for j, sig in enumerate(("gate_ready", "up_ready")):
                        loaded(pe, at + 2 * c + j)
                        w = up_view(at + 2 * c + j)
                        dst = bank[2 * (i % 4) + j][:, 0:T1]
                        for k in range(KT):
                            if i == 0 and j == 0:
                                pe.wait_ge(S("xn_ready"), KT * n + k + 1)
                            ins = mm(dst, w[:, k, P * ft:P * ft + P], xn[:, k, :], start=(k == 0), stop=(k == KT - 1))
                        ins.then_inc(S(sig), 1)
                down(at + 2 * FC, FC, hid, T1, [("hid_ready", FT * f + i + 1) for i in range(FT)])

            def down(at, chunks, rhs, T, ready):
                if len(ready) > 1 and chunks == FC:
                    pe.wait_ge(S(ready[-1][0]), ready[-1][1])
                else:
                    for name, v in ready:
                        pe.wait_ge(S(name), v)
                for c in range(chunks):
                    loaded(pe, at + c)
                    w = down_view(at + c)
                    for f in range(2):
                        for d in range(KT):
                            first, last = c == 0 and f == 0, c == chunks - 1 and f == 1
                            ins = mm(bank[d][:, 0:T], w[:, f, P * d:P * d + P], rhs[:, 2 * c + f, 0:T],
                                     start=first, stop=last)
                            if last:
                                ins.then_inc(S("y_ready"), 1)
                    if c < chunks - 1:
                        ins.then_inc(S("down_used"), 1)

            class Units:
                n = 0

            def bank_free(u, base):
                held = u - base - 8
                if held >= 0 and base < U1:
                    pe.wait_ge(S("proj_saved"), held + 1)
                elif 0 <= held < 3:
                    pe.wait_ge(S("proj_saved"), U1 + SAVED2 * ((base - U1) // U2) + held + 1)
                elif held == 3:
                    pe.wait_ge(S("rotary_read"), 2 * ((base - U1) // U2) + 1)

            def feature_unit(u, base, at, c0, T, n=None):
                bank_free(u, base)
                w = up_view(at)
                loaded(pe, at)
                for k in range(KT):
                    if n is not None:
                        pe.wait_ge(S("xn_ready"), KT * n + k + 1)
                    ins = mm(bank[u % 8][:, 0:T], w[:, k, c0:c0 + P], xn[:, k, 0:T], start=(k == 0), stop=(k == KT - 1))
                ins.then_inc(S("proj_ready"), 1)

            def scores(g):
                u = units_all[g]
                if g >= 2:
                    pe.wait_ge(S("scores_taken"), g - 1)
                for m in range(u["maps"]):
                    parts = u["score"][m]
                    for j, (lhs, rhs) in enumerate(parts):
                        ins = mm(bank[2 * (g % 2) + m][0:u["nq"], 0:u["L"]], lhs, rhs,
                                 start=(j == 0), stop=(j == len(parts) - 1))
                ins.then_inc(S("scores_ready"), 1)

            def turn(g):
                u = units_all[g]
                pe.wait_ge(S("probs_ready"), g + 1)
                if g >= 2:
                    pe.wait_ge(S("aT_saved"), g - 1)
                nq = u["nq"]
                for k, nk in key_tiles(u):
                    ins = nc.tensor.transpose(bank[4 + g % 2][0:nk, nq * k:nq * k + nq],
                                              a_sb[0:nq, g % 2, P * k:P * k + nk], ident[0:nq, 0:nq])
                ins.then_inc(S("aT_ready"), 1)

            def pv(g):
                u = units_all[g]
                pe.wait_ge(S("aT_saved"), g + 1)
                if g >= 2:
                    pe.wait_ge(S("o_saved"), g - 1)
                nq, b, M = u["nq"], u["base"], u["M"]
                kts = key_tiles(u)
                for c, v in enumerate(u["v"]):
                    for k, nk in kts:
                        ins = mm(bank[6 + g % 2][b:b + M, nq * c:nq * c + nq], v(k, nk), aT[0:nk, g % 2, nq * k:nq * k + nq],
                                 start=(k == 0), stop=(k == len(kts) - 1))
                ins.then_inc(S("o_ready"), 1)

            pe.wait_ge(S("consts_loaded"), 16)
            pe.wait_ge(S("x_loaded"), 32)
            for d in range(KT):
                for t, (q0, nq) in enumerate(BLOCKS1):
                    ins = nc.tensor.transpose(bank[d][:, q0:q0 + nq], xtok[0:nq, t, P * d:P * d + P], ident[0:nq, 0:nq])
                ins.then_inc(S("xT_ready"), 1)
            pe.wait_ge(S("input_saved"), 8)
            norm(0)
            pe.wait_ge(S("rb_loaded"), 16)
            mm(bank[7][0:8, :], rb[:, :], cst[0:32, C_OH:C_OH + ROW], start=True, stop=True).then_inc(S("bias_psum"), 1)
            pe.wait_ge(S("bias_rows_ready"), 1)
            ffn(0, A_FFN1, 0)
            norm(1)

            u = 0
            for t in range(8):
                feature_unit(u, 0, A_IN1 + t // 2, P * (t % 2), T1, n=1 if t == 0 else None)
                u += 1
            for c in range(2):
                at_ = A_IN1 + 4 + c
                for t, (q0, nq) in enumerate(BLOCKS1):
                    bank_free(u, 0)
                    loaded(pe, at_)
                    for k in range(KT):
                        ins = mm(bank[u % 8][0:nq, 0:256], xn[:, k, q0:q0 + nq], up_view(at_)[:, k, :],
                                 start=(k == 0), stop=(k == KT - 1))
                    ins.then_inc(S("proj_ready"), 1)
                    u += 1
            for t in range(10):
                feature_unit(u, 0, A_IN1 + 6 + t // 2, P * (t % 2), T1)
                u += 1
            w = up_view(A_IN1 + 11)
            loaded(pe, A_IN1 + 11)
            bank_free(u, 0)
            for half in range(2):
                for k in range(KT):
                    ins = mm(bank[u % 8][64 * half:64 * half + 64, 0:T1], w[:, k, 0:64], xn[:, k, :],
                             start=(k == 0), stop=(k == KT - 1))
            ins.then_inc(S("proj_ready"), 1)
            u += 1
            bank_free(u, 0)
            for t, (q0, nq) in enumerate(BLOCKS1):
                for k in range(KT):
                    ins = mm(bank[u % 8][0:nq, 8 * t:8 * t + 8], xn[:, k, q0:q0 + nq], w[:, k, 64:72],
                             start=(k == 0), stop=(k == KT - 1))
            ins.then_inc(S("proj_ready"), 1)
            pe.wait_ge(S("proj_saved"), U1)
            for t in range(8):
                mm(bank[t][:, 0:T1], bd64, sq[:, t, :], start=True, stop=True).then_inc(S("norm1_psum"), 1)
            pe.wait_ge(S("norm1_done"), 1)
            token_sum(bank[0][:, 0:T1], ones, (8, 9), T1).then_inc(S("normc_psum"), 1)
            pe.wait_ge(S("wuk_loaded"), 16)
            pe.wait_ge(S("normc_done"), 2)
            pe.wait_ge(S("norm1_done"), 8)
            for t in range(8):
                mm(bank[t][:, 0:T1], w_uk[:, t // 2, P * (t % 2):P * (t % 2) + P], uT[:, 8 + t // 2, :],
                   start=True, stop=True).then_inc(S("qlat_ready"), 1)
            pe.wait_ge(S("qlat_saved"), 8)
            for h in range(BH):
                token_sum(bank[h][:, 0:T1], ones, (2 * h, 2 * h + 1), T1).then_inc(S("normq_psum"), 1)
            for t, (q0, nq) in enumerate(BLOCKS1):
                for c in range(2):
                    ins = nc.tensor.transpose(bank[4 + t][0:nq, P * c:P * c + P], uT[:, 12 + c, q0:q0 + nq], ident)
                ins.then_inc(S("ctok_ready"), 1)
            pe.wait_ge(S("normq_done"), 8)
            for i in range(3):
                q0, nq, L = qcols(i)
                for h in range(IH):
                    n, b = IH * i + h, 64 * (h % 2)
                    if n >= 4:
                        pe.wait_ge(S("relu_ready"), n - 3)
                    mm(bank[n % 4][0:nq, 0:L], uT[b:b + 64, 14 + h // 2, q0:q0 + nq], ikT[b:b + 64, 0:L],
                       start=True, stop=True).then_inc(S("dots_ready"), 1)
            pe.wait_ge(S("relu_ready"), 24)
            pe.wait_ge(S("ctok_saved"), 3)
            steps(SEG_A, scores, turn, pv)
            pe.wait_ge(S("o_saved"), SEG_A[1])
            for h in range(AH):
                mm(bank[h][:, 0:T1], ones, sq[:, h, :], start=True, stop=True).then_inc(S("subln_psum"), 1)
            pe.wait_ge(S("subln_done"), AH)
            steps(SEG_B, scores, turn, pv)
            pe.wait_ge(S("o_saved"), SEG_B[1])
            pe.wait_ge(S("wuv_loaded"), 16)
            for h in range(BH):
                for c in range(2):
                    ins = mm(bank[h][:, 0:T1], w_uv[:, h, c, :], olT[:, 2 * h + c, :], start=(c == 0), stop=(c == 1))
                ins.then_inc(S("ob_ready"), 1)
            down(A_OUT1, 4, mixT, T1, [("ob_saved", BH), ("subln_done", AH)])
            norm(2)
            ffn(1, A_FFN2, 2)

            for l in range(LAYERS):
                n1 = 3 + 2 * l
                norm(n1)
                base = U1 + U2 * l
                u = base
                a = A_IN2[l]
                pe.wait_ge(S("xn_ready"), KT * n1 + 1)
                feature_unit(u, base, a, 0, T2, n=n1)
                feature_unit(u + 1, base, a, P, T2)
                feature_unit(u + 2, base, a + 1, 0, T2)
                pe.wait_ge(S("swapped_ready"), l + 1)
                for j in range(2):
                    bank_free(u + 3 + j, base)
                    for k in range(KT):
                        lhs = wkrs[:, k, :] if j else up_view(a + 1)[:, k, P:P + 32]
                        ins = mm(bank[(u + 3 + j) % 8][64:96, 0:T2], lhs, xn[:, k, 0:T2], start=(k == 0), stop=(k == KT - 1))
                    ins.then_inc(S("proj_ready"), 1)
                u += 5
                for t in range(4):
                    feature_unit(u, base, a + 2 + t // 2, P * (t % 2), T2)
                    u += 1
                bank_free(u, base)
                loaded(pe, a + 4)
                for t in range(2):
                    for k in range(KT):
                        ins = mm(bank[u % 8][:, T2 * t:T2 * t + T2], xn[:, k, P * t:P * t + P], up_view(a + 4)[:, k, :],
                                 start=(k == 0), stop=(k == KT - 1))
                ins.then_inc(S("proj_ready"), 1)
                u += 1
                for t in range(2):
                    feature_unit(u, base, a + 5, P * t, T2)
                    u += 1
                pe.wait_ge(S("proj_saved"), U1 + SAVED2 * (l + 1))
                pe.wait_ge(S("rotary_read"), 2 * (l + 1))
                token_sum(bank[0][:, 0:T2], ones, (0, 1), T2).then_inc(S("norm_lat_psum"), 1)
                mm(bank[1][:, 0:T2], ones, sq[:, 2, 0:T2], start=True, stop=True).then_inc(S("norm_lat_psum"), 1)
                pe.wait_ge(S("lat_ready"), 3 * (l + 1))
                for n in range(4):
                    if n >= 2:
                        pe.wait_ge(S("q_nope_saved"), 4 * l + n - 1)
                        pe.wait_ge(S("q_rope_saved"), 4 * l + n - 1)
                    b0, b1 = bank[2 * (n % 2)], bank[2 * (n % 2) + 1]
                    for j in range(2):
                        h = 2 * n + j
                        for k in range(2):
                            mm(b0[0:96, T2 * j:T2 * j + T2], w_uq[:, k, 96 * h:96 * h + 96], cq[:, k, :],
                               start=(k == 0), stop=(k == 1))
                        for k in range(2):
                            ins = mm(b1[64:96, T2 * j:T2 * j + T2], wuqs[:, k, h, :], cq[:, k, :],
                                     start=(k == 0), stop=(k == 1))
                    ins.then_inc(S("q_up_ready"), 1)
                for n in range(4):
                    if n >= 2:
                        pe.wait_ge(S("k_nope_saved"), 4 * l + n - 1)
                    for j in range(2):
                        ins = mm(bank[4 + n % 2][0:64, T2 * j:T2 * j + T2], w_ukv[:, 2 * n + j, 0:64], ckv[:, 0, :],
                                 start=True, stop=True)
                    ins.then_inc(S("k_up_ready"), 1)
                for t in range(2):
                    mm(bank[6 + t][:, :], ckv[:, 0, P * t:P * t + P], w_ukv[:, :, 64:128],
                       start=True, stop=True).then_inc(S("v_up_ready"), 1)
                pe.wait_ge(S("q_nope_saved"), 4 * (l + 1))
                pe.wait_ge(S("q_rope_saved"), 4 * (l + 1))
                pe.wait_ge(S("k_nope_saved"), 4 * (l + 1))
                pe.wait_ge(S("k_rope_saved"), l + 1)
                pe.wait_ge(S("vm_saved"), 2 * (l + 1))
                steps(SEG_M[l], scores, turn, pv)
                pe.wait_ge(S("o_saved"), SEG_M[l][1])
                for h in range(SH):
                    b, t = 64 * (h % 2), h // 2
                    mm(bank[h][:, 0:T2], kbT[b:b + 64, t, 0:P], qbT[b:b + 64, t, :], start=True, stop=True)
                    mm(bank[h][:, T2:384], kbT[b:b + 64, t, P:T2], qbT[b:b + 64, t, P:T2],
                       start=True, stop=True).then_inc(S("z_ready"), 1)
                for h in range(SH):
                    pe.wait_ge(S("softplus_ready"), SH * l + h + 1)
                    mm(bank[h][:, T2:384], upper, ln[:, h, T2:384], start=True, stop=True)
                    mm(bank[h][:, 0:T2], upper, ln[:, h, 0:T2], start=True, stop=True)
                    mm(bank[h][:, P:T2], ones, ln[:, h, T2:384], start=False, stop=True,
                       skip_group_check=True).then_inc(S("later_ready"), 1)
                for h in range(SH):
                    b = 64 * (h % 2)
                    pe.wait_ge(S("stick_ready"), SH * l + h + 1)
                    mm(bank[4 + h][b:b + 64, 0:T2], vb[:, 0, 64 * h:64 * h + 64], ln[:, h, 0:T2], start=True, stop=True)
                    mm(bank[4 + h][b:b + 64, P:T2], vb[:, 1, 64 * h:64 * h + 64], ln[:, h, T2:384], start=False, stop=True,
                       skip_group_check=True).then_inc(S("stick_o_ready"), 1)
                pe.wait_ge(S("pool_d_ready"), l + 1)
                for t in range(2):
                    ins = mm(bank[0][:, T2 * t:T2 * t + T2], w_pool[:, t, :], pd[:, t, :], start=True, stop=True)
                ins.then_inc(S("pool_y_ready"), 1)
                down(A_OUT2[l], 4, mixT, T2, [("stick_saved", SH * (l + 1)), ("pool_saved", 2 * (l + 1))])
                n2 = 4 + 2 * l
                norm(n2)
                pe.wait_ge(S("xn_ready"), KT * (n2 + 1))
                for t in range(2):
                    for k in range(KT):
                        ins = mm(bank[0][:, 36 * t:36 * t + 36], xn[:, k, P * t:P * t + P], w_rt[:, k, :],
                                 start=(k == 0), stop=(k == KT - 1))
                ins.then_inc(S("router_ready"), 1)
                pe.wait_ge(S("comb_ready"), l + 1)
                for t in range(2):
                    ins = nc.tensor.transpose(bank[1][0:NE, P * t:P * t + P], comb[:, t, :], ident)
                ins.then_inc(S("combT_psum"), 1)
                pe.wait_ge(S("combT_ready"), l + 1)
                pe.wait_ge(S("zeros_ready"), 1)
                for b in range(4):
                    mm(bank[b][:, :], zb[:, 0:P], zb[:, :], start=True, stop=True)

                at_ = MOE_AT[l]

                def gate_up(e, p, lap, first):
                    for j, sig in enumerate(("moe_gate_ready", "moe_up_ready")):
                        n = at_ + 3 * p + j
                        pe.wait_ge(slot_sem(n), lap * 16 + 16 * (n // NS + 1))
                        if not first and j == 0:
                            pe.wait_ge(S("moe_hid_ready"), e - 1)
                        for f in range(2):
                            for k in range(KT):
                                ins = mm(bank[4 + 2 * p + j][:, T2 * f:T2 * f + T2], up_view(n)[:, k, P * f:P * f + P],
                                         xn[:, k, 0:T2], start=(k == 0), stop=(k == KT - 1))
                        ins.then_inc(S(sig), 1)

                def expert_down(e, p, lap, last=False):
                    n = at_ + 3 * p + 2
                    pe.wait_ge(slot_sem(n), lap * 16 + 16 * (n // NS + 1))
                    pe.wait_ge(S("moe_hid_ready"), e + 1)
                    for f in range(2):
                        for d in range(KT):
                            ins = mm(bank[d // 2][:, T2 * (d % 2):T2 * (d % 2) + T2], down_view(n)[:, f, P * d:P * d + P],
                                     hm[:, p, T2 * f:T2 * f + T2], start=False, stop=True,
                                     skip_group_check=True)
                    ins.then_inc(S("moe_down_used"), 1)

                e0 = NE * l
                gate_up(e0, 0, 0, True)
                gate_up(e0 + 1, 1, 0, True)
                expert_down(e0, 0, 0)
                with pe.Fori(1, NE // 2) as i:
                    gate_up(i * 2 + e0, 0, i, False)
                    expert_down(i * 2 + (e0 - 1), 1, i - 1)
                    gate_up(i * 2 + (e0 + 1), 1, i, False)
                    expert_down(i * 2 + e0, 0, i)
                expert_down(e0 + NE - 1, 1, NE // 2 - 1, last=True)
            norm(7)
            pe.wait_ge(S("xn_ready"), 64)
            for t in range(2):
                for j in range(4):
                    n = 4 * t + j
                    if n >= 4:
                        pe.wait_ge(S("out_ready"), n - 3)
                    for c in range(2):
                        ins = nc.tensor.transpose(bank[1 + n % 4][:, P * c:P * c + P], xn[:, 2 * j + c, P * t:P * t + P], ident)
                    ins.then_inc(S("outT_ready"), 1)

        @block.vector
        def _(dve):
            n_chain = 0
            V = nc.vector

            def link(ins):
                nonlocal n_chain
                n_chain += 1
                ins.then_inc(S("dve_chain"), 1)
                dve.wait_ge(S("dve_chain"), n_chain)

            n_root = 0

            def inv_rms(dst, T=T1):
                nonlocal n_root
                dve.wait_ge(S("root_ready"), n_root + 1)
                V.reciprocal(dst, root[:, n_root % 2, 0:T]).then_inc(S("root_used"), 1)
                n_root += 1
                dve.wait_ge(S("root_used"), n_root)

            def norm(n):
                off, T = span[n]
                inv_rms(rstd[:, 0, 0:T], T)
                for k in range(KT):
                    V.scalar_tensor_tensor(xn[:, k, 0:T], hT[:, k, off:off + T], gain(G_NORM + KT * n + k), rstd[:, 0, 0:T],
                                           ALU.mult, ALU.mult).then_inc(S("xn_ready"), 1)

            def ffn(f):
                for i in range(FT):
                    g = FT * f + i
                    dve.wait_ge(S("silu_ready"), g + 1)
                    dve.wait_ge(S("up_ready"), g + 1)
                    V.tensor_tensor(hid[:, i, :], sil[:, i % 2, :], bank[2 * (i % 4) + 1][:, 0:T1], ALU.mult
                                    ).then_inc(S("hid_ready"), 1)

            def residual(k, r, factor):
                off, T = span[r]
                for d in range(KT):
                    dve.wait_ge(S("y_ready"), 8 * k + d + 1)
                    h = hT[:, d, 0 if T == T1 else off:T1]
                    V.scalar_tensor_tensor(h, bank[d][:, 0:T], factor, h, ALU.mult, ALU.add
                                           ).then_inc(S("residual_ready"), 1)

            def maxes(g):
                u = units_all[g]
                dve.wait_ge(S("scores_ready"), g + 1)
                nq, L = u["nq"], u["L"]
                bias = u["bias"]
                if u["kind"] == "b":
                    dve.wait_ge(S("bias_ready"), g - SEG_B[0] + 1)
                    bias = gb[0:nq, g % 2, 0:L]
                for m in range(u["maps"]):
                    ins = V.tensor_tensor_reduce(s_sb[0:nq, g % 2, m, 0:L], bank[2 * (g % 2) + m][0:nq, 0:L], bias,
                                                 1.0, -3.4e38, ALU.add, ALU.max, mx[0:nq, g % 2, m:m + 1])
                    if m < u["maps"] - 1:
                        link(ins)
                ins.then_inc(S("scores_taken"), 1)
                dve.wait_ge(S("scores_taken"), g + 1)
                V.tensor_scalar(nmx[0:nq, g % 2, 0:u["maps"]], mx[0:nq, g % 2, 0:u["maps"]], -1.0, None, ALU.mult
                                ).then_inc(S("max_ready"), 1)

            def weights(g):
                u = units_all[g]
                dve.wait_ge(S("exps_ready"), g + 1)
                nq, L = u["nq"], u["L"]
                if g >= 2:
                    dve.wait_ge(S("aT_ready"), g - 1)
                r = rs[0:nq, g % 2, 0:u["maps"]]
                link(V.reciprocal(r, sums[0:nq, g % 2, 0:u["maps"]]))
                a = a_sb[0:nq, g % 2, 0:L]
                if u["kind"] == "a":
                    link(V.tensor_scalar(rs[0:nq, g % 2, 1:2], rs[0:nq, g % 2, 1:2], lamb[0:nq, 4:5], None, ALU.mult))
                    link(V.tensor_scalar(a, s_sb[0:nq, g % 2, 0, 0:L], rs[0:nq, g % 2, 0:1], None, ALU.mult))
                    ins = V.scalar_tensor_tensor(a, s_sb[0:nq, g % 2, 1, 0:L], rs[0:nq, g % 2, 1:2], a, ALU.mult, ALU.add)
                else:
                    ins = V.tensor_scalar(a, s_sb[0:nq, g % 2, 0, 0:L], rs[0:nq, g % 2, 0:1], None, ALU.mult)
                ins.then_inc(S("probs_ready"), 1)
                dve.wait_ge(S("probs_ready"), g + 1)

            dve.wait_ge(S("gains_loaded"), 16)
            link(V.tensor_scalar(gn[:, 0:64], gn[:, 0:64], math.sqrt(D), None, ALU.mult))
            link(V.tensor_scalar(gn[:, G_AK:G_AK + 1], gn[:, G_AK:G_AK + 1], math.sqrt(ADK), None, ALU.mult))
            link(V.tensor_scalar(gn[:, G_AQ:G_AQ + 1], gn[:, G_AQ:G_AQ + 1], math.sqrt(ADK) * ADK ** -0.5, None, ALU.mult))
            link(V.tensor_scalar(gn[:, G_BKV:G_BKV + 2], gn[:, G_BKV:G_BKV + 2], math.sqrt(BDC), None, ALU.mult))
            link(V.tensor_scalar(gn[:, G_BQ:G_BQ + 2], gn[:, G_BQ:G_BQ + 2], math.sqrt(BDC) * BDC ** -0.5, None, ALU.mult))
            link(V.tensor_scalar(gn[:, G_SUB:G_SUB + 1], gn[:, G_SUB:G_SUB + 1], math.sqrt(ADV) * (1.0 - LAM0), None, ALU.mult))
            link(V.tensor_scalar(gn[:, G_QN:G_QN + 4], gn[:, G_QN:G_QN + 4], math.sqrt(256), None, ALU.mult))
            link(V.tensor_scalar(gn[:, G_KVN:G_KVN + 2], gn[:, G_KVN:G_KVN + 2], math.sqrt(128), None, ALU.mult))
            for j in range(2):
                a, b = G_LAM + 2 * j * ADK, G_LAM + (2 * j + 1) * ADK
                ins = V.tensor_tensor_reduce(lprod[:], gn[:, a:a + ADK], gn[:, b:b + ADK], 1.0, 0.0,
                                             ALU.mult, ALU.add, lamb[:, j:j + 1])
                if j == 0:
                    link(ins)
            ins.then_inc(S("lam_sums_ready"), 1)
            dve.wait_ge(S("lam_exp_ready"), 1)
            link(V.scalar_tensor_tensor(lamb[:, 4:5], lamb[:, 3:4], -LAM0, lamb[:, 2:3], ALU.add, ALU.subtract))
            dve.wait_ge(S("input_saved"), 8)
            norm(0)
            dve.wait_ge(S("bias_psum"), 1)
            dve.wait_ge(S("consts_loaded"), 16)
            V.tensor_tensor(btab[:, :], bank[7][0:8, :], cst[0:8, C_OM:C_OM + ROW], ALU.add).then_inc(S("bias_rows_ready"), 1)
            ffn(0)
            residual(0, 0, 0.5)
            dve_total = 8
            norm(1)
            for t in range(8):
                inv_rms(rstd[:, t % 2, :])
                V.scalar_tensor_tensor(uT[:, t, :], uT[:, t, :], gain(G_AQ if t < 4 else G_AK), rstd[:, t % 2, :],
                                       ALU.mult, ALU.mult).then_inc(S("norm1_done"), 1)
            dve.wait_ge(S("norm1_done"), 8)
            inv_rms(rstd[:, 0, :])
            for t in range(2):
                V.scalar_tensor_tensor(uT[:, 12 + t, :], uT[:, 12 + t, :], gain(G_BKV + t), rstd[:, 0, :],
                                       ALU.mult, ALU.mult).then_inc(S("normc_done"), 1)
            for h in range(BH):
                inv_rms(rstd[:, (h + 1) % 2, :])
                for t in range(2):
                    V.scalar_tensor_tensor(qlT[:, 2 * h + t, :], qlT[:, 2 * h + t, :], gain(G_BQ + t),
                                           rstd[:, (h + 1) % 2, :], ALU.mult, ALU.mult).then_inc(S("normq_done"), 1)
            dve.wait_ge(S("normq_done"), 8)
            for i in range(3):
                q0, nq, L = qcols(i)
                s = score[0:nq, 0:L]
                for h in range(IH):
                    n = IH * i + h
                    dve.wait_ge(S("relu_ready"), n + 1)
                    prev = cst[0:nq, C_CM + P * (2 - i):C_CM + P * (2 - i) + L] if h == 0 else s
                    V.scalar_tensor_tensor(s, rel[0:nq, n % 4, 0:L], iw[0:nq, i, h:h + 1], prev, ALU.mult, ALU.add
                                           ).then_inc(S("score_added"), 1)
                    dve.wait_ge(S("score_added"), n + 1)
                for r in range(TOPK // 8):
                    link(V.max(top8[0:nq, :], s))
                    link(V.match_replace(s, top8[0:nq, :], s, TAKEN))
                V.tensor_scalar(selb[0:nq, i, 0:L], s, 0.5 * TAKEN, NEG, ALU.is_gt, ALU.mult).then_inc(S("selected"), 1)
                dve.wait_ge(S("selected"), i + 1)
            dve.wait_ge(S("G_loaded"), 16 * 8)
            steps(SEG_A, maxes, weights)
            for h in range(AH):
                inv_rms(rstd[:, h % 2, :])
                V.scalar_tensor_tensor(mixT[:, h, :], mixT[:, h, :], gain(G_SUB), rstd[:, h % 2, :],
                                       ALU.mult, ALU.mult).then_inc(S("subln_done"), 1)
            steps(SEG_B, maxes, weights)
            residual(1, 1, 1.0)
            norm(2)
            ffn(1)
            residual(2, 2, 0.5)

            for l in range(LAYERS):
                norm(3 + 2 * l)
                base = U1 + U2 * l
                ck, sk = (cst[64:96, C_COS + j * T2:C_COS + (j + 1) * T2] for j in (2, 3))
                dve.wait_ge(S("proj_ready"), base + 5)
                V.tensor_tensor(rt1[64:96, 0, :], bank[(base + 3) % 8][64:96, 0:T2], ck, ALU.mult).then_inc(S("rotary_read"), 1)
                V.tensor_tensor(rt2[64:96, 0, :], bank[(base + 4) % 8][64:96, 0:T2], sk, ALU.mult).then_inc(S("rotary_read"), 1)
                dve.wait_ge(S("rotary_read"), 2 * (l + 1))
                V.tensor_tensor(kcat[64:96, :, :], spread(rt1[64:96, 0:1, :], 1, MH), spread(rt2[64:96, 0:1, :], 1, MH),
                                ALU.add).then_inc(S("k_rope_saved"), 1)
                dve.wait_ge(S("k_rope_saved"), l + 1)
                inv_rms(rstd[:, 0, 0:T2], T2)
                for t in range(2):
                    V.scalar_tensor_tensor(cq[:, t, :], cq[:, t, :], gain(G_QN + 2 * l + t), rstd[:, 0, 0:T2],
                                           ALU.mult, ALU.mult).then_inc(S("lat_ready"), 1)
                inv_rms(rstd[:, 1, 0:T2], T2)
                V.scalar_tensor_tensor(ckv[:, 0, :], ckv[:, 0, :], gain(G_KVN + l), rstd[:, 1, 0:T2],
                                       ALU.mult, ALU.mult).then_inc(S("lat_ready"), 1)
                cqt, sqt = (spread(cst[64:96, C_COS + j * T2:C_COS + (j + 1) * T2].rearrange("p (a n) -> p a n", a=1), 1, 2)
                            for j in (0, 1))
                for n in range(4):
                    dve.wait_ge(S("q_up_ready"), 4 * l + n + 1)
                    b0 = bank[2 * (n % 2)][64:96, :].rearrange("p (h n) -> p h n", h=2)
                    b1 = bank[2 * (n % 2) + 1][64:96, :].rearrange("p (h n) -> p h n", h=2)
                    link(V.tensor_tensor(rt1[64:96, :, :], b0, cqt, ALU.mult))
                    link(V.tensor_tensor(rt2[64:96, :, :], b1, sqt, ALU.mult))
                    V.tensor_tensor(qcat[64:96, 2 * n:2 * n + 2, :], rt1[64:96, :, :], rt2[64:96, :, :], ALU.add
                                    ).then_inc(S("q_rope_saved"), 1)
                    dve.wait_ge(S("q_rope_saved"), 4 * l + n + 1)
                steps(SEG_M[l], maxes, weights)
                nm = cst[:, C_NM:C_NM + 384]
                for h in range(SH):
                    dve.wait_ge(S("z_ready"), SH * l + h + 1)
                    dve.wait_ge(S("aT_saved"), SEG_M[l][1])
                    dve.wait_ge(S("o_ready"), SEG_M[l][1])
                    link(V.scalar_tensor_tensor(zm[:, h, :], bank[h][:, 0:384], 0.125, nm, ALU.mult, ALU.add))
                    V.scalar_tensor_tensor(ln[:, h, :], zm[:, h, :], -1.0, zm[:, h, :], ALU.mult, ALU.min
                                           ).then_inc(S("nabs_ready"), 1)
                for h in range(SH):
                    dve.wait_ge(S("ln_ready"), SH * l + h + 1)
                    V.scalar_tensor_tensor(ln[:, h, :], zm[:, h, :], 0.0, ln[:, h, :], ALU.max, ALU.add
                                           ).then_inc(S("softplus_ready"), 1)
                for h in range(SH):
                    dve.wait_ge(S("later_ready"), SH * l + h + 1)
                    V.tensor_tensor(zm[:, h, :], zm[:, h, :], bank[h][:, 0:384], ALU.subtract
                                    ).then_inc(S("stick_log_ready"), 1)
                residual(3 + l if l == 0 else 4, 3, 1.0)
                norm(4 + 2 * l)
                dve.wait_ge(S("router_ready"), l + 1)
                bias = spread(gn[:, G_RB + 36 * l:G_RB + 36 * l + 36].rearrange("p (a n) -> p a n", a=1), 1, 2)
                link(V.tensor_tensor(rl[:, :, :], bank[0][:, 0:72].rearrange("p (t n) -> p t n", t=2), bias, ALU.add))
                gl = rl[:, :, 0:4]
                gmax = small[:, 0:2]
                bc = lambda v, n: spread(v.rearrange("p (t a) -> p t a", a=1), 2, n)
                v4 = lambda o: small[:, o:o + 8].rearrange("p (t g) -> p t g", t=2)
                link(V.tensor_reduce(gmax, gl, AX_X, ALU.max))
                V.tensor_tensor(v4(8), gl, bc(gmax, 4), ALU.subtract).then_inc(S("router_shifted"), 1)
                dve.wait_ge(S("router_shifted"), l + 1)

                fo = lambda n: spread(cst[:, C_FO:C_FO + n].rearrange("p (a n) -> p a n", a=1), 1, 2)

                def first_of(out, vals, top, n, tmp, tmp1):
                    link(V.tensor_tensor(out, vals, bc(top, n), ALU.is_equal))
                    link(V.tensor_tensor(tmp, out, fo(n), ALU.mult))
                    link(V.tensor_reduce(tmp1, tmp, AX_X, ALU.max))
                    link(V.tensor_tensor(out, tmp, bc(tmp1, n), ALU.is_equal))

                goh = v4(24)
                first_of(goh, gl, gmax, 4, v4(32), small[:, 2:4])
                el = rl[:, :, 4:36].rearrange("p t (g e) -> p t g e", g=4)
                tt = t48.rearrange("p t (g e) -> p t g e", g=4)
                goh8 = spread(goh.rearrange("p t (g a) -> p t g a", a=1), 3, 8)
                for t in range(2):
                    link(V.tensor_tensor(tt[:, t], el[:, t], goh8[:, t], ALU.mult))
                link(V.tensor_reduce(e8[:, :, :], t48.rearrange("p t (g e) -> p t e g", g=4), AX_X, ALU.add))
                v8 = lambda o: small[:, o:o + 16].rearrange("p (t g) -> p t g", t=2)
                o1, o2, tmp8, rest = v8(48), v8(64), v8(80), v8(96)
                l1, l2 = small[:, 4:6], small[:, 6:8]
                link(V.tensor_reduce(l1, e8[:, :, :], AX_X, ALU.max))
                first_of(o1, e8[:, :, :], l1, 8, tmp8, small[:, 42:44])
                link(V.scalar_tensor_tensor(rest, o1, NEG, e8[:, :, :], ALU.mult, ALU.add))
                link(V.tensor_reduce(l2, rest, AX_X, ALU.max))
                first_of(o2, rest, l2, 8, tmp8, small[:, 42:44])
                V.tensor_tensor(small[:, 40:42], l2, l1, ALU.subtract).then_inc(S("router_gap"), 1)
                dve.wait_ge(S("router_exp1"), l + 1)
                dve.wait_ge(S("router_gap"), l + 1)
                psel, den = small[:, 112:114], small[:, 114:116]
                link(V.tensor_reduce(psel, v4(16), AX_X, ALU.add))
                dve.wait_ge(S("router_exp2"), l + 1)
                e2 = small[:, 44:46]
                link(V.scalar_tensor_tensor(den, e2, 1.0, psel, ALU.add, ALU.mult))
                w1, w2 = small[:, 116:118], small[:, 118:120]
                link(V.reciprocal(w1, den))
                link(V.tensor_tensor(w2, w1, e2, ALU.mult))
                link(V.tensor_tensor(o1, o1, bc(w1, 8), ALU.mult))
                link(V.tensor_tensor(o2, o2, bc(w2, 8), ALU.mult))
                link(V.tensor_tensor(o1, o1, o2, ALU.add))
                for t in range(2):
                    inner = spread(o1[:, t:t + 1, :], 1, 4)
                    ins = V.tensor_tensor(comb[:, t, :].rearrange("p (g e) -> p g e", g=4), goh8[:, t], inner, ALU.mult)
                    if t == 0:
                        link(ins)
                ins.then_inc(S("comb_ready"), 1)

                dve.wait_ge(S("comb_loaded"), 16 * (l + 1))

                def hidden(e, p, ce, first, chain):
                    dve.wait_ge(S("moe_silu_ready"), e + 1)
                    dve.wait_ge(S("moe_up_ready"), e + 1)
                    V.tensor_tensor(um[:, :], silm[:, p, :], bank[5 + 2 * p][:, :], ALU.mult).then_inc(S("moe_product"), 1)
                    dve.wait_ge(S("moe_product"), e + 1)
                    if not first:
                        dve.wait_ge(S("moe_down_used"), e - 1)
                    c = spread(comb_bc[:, bass.ds(ce, 1), :], 1, 2)
                    V.tensor_tensor(hm[:, p, :].rearrange("p (f n) -> p f n", f=2), um.rearrange("p (f n) -> p f n", f=2),
                                    c, ALU.mult).then_inc(S("moe_hid_ready"), 1)
                    dve.wait_ge(S("moe_hid_ready"), e + 1)

                hidden(NE * l, 0, 0, True, 0)
                hidden(NE * l + 1, 1, 1, True, 0)
                with dve.Fori(1, NE // 2) as i:
                    for p in range(2):
                        hidden(i * 2 + (NE * l + p), p, i * 2 + p, False, 0)
                dve.wait_ge(S("moe_down_used"), NE * (l + 1))
                for d in range(KT):
                    h = hT[:, d, NMETA:T1]
                    V.tensor_tensor(h, bank[d // 2][:, T2 * (d % 2):T2 * (d % 2) + T2], h, ALU.add
                                    ).then_inc(S("residual_ready"), 1)
            norm(7)


def _chunks(w):
    n = w.shape[1]
    return w.reshape(KT, P, n // 256, 256).transpose(2, 1, 0, 3).reshape(n // 256, P, CH)


def _row_chunks(w):
    n = w.shape[0]
    return w.reshape(n // 256, 2, P, D).transpose(0, 2, 1, 3).reshape(n // 256, P, CH)


def _pad_cols(w, n):
    return np.concatenate([w, np.zeros((w.shape[0], n - w.shape[1]), w.dtype)], axis=1)


def _pairs(a, b):
    return np.stack([a, b], axis=1).reshape(-1, P, CH)


def _layout(i):
    col = lambda v: np.ascontiguousarray(v.reshape(-1, P).T)
    parts = []
    for f in ("ffn1", "ffn2"):
        gu = _pairs(_chunks(i[f + "_w_gate"][0]), _chunks(i[f + "_w_up"][0]))
        parts.append([gu, _row_chunks(i[f + "_w_down"][0])])
    w_in = i["w_in"][0]
    first_in = np.concatenate([w_in[:, 0:2816], _pad_cols(w_in[:, 2816:2888], 256)], axis=1)
    stream = parts[0] + [_chunks(first_in), _row_chunks(i["w_out"][0])] + parts[1]
    small2 = []
    for l in range(LAYERS):
        w = i["w_in_2"][l]
        w = np.concatenate([w[:, 0:256], _pad_cols(w[:, 256:416], 256), w[:, 416:1440]], axis=1)
        stream += [_chunks(w), _row_chunks(i["w_out_2"][l])]
        g, u, d = (i[k][l].reshape(NE, -1, i[k].shape[-1]) for k in ("w_gate_2", "w_up_2", "w_down_2"))
        g, u = (a.reshape(NE, KT, P, 256).transpose(0, 2, 1, 3).reshape(NE, P, CH) for a in (g, u))
        d = d.reshape(NE, 2, P, D).transpose(0, 2, 1, 3).reshape(NE, P, CH)
        stream.append(np.stack([g, u, d], axis=1).reshape(3 * NE, P, CH))
        wp = np.zeros((P, 2, P), np.float32)
        for t in range(2):
            for j in range(2):
                wp[64 * j:64 * j + 64, t, 64 * j:64 * j + 64] = i["pool_w_2"][l][2 * t + j]
        rt = np.concatenate([i["w_group_2"][l], i["w_expert_2"][l]], axis=1)
        small2.append(np.concatenate([
            i["w_uq_2"][l].reshape(2, P, 768).transpose(1, 0, 2).reshape(P, -1),
            i["w_ukv_2"][l].reshape(P, -1),
            wp.reshape(P, -1),
            rt.reshape(KT, P, 36).transpose(1, 0, 2).reshape(P, -1)], axis=1))
    norms = [i["ffn1_norm"][0], i["mix_norm"][0], i["ffn2_norm"][0]]
    for l in range(LAYERS):
        norms += [i["norm1_g_2"][l], i["norm2_g_2"][l]]
    norms.append(i["final_g_2"])
    twice = lambda v: np.concatenate([v, v]).reshape(P, 1)
    rows = [i[f"a_lambda_{k}"][0] for k in ("q1", "k1", "q2", "k2")]
    for l in range(LAYERS):
        rows += [i["b_group_2"][l], i["b_expert_2"][l]]
    gains = [col(v) for v in norms] + [twice(i["a_q_norm"][0]), twice(i["a_k_norm"][0]), col(i["b_kv_norm"][0]),
                                       col(i["b_q_norm"][0]), col(i["a_subln"][0])]
    gains += [col(i["q_norm_g_2"][l]) for l in range(LAYERS)] + [col(i["kv_norm_g_2"][l]) for l in range(LAYERS)]
    gains += [col(i["pool_scale_2"][l]) for l in range(LAYERS)]
    gains.append(np.broadcast_to(np.concatenate(rows)[None], (P, 4 * ADK + LAYERS * 36)))
    gains.append(np.broadcast_to(np.array([w * EPS for w in EPS_AT], np.float32), (P, len(EPS_AT))))
    return {
        "stream": np.concatenate(stream),
        "gains": np.concatenate(gains, axis=1),
        "consts": constants(),
        "x_tok": np.concatenate([i["meta_tokens"], i["x"][0]]),
        "rel_bias": i["rel_bias"],
        "wuk": i["b_w_uk"][0].transpose(1, 0, 2),
        "wuv": i["b_w_uv"][0].reshape(4, 2, P, P).transpose(2, 0, 1, 3),
        "small2": np.stack(small2),
    }


def kernel(**inputs):
    import concourse.bacc as bacc
    from concourse.bass_utils import run_bass_kernel_spmd

    nc = bacc.Bacc("TRN2", target_bir_lowering=False, num_devices=1)
    arrays, args = {}, []
    for name, a in _layout({k: np.asarray(v) for k, v in inputs.items()}).items():
        a = np.ascontiguousarray(a)
        arrays[f"in_{name}"] = a
        args.append(nc.dram_tensor(f"in_{name}", a.shape, mybir.dt.from_np(a.dtype), kind="ExternalInput").ap())
    out = nc.dram_tensor("out", (1, SEQ, D), F32, kind="ExternalOutput").ap()
    build(nc, *args, out)
    r = run_bass_kernel_spmd(nc, [arrays], core_ids=[0])
    return r.results[0]["out"]
```

```python
from contextlib import ExitStack
import math

import numpy as np

import concourse.bass as bass
from concourse import mybir

F32 = mybir.dt.float32
F32R = mybir.dt.float32r
I32 = mybir.dt.int32
BF16 = mybir.dt.bfloat16
ALU = mybir.AluOpType
ACT = mybir.ActivationFunctionType
AX_X = mybir.AxisListType.X

P = 128
D = 1024
KT = D // P
NMETA, SEQ = 16, 256
T1 = NMETA + SEQ
T2 = SEQ
D_FF = 2816
FT = D_FF // P
FC = FT // 2
CH = KT * 256
AH, ADK, ADV = 4, 64, 128
BH, BDC = 4, 256
IH, TOPK = 8, 64
BLOCKS1 = [(0, 128), (128, 128), (256, T1 - 256)]
BLOCKS2 = [(0, 128), (128, 128)]
MH = 8
SH = 4
NE = 32
LAYERS = 2
CAP = 64
PAIRS = NE // 2
NEG = -1e30
TAKEN = -3e38
EPS = 1e-6
LAM0 = 0.8 - 0.6 * math.exp(0.0)
GX = 384
ROW = 512
NS = 6

G_NORM = 0
G_AQ, G_AK, G_BKV, G_BQ, G_SUB = 64, 65, 66, 68, 70
G_QN, G_KVN, G_PS = 71, 75, 77
G_LAM = 81
G_RB = G_LAM + 4 * ADK
G_EPS = G_RB + LAYERS * 36
EPS_AT = {1024: 0, 64: 1, 256: 2, 128: 3}
G_ALL = G_EPS + len(EPS_AT)

C_ID, C_ONE, C_BD, C_UP = 0, 128, 256, 384
C_CM = 512
C_M2 = C_CM + GX
C_NM = C_M2 + 256
C_COS = C_NM + 384
C_IC = C_COS + 4 * T2
C_FO = C_IC + 2 * T2
C_OH = C_FO + 32
C_OM = C_OH + ROW
C_IO = C_OM + ROW
C_BE = C_IO + CAP
C_ALL = C_BE + P

NORM_D = {"first_in": 12, "second_in": 6}


def spread(ap, axis, n):
    shape = list(ap.shape)
    shape[axis] = n
    return ap.broadcast_to(shape)


def constants():
    c = np.zeros((P, C_ALL), np.float32)
    p = np.arange(P)
    c[:, C_ID:C_ID + P] = np.eye(P)
    c[:, C_ONE:C_ONE + P] = 1.0
    c[:, C_BD:C_BD + P] = (p[:, None] // 64) == (p[None, :] // 64)
    c[:, C_UP:C_UP + P] = p[:, None] >= p[None, :]
    x = np.arange(GX)
    c[:, C_CM:C_CM + GX] = np.where(p[:, None] + 256 - x[None, :] >= 0, 0.0, NEG)
    c[:64, C_M2 + 192:C_M2 + 256] = NEG
    q = np.arange(T2)
    c[:, C_NM:C_NM + T2] = np.where(p[:, None] < q[None, :], 0.0, NEG)
    c[:, C_NM + T2:C_NM + 384] = np.where(p[:, None] < p[None, :], 0.0, NEG)
    inv = (np.float32(10000.0) ** (-np.arange(0, 32, 2, dtype=np.float32) / np.float32(32))).astype(np.float32)
    ang = np.arange(T2, dtype=np.float32)[:, None] * inv[None, :]
    cos, sin = np.cos(ang).T, np.sin(ang).T
    cos2, sin2 = np.concatenate([cos, cos]), np.concatenate([-sin, sin])
    s = 96.0 ** -0.5
    for j, t in enumerate((cos2 * s, sin2 * s, cos2, sin2)):
        c[64:96, C_COS + j * T2:C_COS + (j + 1) * T2] = t
    for g, w in enumerate((2, 4, 8, 16)):
        r = slice(64 * (g % 2), 64 * (g % 2) + 64)
        c[r, C_IC + (g // 2) * T2:C_IC + (g // 2 + 1) * T2] = 1.0 / np.minimum(q + 1.0, w)
    c[:, C_FO:C_FO + 32] = 32 - np.arange(32)
    n = 383 - np.arange(ROW)
    nf = np.maximum(n, 1).astype(np.float32)
    large = 16 + (np.log(nf / np.float32(16)) / np.float32(math.log(8)) * np.float32(16)).astype(np.int32)
    bucket = np.where(np.maximum(n, 0) < 16, np.maximum(n, 0), np.minimum(large, 31))
    c[:32, C_OH:C_OH + ROW] = np.arange(32)[:, None] == bucket[None, :]
    c[:, C_OM:C_OM + ROW] = np.where(n >= 0, 0.0, NEG)
    c[:, C_IO:C_IO + CAP] = np.arange(CAP)
    c[:, C_BE:C_BE + P] = p[:, None] < p[None, :]
    return c


def build(nc, stream, gains, consts, x_tok, rel_bias, wuk, wuv, small2, out):
    with ExitStack() as ctx:
        sems = {}

        def S(name):
            if name not in sems:
                sems[name] = ctx.enter_context(nc.semaphore(name))
            return sems[name]

        def sb(name, shape, dt=F32):
            return ctx.enter_context(nc.sbuf_tensor(name, shape, dt))

        ring = sb("ring", [P, NS, CH])
        hT = sb("hT", [P, KT, T1])
        xn = sb("xn", [P, KT, T1])
        sq = sb("sq", [P, 10, T1])
        root = sb("root", [P, 2, T1])
        rstd = sb("rstd", [P, 2, T1])
        mixT = sb("mixT", [P, KT, T1])
        G = sb("G", [P, 8, GX])
        cst = sb("cst", [P, C_ALL])
        gn = sb("gn", [P, G_ALL])
        w_uk = sb("w_uk", [P, 4, 256])
        w_uv = sb("w_uv", [P, 4, 2, P])
        SM = 1536 + 1024 + 256 + 288
        sm = sb("sm", [P, SM])
        w_uq = sm[:, 0:1536].rearrange("p (k n) -> p k n", k=2)
        w_ukv = sm[:, 1536:2560].rearrange("p (h n) -> p h n", h=MH)
        w_pool = sm[:, 2560:2816].rearrange("p (t n) -> p t n", t=2)
        w_rt = sm[:, 2816:3104].rearrange("p (k n) -> p k n", k=KT)
        rb = sb("rb", [32, 8])
        zb = sb("zb", [P, 512], BF16)
        wslot = sb("wslot", [P, 1])
        load = sb("load", [P, 1])
        load_i = sb("load_i", [P, 1], I32)
        mx = sb("mx", [P, 2, 2])
        nmx = sb("nmx", [P, 2, 2])
        sums = sb("sums", [P, 2, 2])
        rs = sb("rs", [P, 2, 2])
        top8 = sb("top8", [P, 8])
        lamb = sb("lamb", [P, 8])
        lprod = sb("lprod", [P, ADK])
        arena_space = nc.sbuf_tensor("arena", [P, 16900], F32)
        arena = arena_space.__enter__()
        arena_space.__exit__(None, None, None)
        x_hi = sb("x_hi", [P, 2, D], F32R)
        x_lo = sb("x_lo", [P, 2, D], F32R)
        slots = sb("slots", [P, 2, 2, P], F32R)
        slotsT = sb("slotsT", [P, T2], F32R)
        o_hi = sb("o_hi", [P, D], F32R)
        o_lo = sb("o_lo", [P, D], F32R)

        at = {}

        def carve(name, off, *shape):
            n = int(np.prod(shape))
            at[name] = off + n
            assert off + n <= 16900, (name, off + n)
            v = arena[:, off:off + n]
            if len(shape) == 2:
                v = v.rearrange("p (a b) -> p a b", a=shape[0])
            if len(shape) == 3:
                v = v.rearrange("p (a b c) -> p a b c", a=shape[0], b=shape[1])
            return v

        xtok = carve("xtok", 0, 3, D)
        hid = carve("hid", 0, FT, T1)
        sil = carve("sil", at["hid"], 2, T1)
        uT = carve("uT", 0, 18, T1)
        va = carve("va", at["uT"], 3, 512)
        ikT = carve("ikT", at["va"], T1)
        iw = carve("iw", at["ikT"], 3, IH)
        qlT = carve("qlT", at["iw"], 8, T1)
        ctok = carve("ctok", at["qlT"], 3, BDC)
        selb = carve("selb", at["ctok"], 3, T1)
        olT = carve("olT", at["selb"], 8, T1)
        W0 = at["olT"]
        s_sb = carve("s_sb", W0, 2, 2, 272)
        a_sb = carve("a_sb", at["s_sb"], 2, 272)
        aT = carve("aT", at["a_sb"], 2, 384)
        gb = carve("gb", at["aT"], 2, 272)
        score = carve("score", W0, 272)
        rel = carve("rel", W0 + 272, 4, 272)
        score2 = carve("score2", W0 + 272 * 5, 272)
        qcat = carve("qcat", 0, MH, T2)
        kcat = carve("kcat", at["qcat"], MH, T2)
        vm = carve("vm", at["kcat"], 2, 512)
        qbT = carve("qbT", at["vm"], 2, T2)
        kbT = carve("kbT", at["qbT"], 2, T2)
        vb = carve("vb", at["kbT"], 2, T2)
        cq = carve("cq", at["vb"], 2, T2)
        ckv = carve("ckv", at["cq"], 1, T2)
        wuqs = carve("wuqs", at["ckv"], 2, MH, 32)
        wkrs = carve("wkrs", at["wuqs"], KT, 32)
        rt1 = carve("rt1", at["wkrs"], 2, T2)
        rt2 = carve("rt2", at["rt1"], 2, T2)
        PO = at["rt2"]
        upad = carve("upad", PO, 2, 272)
        ps2 = carve("ps2", at["upad"], 2, 272)
        ps4 = carve("ps4", at["ps2"], 2, 272)
        pd = carve("pd", at["ps4"], 2, T2)
        assert at["pd"] <= W0, (at["pd"], W0)
        zm = carve("zm", W0, SH, 384)
        ln = carve("ln", at["zm"], SH, 384)
        comb_bc = carve("comb_bc", 0, NE, T2)
        silm = carve("silm", at["comb_bc"], 2, 512)
        um = carve("um", at["silm"], 512)
        hm = carve("hm", at["um"], 2, 512)
        rl = carve("rl", at["hm"], 2, 36)
        comb = carve("comb", at["rl"], 2, NE)
        combT = carve("combT", at["comb"], T2)
        e8 = carve("e8", at["combT"], 2, 8)
        t48 = carve("t48", at["e8"], 2, NE)
        small = carve("small", at["t48"], 160)
        sel = carve("sel", at["small"], 2, NE)
        posm = carve("posm", at["sel"], 2, NE)
        XF = 6912
        xg = carve("xg", XF, KT, P)
        hs = carve("hs", at["xg"], 256)
        sl = carve("sl", at["hs"], 256)
        slotw = carve("slotw", at["sl"], 2, P)
        assert at["slotw"] <= at["comb_bc"] + 2560
        otok = carve("otok", 0, 2, D)
        btab = carve("btab", at["sil"], ROW)[0:8, :]

        bank = [ctx.enter_context(nc.psum_tensor(f"bank{i}", [P, 512], F32)) for i in range(8)]
        bias_rows = nc.dram_tensor("bias_rows", (8, ROW), F32).ap()
        bias_skew = nc.dram_tensor("bias_skew", (P, 8 * ROW), F32).ap()
        comb_dram = nc.dram_tensor("comb_dram", (LAYERS, NE, T2), F32).ap()

        ident, ones = cst[:, C_ID:C_ID + P], cst[:, C_ONE:C_ONE + P]
        bd64, upper = cst[:, C_BD:C_BD + P], cst[:, C_UP:C_UP + P]

        def gain(c):
            return gn[:, c:c + 1]

        span = [(0, T1)] * 3 + [(NMETA, T2)] * 5

        PAIR_ORDER = [("moe_gate_ready", 0), ("moe_up_ready", 0), ("moe_gate_ready", 1), ("moe_up_ready", 1),
                      ("moe_down_used", 0), ("moe_down_used", 1)]

        freed = []
        down_first = []
        used = 0
        units = 0
        MOE_AT = []
        STARTS = []

        def plan_ffn(f, k):
            nonlocal used
            for c in range(FC):
                freed.append(("gate_ready", 2 * FC * f + 2 * c + 2))
                freed.append(("up_ready", 2 * FC * f + 2 * c + 2))
            plan_down(k, FC)

        def plan_down(k, n):
            nonlocal used
            for c in range(n - 1):
                used += 1
                freed.append(("down_used", used))
            freed.append(("y_ready", 8 * (k + 1)))

        def plan_proj(per_chunk):
            nonlocal units
            for n in per_chunk:
                units += n
                freed.append(("proj_ready", units))

        A_FFN1 = len(freed)
        plan_ffn(0, 0)
        A_IN1 = len(freed)
        PER1 = [2, 2, 2, 2, 3, 3, 2, 2, 2, 2, 2, 2]
        plan_proj(PER1)
        A_OUT1 = len(freed)
        plan_down(1, 4)
        A_FFN2 = len(freed)
        plan_ffn(1, 2)
        A_IN2, A_OUT2 = [], []
        PER2 = [2, 3, 2, 2, 1, 2]
        for l in range(LAYERS):
            A_IN2.append(len(freed))
            plan_proj(PER2)
            A_OUT2.append(len(freed))
            plan_down(3 + l, 4)
            MOE_AT.append(len(freed))
            for s in range(PAIRS):
                for j, (name, e) in enumerate(PAIR_ORDER):
                    freed.append((name, NE * l + 2 * s + e + 1))
        NCHUNK = len(freed)
        U1, U2 = sum(PER1), sum(PER2)
        SAVED2 = U2 - 2

        def chunk(n):
            return ring[:, n % NS, :]

        def up_view(n):
            return chunk(n).rearrange("p (k n) -> p k n", k=KT)

        def down_view(n):
            return chunk(n).rearrange("p (f n) -> p f n", f=2)

        def slot_sem(n):
            return S(f"slot{n % NS}_loaded")

        def loaded(eng, n):
            eng.wait_ge(slot_sem(n), 16 * (n // NS + 1))

        units_all = []

        def seg(make):
            at0 = len(units_all)
            units_all.extend(make)
            return at0, len(units_all)

        def block_bias(h, i, nq, L):
            x0 = P * (2 - i)
            return G[0:nq, h, x0:x0 + L]

        def unit_a(i, h):
            q0, nq = BLOCKS1[i]
            L = q0 + nq
            return dict(
                maps=2, nq=nq, L=L, q0=q0, kind="a", h=h, i=i,
                score=[[(uT[64 * m:64 * m + 64, h, q0:q0 + nq], uT[64 * m:64 * m + 64, 4 + h, 0:L])] for m in range(2)],
                bias=block_bias(h, i, nq, L),
                v=[lambda k, nk: va[0:nk, k, P * h:P * h + P]], base=0, M=P,
                out=mixT[:, h, q0:q0 + nq])

        def unit_b(i, h):
            q0, nq = BLOCKS1[i]
            L = q0 + nq
            return dict(
                maps=1, nq=nq, L=L, q0=q0, kind="b", h=h, i=i,
                score=[[(qlT[:, 2 * h + c, q0:q0 + nq], uT[:, 12 + c, 0:L]) for c in range(2)]],
                bias=None,
                v=[lambda k, nk, c=c: ctok[0:nk, k, P * c:P * c + P] for c in range(2)], base=0, M=P,
                out=olT[:, 2 * h:2 * h + 2, q0:q0 + nq])

        def unit_m(i, h):
            q0, nq = BLOCKS2[i]
            L = q0 + nq
            b = 64 * (h % 2)
            return dict(
                maps=1, nq=nq, L=L, q0=q0, kind="m", h=h, i=i,
                score=[[(qcat[0:96, h, q0:q0 + nq], kcat[0:96, h, 0:L])]],
                bias=cst[:, C_M2 + P * (1 - i):C_M2 + 256],
                v=[lambda k, nk: vm[0:nk, k, 64 * h:64 * h + 64]], base=b, M=64,
                out=mixT[b:b + 64, h // 2, q0:q0 + nq])

        SEG_A = seg([unit_a(i, h) for i in range(3) for h in range(AH)])
        SEG_B = seg([unit_b(i, h) for i in range(3) for h in range(BH)])
        SEG_M = [seg([unit_m(i, h) for i in range(2) for h in range(MH)]) for l in range(LAYERS)]

        def key_tiles(u):
            return [(k, min(P, u["L"] - P * k)) for k in range((u["L"] + P - 1) // P)]

        def steps(segment, *stages):
            a, b = segment
            for s in range(a, b + len(stages) - 1):
                for j, stage in enumerate(stages):
                    if a <= s - j < b:
                        stage(s - j)

        def qcols(i):
            q0, nq = BLOCKS1[i]
            return q0, nq, q0 + nq

        block = ctx.enter_context(nc.Block())

        @block.sync
        def _(sp):
            def load(n):
                if n >= NS:
                    name, v = freed[n - NS]
                    sp.wait_ge(S(name), v)
                sp.dma_start(chunk(n), stream[n]).then_inc(slot_sem(n), 16)

            n = 0
            for l in range(LAYERS):
                while n < MOE_AT[l] + 6:
                    load(n)
                    n += 1
                with sp.Fori(1, NE // 2) as i:
                    for j in range(6):
                        m = MOE_AT[l] + j
                        name, e = PAIR_ORDER[j]
                        sp.wait_ge(S(name), i * 2 + (NE * l - 1 + e))
                        sp.dma_start(chunk(m), stream[bass.ds(i * 6 + m, 1)].rearrange("a p n -> p (a n)")
                                     ).then_inc(slot_sem(m), 16)
                n = MOE_AT[l] + 3 * NE
            for t in range(2):
                sp.wait_ge(S("out_ready"), 4 * (t + 1))
                sp.dma_start(out[0, P * t:P * t + P, :], otok[:, t, :]).then_inc(S("out_written"), 16)
            sp.wait_ge(S("out_written"), 32)

        @block.gpsimd
        def _(pool):
            n_chain = 0

            def link(ins):
                nonlocal n_chain
                n_chain += 1
                ins.then_inc(S("pool_chain"), 1)
                pool.wait_ge(S("pool_chain"), n_chain)

            nc.gpsimd.memset(zb[:], 0.0).then_inc(S("zeros_ready"), 1)
            pool.wait_ge(S("bias_rows_ready"), 1)
            pool.dma_start(bias_rows, btab[:, :]).then_inc(S("bias_rows_written"), 16)
            pool.wait_ge(S("bias_rows_written"), 16)
            src = spread(bias_rows.rearrange("(a h) n -> a (h n)", a=1), 0, P)
            pool.dma_start(bias_skew, src).then_inc(S("bias_skew_written"), 16)
            pool.wait_ge(S("bias_skew_written"), 16)
            for h in range(8):
                src = bass.AP(bias_skew.tensor, 127 + ROW * h, [[8 * ROW - 1, P], [1, GX]])
                pool.dma_start(G[:, h, :], src).then_inc(S("G_loaded"), 16)

            for g in range(*SEG_B):
                u = units_all[g]
                pool.wait_ge(S("G_loaded"), 16 * 8)
                pool.wait_ge(S("selected"), u["i"] + 1)
                if g - SEG_B[0] >= 2:
                    pool.wait_ge(S("scores_taken"), g - 1)
                else:
                    pool.wait_ge(S("subln_done"), AH)
                nc.gpsimd.tensor_tensor(gb[0:u["nq"], g % 2, 0:u["L"]], block_bias(4 + u["h"], u["i"], u["nq"], u["L"]),
                                        selb[0:u["nq"], u["i"], 0:u["L"]], ALU.add).then_inc(S("bias_ready"), 1)

            for l in range(LAYERS):
                pool.wait_ge(S("small2_loaded"), 16 * (l + 1))
                if l == 0:
                    pool.wait_ge(S("residual_ready"), 8 * 3)
                else:
                    pool.wait_ge(S("residual_ready"), 8 * 5)
                wq = w_uq.rearrange("p k (h n) -> p k h n", h=MH)
                for k in range(2):
                    link(nc.gpsimd.tensor_copy(wuqs[:, k, :, 0:16], wq[:, k, :, 80:96]))
                    link(nc.gpsimd.tensor_copy(wuqs[:, k, :, 16:32], wq[:, k, :, 64:80]))
                pool.wait_ge(slot_sem(A_IN2[l] + 1), 16 * ((A_IN2[l] + 1) // NS + 1))
                wk = up_view(A_IN2[l] + 1)
                link(nc.gpsimd.tensor_copy(wkrs[:, :, 0:16], wk[:, :, 144:160]))
                nc.gpsimd.tensor_copy(wkrs[:, :, 16:32], wk[:, :, 128:144]).then_inc(S("swapped_ready"), 1)
                nc.gpsimd.memset(upad[:, :, 0:16], 0.0).then_inc(S("pad_ready"), 1)
                pool.wait_ge(S("pad_ready"), l + 1)
                pool.wait_ge(S("proj_saved"), U1 + SAVED2 * (l + 1))
                link(nc.gpsimd.tensor_tensor(ps2[:, :, 1:272], upad[:, :, 1:272], upad[:, :, 0:271], ALU.add))
                link(nc.gpsimd.tensor_tensor(ps4[:, :, 3:272], ps2[:, :, 3:272], ps2[:, :, 1:270], ALU.add))
                ic = cst[:, C_IC:C_IC + 2 * T2].rearrange("p (t n) -> p t n", t=2)
                link(nc.gpsimd.tensor_tensor(pd[0:64, 0, :], ps2[0:64, 0, 16:272], ic[0:64, 0, :], ALU.mult))
                link(nc.gpsimd.tensor_tensor(pd[64:128, 0, :], ps4[64:128, 0, 16:272], ic[64:128, 0, :], ALU.mult))
                link(nc.gpsimd.tensor_tensor(ps2[:, 1, 7:272], ps4[:, 1, 7:272], ps4[:, 1, 3:268], ALU.add))
                link(nc.gpsimd.tensor_tensor(pd[0:64, 1, :], ps2[0:64, 1, 16:272], ic[0:64, 1, :], ALU.mult))
                link(nc.gpsimd.tensor_tensor(ps4[:, 1, 15:272], ps2[:, 1, 15:272], ps2[:, 1, 7:264], ALU.add))
                link(nc.gpsimd.tensor_tensor(pd[64:128, 1, :], ps4[64:128, 1, 16:272], ic[64:128, 1, :], ALU.mult))
                nc.gpsimd.tensor_tensor(pd[:, :, :], pd[:, :, :], upad[:, :, 16:272], ALU.subtract
                                        ).then_inc(S("pool_d_ready"), 1)
                pool.wait_ge(S("load_known"), l + 1)
                with pool.If(pool.value_load(load_i[0:1, 0:1]) > CAP):
                    pool.wait_ge(S(f"combT_ready{l}"), 1)
                    pool.dma_start(comb_dram[l], combT[0:NE, :]).then_inc(S(f"comb_written{l}"), 16)
                    pool.wait_ge(S(f"comb_written{l}"), 16)
                    src = spread(comb_dram[l].rearrange("(a e) n -> a (e n)", a=1), 0, P)
                    pool.dma_start(comb_bc.rearrange("p e n -> p (e n)"), src).then_inc(S(f"comb_loaded{l}"), 16)
                    pool.wait_ge(S(f"comb_loaded{l}"), 16)
            pool.wait_ge(S("G_loaded"), 16 * 8)

        @block.scalar
        def _(act):
            n_chain = 0

            def link(ins):
                nonlocal n_chain
                n_chain += 1
                ins.then_inc(S("act_chain"), 1)
                act.wait_ge(S("act_chain"), n_chain)

            copy = nc.scalar.activation

            act.dma_start(cst[:], consts).then_inc(S("consts_loaded"), 16)
            act.dma_start(xtok[:, 0:2, :], x_tok[0:256].rearrange("(t p) n -> p t n", p=P)).then_inc(S("x_loaded"), 16)
            act.dma_start(xtok[0:16, 2, :], x_tok[256:272]).then_inc(S("x_loaded"), 16)
            act.dma_start(gn[:], gains).then_inc(S("gains_loaded"), 16)
            act.dma_start(rb[:], rel_bias).then_inc(S("rb_loaded"), 16)
            act.dma_start(w_uk[:], wuk).then_inc(S("wuk_loaded"), 16)
            act.dma_start(w_uv[:], wuv).then_inc(S("wuv_loaded"), 16)
            act.dma_start(sm[:], small2[0]).then_inc(S("small2_loaded"), 16)

            for d in range(KT):
                act.wait_ge(S("xT_ready"), d + 1)
                copy(hT[:, d, :], bank[d][:, 0:T1], ACT.Copy).then_inc(S("input_saved"), 1)
            act.wait_ge(S("lam_sums_ready"), 1)
            copy(lamb[:, 2:4], lamb[:, 0:2], ACT.Exp).then_inc(S("lam_exp_ready"), 1)

            n_root = 0

            def take_root(src, width, ready, v):
                nonlocal n_root
                act.wait_ge(S(ready), v)
                if n_root >= 2:
                    act.wait_ge(S("root_used"), n_root - 1)
                nc.scalar.activation(root[:, n_root % 2, 0:src.shape[1]], src, ACT.Sqrt, bias=gain(G_EPS + EPS_AT[width])
                                     ).then_inc(S("root_ready"), 1)
                n_root += 1

            def squares(n):
                off, T = span[n]
                for half in range(2):
                    if n == 0:
                        act.wait_ge(S("input_saved"), 4 * (half + 1))
                    else:
                        act.wait_ge(S("residual_ready"), 8 * (n - 1) + 4 * (half + 1))
                    copy(sq[:, 4 * half:4 * half + 4, 0:T], hT[:, 4 * half:4 * half + 4, off:off + T], ACT.Square
                         ).then_inc(S("squares_ready"), 1)
                if n == 0:
                    act.wait_ge(S("gains_loaded"), 16)
                take_root(bank[0][:, 0:T], D, "sumsq_ready", n + 1)

            def ffn(f):
                for i in range(FT):
                    g = FT * f + i
                    act.wait_ge(S("gate_ready"), g + 1)
                    if i >= 2:
                        act.wait_ge(S("hid_ready"), g - 1)
                    copy(sil[:, i % 2, :], bank[2 * (i % 4)][:, 0:T1], ACT.Silu).then_inc(S("silu_ready"), 1)

            def save(u, *ops):
                act.wait_ge(S("proj_ready"), u + 1)
                for op in ops[:-1]:
                    link(op())
                ops[-1]().then_inc(S("proj_saved"), 1)

            def exps(g):
                u = units_all[g]
                act.wait_ge(S("max_ready"), g + 1)
                for m in range(u["maps"]):
                    s = s_sb[0:u["nq"], g % 2, m, 0:u["L"]]
                    ins = nc.scalar.activation(s, s, ACT.Exp, bias=nmx[0:u["nq"], g % 2, m:m + 1],
                                               accum_out=sums[0:u["nq"], g % 2, m:m + 1])
                ins.then_inc(S("exps_ready"), 1)

            def save_T(g):
                u = units_all[g]
                act.wait_ge(S("aT_ready"), g + 1)
                if g >= 2:
                    act.wait_ge(S("o_ready"), g - 1)
                kts = key_tiles(u)
                nq = u["nq"]
                full = [k for k, nk in kts if nk == P]
                ops = []
                if full:
                    w = nq * len(full)
                    ops.append((aT[:, g % 2, 0:w], bank[4 + g % 2][:, 0:w]))
                if kts[-1][1] < P:
                    k, nk = kts[-1]
                    ops.append((aT[0:nk, g % 2, nq * k:nq * k + nq], bank[4 + g % 2][0:nk, nq * k:nq * k + nq]))
                for o, i in ops[:-1]:
                    link(copy(o, i, ACT.Copy))
                copy(ops[-1][0], ops[-1][1], ACT.Copy).then_inc(S("aT_saved"), 1)

            def save_o(g):
                u = units_all[g]
                act.wait_ge(S("o_ready"), g + 1)
                b, M, nq = u["base"], u["M"], u["nq"]
                src = bank[6 + g % 2][b:b + M, 0:nq * len(u["v"])]
                if len(u["v"]) == 2:
                    src = src.rearrange("p (c n) -> p c n", c=2)
                if u["kind"] == "a":
                    link(copy(u["out"], src, ACT.Copy))
                    copy(sq[:, u["h"], u["q0"]:u["q0"] + nq], src, ACT.Square).then_inc(S("o_saved"), 1)
                else:
                    copy(u["out"], src, ACT.Copy).then_inc(S("o_saved"), 1)

            squares(0)
            ffn(0)
            squares(1)
            act.wait_ge(S("bias_rows_written"), 16)
            u = 0
            for t in range(8):
                save(u, lambda: copy(uT[:, t, :], bank[u % 8][:, 0:T1], ACT.Copy),
                     lambda: copy(sq[:, t, :], bank[u % 8][:, 0:T1], ACT.Square))
                u += 1
            for c in range(2):
                for t, (q0, nq) in enumerate(BLOCKS1):
                    save(u, lambda: copy(va[0:nq, t, 256 * c:256 * c + 256], bank[u % 8][0:nq, 0:256], ACT.Copy))
                    u += 1
            for t in range(4):
                save(u, lambda: copy(uT[:, 8 + t, :], bank[u % 8][:, 0:T1], ACT.Copy))
                u += 1
            for t in range(2):
                save(u, lambda: copy(uT[:, 12 + t, :], bank[u % 8][:, 0:T1], ACT.Copy),
                     lambda: copy(sq[:, 8 + t, :], bank[u % 8][:, 0:T1], ACT.Square))
                u += 1
            for t in range(4):
                save(u, lambda: copy(uT[:, 14 + t, :], bank[u % 8][:, 0:T1], ACT.Copy))
                u += 1
            save(u, lambda: copy(ikT[:, :], bank[u % 8][:, 0:T1], ACT.Copy))
            u += 1
            iwb = bank[u % 8][:, 0:24].rearrange("p (t n) -> p t n", t=3)
            save(u, lambda: nc.scalar.activation(iw[:, 0:2, :], iwb[:, 0:2, :], ACT.Copy, scale=IH ** -0.5),
                 lambda: nc.scalar.activation(iw[0:16, 2, :], iwb[0:16, 2, :], ACT.Copy, scale=IH ** -0.5))
            for t in range(8):
                take_root(bank[t][:, 0:T1], ADK, "norm1_psum", t + 1)
            take_root(bank[0][:, 0:T1], BDC, "normc_psum", 1)
            for t in range(8):
                act.wait_ge(S("qlat_ready"), t + 1)
                link(copy(qlT[:, t, :], bank[t][:, 0:T1], ACT.Copy))
                copy(sq[:, t, :], bank[t][:, 0:T1], ACT.Square).then_inc(S("qlat_saved"), 1)
            for h in range(BH):
                take_root(bank[h][:, 0:T1], BDC, "normq_psum", h + 1)
            for t, (q0, nq) in enumerate(BLOCKS1):
                act.wait_ge(S("ctok_ready"), t + 1)
                copy(ctok[0:nq, t, :], bank[4 + t][0:nq, 0:BDC], ACT.Copy).then_inc(S("ctok_saved"), 1)
            for i in range(3):
                q0, nq, L = qcols(i)
                for h in range(IH):
                    n = IH * i + h
                    act.wait_ge(S("dots_ready"), n + 1)
                    if n >= 4:
                        act.wait_ge(S("score_added"), n - 3)
                    nc.scalar.activation(rel[0:nq, n % 4, 0:L], bank[n % 4][0:nq, 0:L], ACT.Relu, scale=0.125
                                         ).then_inc(S("relu_ready"), 1)
            steps(SEG_A, exps, save_T, save_o)
            for h in range(AH):
                take_root(bank[h][:, 0:T1], ADV, "subln_psum", h + 1)
            steps(SEG_B, exps, save_T, save_o)
            for h in range(BH):
                act.wait_ge(S("ob_ready"), h + 1)
                copy(mixT[:, 4 + h, :], bank[h][:, 0:T1], ACT.Copy).then_inc(S("ob_saved"), 1)
            squares(2)
            ffn(1)

            for l in range(LAYERS):
                squares(3 + 2 * l)
                u = U1 + U2 * l
                v = lambda b: bank[b % 8][:, 0:T2]
                for t in range(2):
                    save(u, lambda: copy(cq[:, t, :], v(u), ACT.Copy), lambda: copy(sq[:, t, 0:T2], v(u), ACT.Square))
                    u += 1
                save(u, lambda: copy(ckv[:, 0, :], v(u), ACT.Copy), lambda: copy(sq[:, 2, 0:T2], v(u), ACT.Square))
                u += 1
                u += 2
                for dst in (qbT, kbT):
                    for t in range(2):
                        save(u, lambda: copy(dst[:, t, :], v(u), ACT.Copy))
                        u += 1
                save(u, lambda: copy(vb.rearrange("p t n -> p (t n)"), bank[u % 8][:, :], ACT.Copy))
                u += 1
                act.wait_ge(S("pad_ready"), l + 1)
                for t in range(2):
                    save(u, lambda: copy(upad[:, t, 16:272], v(u), ACT.Copy))
                    u += 1
                take_root(bank[0][:, 0:T2], 256, "norm_lat_psum", 2 * l + 1)
                take_root(bank[1][:, 0:T2], 128, "norm_lat_psum", 2 * l + 2)
                for n in range(4):
                    act.wait_ge(S("q_up_ready"), 4 * l + n + 1)
                    nc.scalar.activation(qcat[0:64, 2 * n:2 * n + 2, :],
                                         bank[2 * (n % 2)][0:64, :].rearrange("p (h n) -> p h n", h=2),
                                         ACT.Copy, scale=96.0 ** -0.5).then_inc(S("q_nope_saved"), 1)
                for n in range(4):
                    act.wait_ge(S("k_up_ready"), 4 * l + n + 1)
                    copy(kcat[0:64, 2 * n:2 * n + 2, :], bank[4 + n % 2][0:64, :].rearrange("p (h n) -> p h n", h=2),
                         ACT.Copy).then_inc(S("k_nope_saved"), 1)
                for t in range(2):
                    act.wait_ge(S("v_up_ready"), 2 * l + t + 1)
                    copy(vm[:, t, :], bank[6 + t][:, :], ACT.Copy).then_inc(S("vm_saved"), 1)
                steps(SEG_M[l], exps, save_T, save_o)
                for h in range(SH):
                    act.wait_ge(S("nabs_ready"), SH * l + h + 1)
                    link(copy(ln[:, h, :], ln[:, h, :], ACT.Exp))
                for h in range(SH):
                    nc.scalar.activation(ln[:, h, :], ln[:, h, :], ACT.Ln, bias=1.0).then_inc(S("ln_ready"), 1)
                for h in range(SH):
                    act.wait_ge(S("stick_log_ready"), SH * l + h + 1)
                    copy(ln[:, h, :], zm[:, h, :], ACT.Exp).then_inc(S("stick_ready"), 1)
                for h in range(SH):
                    b = 64 * (h % 2)
                    act.wait_ge(S("stick_o_ready"), SH * l + h + 1)
                    copy(mixT[b:b + 64, 4 + h // 2, 0:T2], bank[4 + h][b:b + 64, 0:T2], ACT.Copy
                         ).then_inc(S("stick_saved"), 1)
                for t in range(2):
                    act.wait_ge(S("pool_y_ready"), l + 1)
                    nc.scalar.activation(mixT[:, 6 + t, 0:T2], bank[0][:, T2 * t:T2 * t + T2], ACT.Copy,
                                         scale=gain(G_PS + 2 * l + t)).then_inc(S("pool_saved"), 1)
                squares(4 + 2 * l)
                act.wait_ge(S("router_shifted"), l + 1)
                copy(small[:, 16:24], small[:, 8:16], ACT.Exp).then_inc(S("router_exp1"), 1)
                act.wait_ge(S("router_gap"), l + 1)
                copy(small[:, 44:46], small[:, 40:42], ACT.Exp).then_inc(S("router_exp2"), 1)
                if l + 1 < LAYERS:
                    act.wait_ge(S("router_ready"), l + 1)
                    act.dma_start(sm[:], small2[l + 1]).then_inc(S("small2_loaded"), 16)
                for b in range(4):
                    act.wait_ge(S("x_turned"), 4 * l + b + 1)
                    copy(x_hi[:, b // 2, 512 * (b % 2):512 * (b % 2) + 512], bank[2 + b][:, :], ACT.Copy
                         ).then_inc(S("x_hi_ready"), 1)

                def silu(e, p, first):
                    act.wait_ge(S("moe_gate_ready"), e + (NE * l + 1))
                    if not first:
                        act.wait_ge(S(f"moe_hid_ready{l}"), e - 1)
                    copy(silm[:, p, :], bank[4 + 2 * p][:, :], ACT.Silu).then_inc(S(f"moe_silu_ready{l}"), 1)

                def high(s):
                    act.wait_ge(S("moe_down_used"), s * 2 + (NE * l + 2))
                    act.wait_ge(S(f"slots_saved{l}"), s + 1)
                    for half in range(2):
                        ins = nc.scalar.activation(o_hi[:, 512 * half:512 * half + 512], bank[4 + half][:, :], ACT.Copy,
                                                   scale=wslot[:, 0:1])
                    ins.then_inc(S(f"o_hi_ready{l}"), 1)

                def silu_pair(s):
                    act.wait_ge(S("moe_up_ready"), s * 2 + (NE * l + 2))
                    copy(sl[:, :], bank[6][:, 0:256], ACT.Silu).then_inc(S(f"silu_pair_ready{l}"), 1)

                def save_slots(s):
                    act.wait_ge(S(f"slots_turned{l}"), s + 1)
                    copy(slotsT[:, :], bank[7][:, 0:T2], ACT.Copy)
                    copy(wslot[:, :], bank[7][:, T2:T2 + 1], ACT.Copy).then_inc(S(f"slots_saved{l}"), 1)

                def save_gathered(s):
                    act.wait_ge(S(f"gathered{l}"), s * 2 + 1)
                    copy(xg[:, 0:4, :], bank[4].rearrange("p (k n) -> p k n", k=4), ACT.Copy
                         ).then_inc(S(f"xg_low_ready{l}"), 1)

                act.wait_ge(S("load_known"), l + 1)
                with act.If(act.value_load(load_i[0:1, 0:1]) > CAP):
                    act.wait_ge(S(f"combT_psum{l}"), 1)
                    copy(combT[0:NE, :], bank[1][0:NE, 0:T2], ACT.Copy).then_inc(S(f"combT_ready{l}"), 1)
                    silu(0, 0, True)
                    silu(1, 1, True)
                    with act.Fori(1, PAIRS) as i:
                        for p in range(2):
                            silu(i * 2 + p, p, False)
                with act.Else():
                    save_gathered(0)
                    silu_pair(0)
                    save_slots(0)
                    save_gathered(1)

                    def step(s):
                        high(s)
                        silu_pair(s + 1)
                        save_slots(s + 1)
                        save_gathered(s + 2)

                    with act.Fori(0, PAIRS // 2 - 1) as i:
                        for p in range(2):
                            step(i * 2 + p)
                    high(PAIRS - 2)
                    silu_pair(PAIRS - 1)
                    save_slots(PAIRS - 1)
                    high(PAIRS - 1)
            squares(7)
            for t in range(2):
                for j in range(4):
                    n = 4 * t + j
                    act.wait_ge(S("outT_ready"), n + 1)
                    copy(otok[:, t, 256 * j:256 * j + 256], bank[1 + n % 4][:, 0:256], ACT.Copy).then_inc(S("out_ready"), 1)

        @block.tensor
        def _(pe):
            mm = nc.tensor.matmul

            def token_sum(dst, lhs, tiles, T):
                for j, t in enumerate(tiles):
                    ins = mm(dst, lhs, sq[:, t, 0:T], start=(j == 0), stop=(j == len(tiles) - 1))
                return ins

            def norm(n):
                off, T = span[n]
                pe.wait_ge(S("squares_ready"), 2 * n + 1)
                token_sum(bank[0][:, 0:T], ones, range(4), T) if False else None
                for t in range(KT):
                    if t == 4:
                        pe.wait_ge(S("squares_ready"), 2 * n + 2)
                    ins = mm(bank[0][:, 0:T], ones, sq[:, t, 0:T], start=(t == 0), stop=(t == KT - 1))
                ins.then_inc(S("sumsq_ready"), 1)

            def ffn(f, at, n):
                for i in range(FT):
                    g, c, ft = FT * f + i, i // 2, i % 2
                    if i >= 4:
                        pe.wait_ge(S("hid_ready"), g - 3)
                    for j, sig in enumerate(("gate_ready", "up_ready")):
                        loaded(pe, at + 2 * c + j)
                        w = up_view(at + 2 * c + j)
                        dst = bank[2 * (i % 4) + j][:, 0:T1]
                        for k in range(KT):
                            if i == 0 and j == 0:
                                pe.wait_ge(S("xn_ready"), KT * n + k + 1)
                            ins = mm(dst, w[:, k, P * ft:P * ft + P], xn[:, k, :], start=(k == 0), stop=(k == KT - 1))
                        ins.then_inc(S(sig), 1)
                down(at + 2 * FC, FC, hid, T1, [("hid_ready", FT * f + i + 1) for i in range(FT)])

            def down(at, chunks, rhs, T, ready):
                if len(ready) > 1 and chunks == FC:
                    pe.wait_ge(S(ready[-1][0]), ready[-1][1])
                else:
                    for name, v in ready:
                        pe.wait_ge(S(name), v)
                for c in range(chunks):
                    loaded(pe, at + c)
                    w = down_view(at + c)
                    for f in range(2):
                        for d in range(KT):
                            first, last = c == 0 and f == 0, c == chunks - 1 and f == 1
                            ins = mm(bank[d][:, 0:T], w[:, f, P * d:P * d + P], rhs[:, 2 * c + f, 0:T],
                                     start=first, stop=last)
                            if last:
                                ins.then_inc(S("y_ready"), 1)
                    if c < chunks - 1:
                        ins.then_inc(S("down_used"), 1)

            class Units:
                n = 0

            def bank_free(u, base):
                held = u - base - 8
                if held >= 0 and base < U1:
                    pe.wait_ge(S("proj_saved"), held + 1)
                elif 0 <= held < 3:
                    pe.wait_ge(S("proj_saved"), U1 + SAVED2 * ((base - U1) // U2) + held + 1)
                elif held == 3:
                    pe.wait_ge(S("rotary_read"), 2 * ((base - U1) // U2) + 1)

            def feature_unit(u, base, at, c0, T, n=None):
                bank_free(u, base)
                w = up_view(at)
                loaded(pe, at)
                for k in range(KT):
                    if n is not None:
                        pe.wait_ge(S("xn_ready"), KT * n + k + 1)
                    ins = mm(bank[u % 8][:, 0:T], w[:, k, c0:c0 + P], xn[:, k, 0:T], start=(k == 0), stop=(k == KT - 1))
                ins.then_inc(S("proj_ready"), 1)

            def scores(g):
                u = units_all[g]
                if g >= 2:
                    pe.wait_ge(S("scores_taken"), g - 1)
                for m in range(u["maps"]):
                    parts = u["score"][m]
                    for j, (lhs, rhs) in enumerate(parts):
                        ins = mm(bank[2 * (g % 2) + m][0:u["nq"], 0:u["L"]], lhs, rhs,
                                 start=(j == 0), stop=(j == len(parts) - 1))
                ins.then_inc(S("scores_ready"), 1)

            def turn(g):
                u = units_all[g]
                pe.wait_ge(S("probs_ready"), g + 1)
                if g >= 2:
                    pe.wait_ge(S("aT_saved"), g - 1)
                nq = u["nq"]
                for k, nk in key_tiles(u):
                    ins = nc.tensor.transpose(bank[4 + g % 2][0:nk, nq * k:nq * k + nq],
                                              a_sb[0:nq, g % 2, P * k:P * k + nk], ident[0:nq, 0:nq])
                ins.then_inc(S("aT_ready"), 1)

            def pv(g):
                u = units_all[g]
                pe.wait_ge(S("aT_saved"), g + 1)
                if g >= 2:
                    pe.wait_ge(S("o_saved"), g - 1)
                nq, b, M = u["nq"], u["base"], u["M"]
                kts = key_tiles(u)
                for c, v in enumerate(u["v"]):
                    for k, nk in kts:
                        ins = mm(bank[6 + g % 2][b:b + M, nq * c:nq * c + nq], v(k, nk), aT[0:nk, g % 2, nq * k:nq * k + nq],
                                 start=(k == 0), stop=(k == len(kts) - 1))
                ins.then_inc(S("o_ready"), 1)

            pe.wait_ge(S("consts_loaded"), 16)
            pe.wait_ge(S("x_loaded"), 32)
            for d in range(KT):
                for t, (q0, nq) in enumerate(BLOCKS1):
                    ins = nc.tensor.transpose(bank[d][:, q0:q0 + nq], xtok[0:nq, t, P * d:P * d + P], ident[0:nq, 0:nq])
                ins.then_inc(S("xT_ready"), 1)
            pe.wait_ge(S("input_saved"), 8)
            norm(0)
            pe.wait_ge(S("rb_loaded"), 16)
            mm(bank[7][0:8, :], rb[:, :], cst[0:32, C_OH:C_OH + ROW], start=True, stop=True).then_inc(S("bias_psum"), 1)
            pe.wait_ge(S("bias_rows_ready"), 1)
            ffn(0, A_FFN1, 0)
            norm(1)

            u = 0
            for t in range(8):
                feature_unit(u, 0, A_IN1 + t // 2, P * (t % 2), T1, n=1 if t == 0 else None)
                u += 1
            for c in range(2):
                at_ = A_IN1 + 4 + c
                for t, (q0, nq) in enumerate(BLOCKS1):
                    bank_free(u, 0)
                    loaded(pe, at_)
                    for k in range(KT):
                        ins = mm(bank[u % 8][0:nq, 0:256], xn[:, k, q0:q0 + nq], up_view(at_)[:, k, :],
                                 start=(k == 0), stop=(k == KT - 1))
                    ins.then_inc(S("proj_ready"), 1)
                    u += 1
            for t in range(10):
                feature_unit(u, 0, A_IN1 + 6 + t // 2, P * (t % 2), T1)
                u += 1
            w = up_view(A_IN1 + 11)
            loaded(pe, A_IN1 + 11)
            bank_free(u, 0)
            for half in range(2):
                for k in range(KT):
                    ins = mm(bank[u % 8][64 * half:64 * half + 64, 0:T1], w[:, k, 0:64], xn[:, k, :],
                             start=(k == 0), stop=(k == KT - 1))
            ins.then_inc(S("proj_ready"), 1)
            u += 1
            bank_free(u, 0)
            for t, (q0, nq) in enumerate(BLOCKS1):
                for k in range(KT):
                    ins = mm(bank[u % 8][0:nq, 8 * t:8 * t + 8], xn[:, k, q0:q0 + nq], w[:, k, 64:72],
                             start=(k == 0), stop=(k == KT - 1))
            ins.then_inc(S("proj_ready"), 1)
            pe.wait_ge(S("proj_saved"), U1)
            for t in range(8):
                mm(bank[t][:, 0:T1], bd64, sq[:, t, :], start=True, stop=True).then_inc(S("norm1_psum"), 1)
            pe.wait_ge(S("norm1_done"), 1)
            token_sum(bank[0][:, 0:T1], ones, (8, 9), T1).then_inc(S("normc_psum"), 1)
            pe.wait_ge(S("wuk_loaded"), 16)
            pe.wait_ge(S("normc_done"), 2)
            pe.wait_ge(S("norm1_done"), 8)
            for t in range(8):
                mm(bank[t][:, 0:T1], w_uk[:, t // 2, P * (t % 2):P * (t % 2) + P], uT[:, 8 + t // 2, :],
                   start=True, stop=True).then_inc(S("qlat_ready"), 1)
            pe.wait_ge(S("qlat_saved"), 8)
            for h in range(BH):
                token_sum(bank[h][:, 0:T1], ones, (2 * h, 2 * h + 1), T1).then_inc(S("normq_psum"), 1)
            for t, (q0, nq) in enumerate(BLOCKS1):
                for c in range(2):
                    ins = nc.tensor.transpose(bank[4 + t][0:nq, P * c:P * c + P], uT[:, 12 + c, q0:q0 + nq], ident)
                ins.then_inc(S("ctok_ready"), 1)
            pe.wait_ge(S("normq_done"), 8)
            for i in range(3):
                q0, nq, L = qcols(i)
                for h in range(IH):
                    n, b = IH * i + h, 64 * (h % 2)
                    if n >= 4:
                        pe.wait_ge(S("relu_ready"), n - 3)
                    mm(bank[n % 4][0:nq, 0:L], uT[b:b + 64, 14 + h // 2, q0:q0 + nq], ikT[b:b + 64, 0:L],
                       start=True, stop=True).then_inc(S("dots_ready"), 1)
            pe.wait_ge(S("relu_ready"), 24)
            pe.wait_ge(S("ctok_saved"), 3)
            steps(SEG_A, scores, turn, pv)
            pe.wait_ge(S("o_saved"), SEG_A[1])
            for h in range(AH):
                mm(bank[h][:, 0:T1], ones, sq[:, h, :], start=True, stop=True).then_inc(S("subln_psum"), 1)
            pe.wait_ge(S("subln_done"), AH)
            steps(SEG_B, scores, turn, pv)
            pe.wait_ge(S("o_saved"), SEG_B[1])
            pe.wait_ge(S("wuv_loaded"), 16)
            for h in range(BH):
                for c in range(2):
                    ins = mm(bank[h][:, 0:T1], w_uv[:, h, c, :], olT[:, 2 * h + c, :], start=(c == 0), stop=(c == 1))
                ins.then_inc(S("ob_ready"), 1)
            down(A_OUT1, 4, mixT, T1, [("ob_saved", BH), ("subln_done", AH)])
            norm(2)
            ffn(1, A_FFN2, 2)

            for l in range(LAYERS):
                n1 = 3 + 2 * l
                norm(n1)
                base = U1 + U2 * l
                u = base
                a = A_IN2[l]
                pe.wait_ge(S("xn_ready"), KT * n1 + 1)
                feature_unit(u, base, a, 0, T2, n=n1)
                feature_unit(u + 1, base, a, P, T2)
                feature_unit(u + 2, base, a + 1, 0, T2)
                pe.wait_ge(S("swapped_ready"), l + 1)
                for j in range(2):
                    bank_free(u + 3 + j, base)
                    for k in range(KT):
                        lhs = wkrs[:, k, :] if j else up_view(a + 1)[:, k, P:P + 32]
                        ins = mm(bank[(u + 3 + j) % 8][64:96, 0:T2], lhs, xn[:, k, 0:T2], start=(k == 0), stop=(k == KT - 1))
                    ins.then_inc(S("proj_ready"), 1)
                u += 5
                for t in range(4):
                    feature_unit(u, base, a + 2 + t // 2, P * (t % 2), T2)
                    u += 1
                bank_free(u, base)
                loaded(pe, a + 4)
                for t in range(2):
                    for k in range(KT):
                        ins = mm(bank[u % 8][:, T2 * t:T2 * t + T2], xn[:, k, P * t:P * t + P], up_view(a + 4)[:, k, :],
                                 start=(k == 0), stop=(k == KT - 1))
                ins.then_inc(S("proj_ready"), 1)
                u += 1
                for t in range(2):
                    feature_unit(u, base, a + 5, P * t, T2)
                    u += 1
                pe.wait_ge(S("proj_saved"), U1 + SAVED2 * (l + 1))
                pe.wait_ge(S("rotary_read"), 2 * (l + 1))
                token_sum(bank[0][:, 0:T2], ones, (0, 1), T2).then_inc(S("norm_lat_psum"), 1)
                mm(bank[1][:, 0:T2], ones, sq[:, 2, 0:T2], start=True, stop=True).then_inc(S("norm_lat_psum"), 1)
                pe.wait_ge(S("lat_ready"), 3 * (l + 1))
                for n in range(4):
                    if n >= 2:
                        pe.wait_ge(S("q_nope_saved"), 4 * l + n - 1)
                        pe.wait_ge(S("q_rope_saved"), 4 * l + n - 1)
                    b0, b1 = bank[2 * (n % 2)], bank[2 * (n % 2) + 1]
                    for j in range(2):
                        h = 2 * n + j
                        for k in range(2):
                            mm(b0[0:96, T2 * j:T2 * j + T2], w_uq[:, k, 96 * h:96 * h + 96], cq[:, k, :],
                               start=(k == 0), stop=(k == 1))
                        for k in range(2):
                            ins = mm(b1[64:96, T2 * j:T2 * j + T2], wuqs[:, k, h, :], cq[:, k, :],
                                     start=(k == 0), stop=(k == 1))
                    ins.then_inc(S("q_up_ready"), 1)
                for n in range(4):
                    if n >= 2:
                        pe.wait_ge(S("k_nope_saved"), 4 * l + n - 1)
                    for j in range(2):
                        ins = mm(bank[4 + n % 2][0:64, T2 * j:T2 * j + T2], w_ukv[:, 2 * n + j, 0:64], ckv[:, 0, :],
                                 start=True, stop=True)
                    ins.then_inc(S("k_up_ready"), 1)
                for t in range(2):
                    mm(bank[6 + t][:, :], ckv[:, 0, P * t:P * t + P], w_ukv[:, :, 64:128],
                       start=True, stop=True).then_inc(S("v_up_ready"), 1)
                pe.wait_ge(S("q_nope_saved"), 4 * (l + 1))
                pe.wait_ge(S("q_rope_saved"), 4 * (l + 1))
                pe.wait_ge(S("k_nope_saved"), 4 * (l + 1))
                pe.wait_ge(S("k_rope_saved"), l + 1)
                pe.wait_ge(S("vm_saved"), 2 * (l + 1))
                steps(SEG_M[l], scores, turn, pv)
                pe.wait_ge(S("o_saved"), SEG_M[l][1])
                for h in range(SH):
                    b, t = 64 * (h % 2), h // 2
                    mm(bank[h][:, 0:T2], kbT[b:b + 64, t, 0:P], qbT[b:b + 64, t, :], start=True, stop=True)
                    mm(bank[h][:, T2:384], kbT[b:b + 64, t, P:T2], qbT[b:b + 64, t, P:T2],
                       start=True, stop=True).then_inc(S("z_ready"), 1)
                for h in range(SH):
                    pe.wait_ge(S("softplus_ready"), SH * l + h + 1)
                    mm(bank[h][:, T2:384], upper, ln[:, h, T2:384], start=True, stop=True)
                    mm(bank[h][:, 0:T2], upper, ln[:, h, 0:T2], start=True, stop=True)
                    mm(bank[h][:, P:T2], ones, ln[:, h, T2:384], start=False, stop=True,
                       skip_group_check=True).then_inc(S("later_ready"), 1)
                for h in range(SH):
                    b = 64 * (h % 2)
                    pe.wait_ge(S("stick_ready"), SH * l + h + 1)
                    mm(bank[4 + h][b:b + 64, 0:T2], vb[:, 0, 64 * h:64 * h + 64], ln[:, h, 0:T2], start=True, stop=True)
                    mm(bank[4 + h][b:b + 64, P:T2], vb[:, 1, 64 * h:64 * h + 64], ln[:, h, T2:384], start=False, stop=True,
                       skip_group_check=True).then_inc(S("stick_o_ready"), 1)
                pe.wait_ge(S("pool_d_ready"), l + 1)
                for t in range(2):
                    ins = mm(bank[0][:, T2 * t:T2 * t + T2], w_pool[:, t, :], pd[:, t, :], start=True, stop=True)
                ins.then_inc(S("pool_y_ready"), 1)
                down(A_OUT2[l], 4, mixT, T2, [("stick_saved", SH * (l + 1)), ("pool_saved", 2 * (l + 1))])
                n2 = 4 + 2 * l
                norm(n2)
                pe.wait_ge(S("xn_ready"), KT * (n2 + 1))
                for t in range(2):
                    for k in range(KT):
                        ins = mm(bank[0][:, 36 * t:36 * t + 36], xn[:, k, P * t:P * t + P], w_rt[:, k, :],
                                 start=(k == 0), stop=(k == KT - 1))
                ins.then_inc(S("router_ready"), 1)
                for b in range(4):
                    for k in range(4):
                        f = 4 * (b % 2) + k
                        ins = nc.tensor.transpose(bank[2 + b][:, P * k:P * k + P],
                                                  xn[:, f, P * (b // 2):P * (b // 2) + P], ident)
                    ins.then_inc(S("x_turned"), 1)
                pe.wait_ge(S("sel_ready"), l + 1)
                before = cst[:, C_BE:C_BE + P]
                mm(bank[1][:, 0:NE], before, sel[:, 0, :], start=True, stop=True)
                mm(bank[1][:, NE:2 * NE], before, sel[:, 1, :], start=True, stop=False)
                mm(bank[1][:, NE:2 * NE], ones, sel[:, 0, :], start=False, stop=True)
                mm(bank[1][:, 2 * NE:3 * NE], ones, sel[:, 0, :], start=True, stop=False)
                mm(bank[1][:, 2 * NE:3 * NE], ones, sel[:, 1, :], start=False, stop=True).then_inc(S("places_psum"), 1)
                pe.wait_ge(S("comb_ready"), l + 1)
                pe.wait_ge(S("x_lo_ready"), 4 * (l + 1))
                pe.wait_ge(S("load_known"), l + 1)
                pe.wait_ge(S("zeros_ready"), 1)

                def zero_sum():
                    for b in range(4):
                        mm(bank[b][:, :], zb[:, 0:P], zb[:, :], start=True, stop=True)

                at_ = MOE_AT[l]

                def chunk_loaded(n, lap):
                    pe.wait_ge(slot_sem(n), lap * 16 + 16 * (n // NS + 1))

                def gate_up(e, p, lap, first):
                    for j, sig in enumerate(("moe_gate_ready", "moe_up_ready")):
                        n = at_ + 2 * p + j
                        chunk_loaded(n, lap)
                        if not first and j == 0:
                            pe.wait_ge(S(f"moe_hid_ready{l}"), e - 1)
                        for f in range(2):
                            for k in range(KT):
                                ins = mm(bank[4 + 2 * p + j][:, T2 * f:T2 * f + T2], up_view(n)[:, k, P * f:P * f + P],
                                         xn[:, k, 0:T2], start=(k == 0), stop=(k == KT - 1))
                        ins.then_inc(S(sig), 1)

                def expert_down(e, p, lap):
                    n = at_ + 4 + p
                    chunk_loaded(n, lap)
                    pe.wait_ge(S(f"moe_hid_ready{l}"), e + 1)
                    for f in range(2):
                        for d in range(KT):
                            ins = mm(bank[d // 2][:, T2 * (d % 2):T2 * (d % 2) + T2], down_view(n)[:, f, P * d:P * d + P],
                                     hm[:, p, T2 * f:T2 * f + T2], start=False, stop=True, skip_group_check=True)
                    ins.then_inc(S("moe_down_used"), 1)

                def gather(s, p, first=False):
                    pe.wait_ge(S(f"slots_ready{l}"), s + 1)
                    if not first:
                        pe.wait_ge(S(f"o_lo_ready{l}"), s - 1)
                    for half in range(2):
                        for kk in range(4):
                            k = 4 * half + kk
                            for j, x in enumerate((x_hi, x_lo)):
                                for t in range(2):
                                    ins = mm(bank[4 + half][:, P * kk:P * kk + P], x[:, t, P * k:P * k + P],
                                             slots[:, p, t, :], start=(j == 0 and t == 0), stop=(j == 1 and t == 1))
                        ins.then_inc(S(f"gathered{l}"), 1)

                def gate_up_pair(s, first=False):
                    pe.wait_ge(S(f"xg_low_ready{l}"), s + 1)
                    pe.wait_ge(S(f"xg_high_ready{l}"), s + 1)
                    if not first:
                        pe.wait_ge(S(f"hs_ready{l}"), s)
                    for e in range(2):
                        for j, sig in enumerate(("moe_gate_ready", "moe_up_ready")):
                            n = at_ + 2 * e + j
                            chunk_loaded(n, s)
                            for f in range(2):
                                c = 256 * j + CAP * (2 * e + f)
                                for k in range(KT):
                                    ins = mm(bank[6][:, c:c + CAP], up_view(n)[:, k, P * f:P * f + P],
                                             xg[:, k, CAP * e:CAP * e + CAP], start=(k == 0), stop=(k == KT - 1))
                            ins.then_inc(S(sig), 1)

                def turn_slots(s, p, first=False):
                    pe.wait_ge(S(f"slotw_ready{l}"), s + 1)
                    if not first:
                        pe.wait_ge(S(f"slots_saved{l}"), s)
                    for t in range(2):
                        nc.tensor.transpose(bank[7][:, P * t:P * t + P], slots[:, p, t, :].bitcast(F32), ident)
                    for t in range(2):
                        ins = mm(bank[7][:, T2:T2 + 2], slotw[:, t, :], ones[:, 0:2], start=(t == 0), stop=(t == 1))
                    ins.then_inc(S(f"slots_turned{l}"), 1)

                def down_pair(s, last=False):
                    pe.wait_ge(S(f"hs_ready{l}"), s + 1)
                    pe.wait_ge(S(f"xg_low_ready{l}"), s + (1 if last else 2))
                    pe.wait_ge(S(f"xg_high_ready{l}"), s + (1 if last else 2))
                    for e in range(2):
                        n = at_ + 4 + e
                        chunk_loaded(n, s)
                        for half in range(2):
                            for f in range(2):
                                c = CAP * (2 * e + f)
                                ins = mm(bank[4 + half][64 * e:64 * e + 64, :], hs[:, c:c + CAP],
                                         down_view(n)[:, f, 512 * half:512 * half + 512], start=(f == 0), stop=(f == 1))
                        ins.then_inc(S("moe_down_used"), 1)

                def scatter(s):
                    pe.wait_ge(S(f"o_hi_ready{l}"), s + 1)
                    pe.wait_ge(S(f"o_lo_ready{l}"), s + 1)
                    pe.wait_ge(S(f"slots_saved{l}"), s + 1)
                    for d in range(KT):
                        for o in (o_hi, o_lo):
                            ins = mm(bank[d // 2][:, T2 * (d % 2):T2 * (d % 2) + T2], o[:, P * d:P * d + P],
                                     slotsT[:, :], start=False, stop=True, skip_group_check=True)
                    return ins

                with pe.If(pe.value_load(load_i[0:1, 0:1]) > CAP):
                    for t in range(2):
                        ins = nc.tensor.transpose(bank[1][0:NE, P * t:P * t + P], comb[:, t, :], ident)
                    ins.then_inc(S(f"combT_psum{l}"), 1)
                    pe.wait_ge(S(f"combT_ready{l}"), 1)
                    zero_sum()
                    gate_up(0, 0, 0, True)
                    gate_up(1, 1, 0, True)
                    expert_down(0, 0, 0)
                    with pe.Fori(1, PAIRS) as i:
                        gate_up(i * 2, 0, i, False)
                        expert_down(i * 2 - 1, 1, i - 1)
                        gate_up(i * 2 + 1, 1, i, False)
                        expert_down(i * 2, 0, i)
                    expert_down(NE - 1, 1, PAIRS - 1)
                with pe.Else():
                    zero_sum()
                    gather(0, 0, True)
                    gate_up_pair(0, True)
                    turn_slots(0, 0, True)
                    gather(1, 1, True)
                    with pe.Fori(0, PAIRS // 2 - 1) as i:
                        for p in range(2):
                            s = i * 2 + p
                            down_pair(s)
                            gate_up_pair(s + 1)
                            scatter(s)
                            turn_slots(s + 1, 1 - p)
                            gather(s + 2, p)
                    down_pair(PAIRS - 2)
                    gate_up_pair(PAIRS - 1)
                    scatter(PAIRS - 2)
                    turn_slots(PAIRS - 1, 1)
                    down_pair(PAIRS - 1, last=True)
                    scatter(PAIRS - 1)
                mm(bank[4][:, :], zb[:, 0:P], zb[:, :], start=True, stop=True).then_inc(S("experts_done"), 1)
            norm(7)
            pe.wait_ge(S("xn_ready"), 64)
            for t in range(2):
                for j in range(4):
                    n = 4 * t + j
                    if n >= 4:
                        pe.wait_ge(S("out_ready"), n - 3)
                    for c in range(2):
                        ins = nc.tensor.transpose(bank[1 + n % 4][:, P * c:P * c + P], xn[:, 2 * j + c, P * t:P * t + P], ident)
                    ins.then_inc(S("outT_ready"), 1)

        @block.vector
        def _(dve):
            n_chain = 0
            V = nc.vector

            def link(ins):
                nonlocal n_chain
                n_chain += 1
                ins.then_inc(S("dve_chain"), 1)
                dve.wait_ge(S("dve_chain"), n_chain)

            n_root = 0

            def inv_rms(dst, T=T1):
                nonlocal n_root
                dve.wait_ge(S("root_ready"), n_root + 1)
                V.reciprocal(dst, root[:, n_root % 2, 0:T]).then_inc(S("root_used"), 1)
                n_root += 1
                dve.wait_ge(S("root_used"), n_root)

            def norm(n):
                off, T = span[n]
                inv_rms(rstd[:, 0, 0:T], T)
                for k in range(KT):
                    V.scalar_tensor_tensor(xn[:, k, 0:T], hT[:, k, off:off + T], gain(G_NORM + KT * n + k), rstd[:, 0, 0:T],
                                           ALU.mult, ALU.mult).then_inc(S("xn_ready"), 1)

            def ffn(f):
                for i in range(FT):
                    g = FT * f + i
                    dve.wait_ge(S("silu_ready"), g + 1)
                    dve.wait_ge(S("up_ready"), g + 1)
                    V.tensor_tensor(hid[:, i, :], sil[:, i % 2, :], bank[2 * (i % 4) + 1][:, 0:T1], ALU.mult
                                    ).then_inc(S("hid_ready"), 1)

            def residual(k, r, factor):
                off, T = span[r]
                for d in range(KT):
                    dve.wait_ge(S("y_ready"), 8 * k + d + 1)
                    h = hT[:, d, 0 if T == T1 else off:T1]
                    V.scalar_tensor_tensor(h, bank[d][:, 0:T], factor, h, ALU.mult, ALU.add
                                           ).then_inc(S("residual_ready"), 1)

            def maxes(g):
                u = units_all[g]
                dve.wait_ge(S("scores_ready"), g + 1)
                nq, L = u["nq"], u["L"]
                bias = u["bias"]
                if u["kind"] == "b":
                    dve.wait_ge(S("bias_ready"), g - SEG_B[0] + 1)
                    bias = gb[0:nq, g % 2, 0:L]
                for m in range(u["maps"]):
                    ins = V.tensor_tensor_reduce(s_sb[0:nq, g % 2, m, 0:L], bank[2 * (g % 2) + m][0:nq, 0:L], bias,
                                                 1.0, -3.4e38, ALU.add, ALU.max, mx[0:nq, g % 2, m:m + 1])
                    if m < u["maps"] - 1:
                        link(ins)
                ins.then_inc(S("scores_taken"), 1)
                dve.wait_ge(S("scores_taken"), g + 1)
                V.tensor_scalar(nmx[0:nq, g % 2, 0:u["maps"]], mx[0:nq, g % 2, 0:u["maps"]], -1.0, None, ALU.mult
                                ).then_inc(S("max_ready"), 1)

            def weights(g):
                u = units_all[g]
                dve.wait_ge(S("exps_ready"), g + 1)
                nq, L = u["nq"], u["L"]
                if g >= 2:
                    dve.wait_ge(S("aT_ready"), g - 1)
                r = rs[0:nq, g % 2, 0:u["maps"]]
                link(V.reciprocal(r, sums[0:nq, g % 2, 0:u["maps"]]))
                a = a_sb[0:nq, g % 2, 0:L]
                if u["kind"] == "a":
                    link(V.tensor_scalar(rs[0:nq, g % 2, 1:2], rs[0:nq, g % 2, 1:2], lamb[0:nq, 4:5], None, ALU.mult))
                    link(V.tensor_scalar(a, s_sb[0:nq, g % 2, 0, 0:L], rs[0:nq, g % 2, 0:1], None, ALU.mult))
                    ins = V.scalar_tensor_tensor(a, s_sb[0:nq, g % 2, 1, 0:L], rs[0:nq, g % 2, 1:2], a, ALU.mult, ALU.add)
                else:
                    ins = V.tensor_scalar(a, s_sb[0:nq, g % 2, 0, 0:L], rs[0:nq, g % 2, 0:1], None, ALU.mult)
                ins.then_inc(S("probs_ready"), 1)
                dve.wait_ge(S("probs_ready"), g + 1)

            dve.wait_ge(S("gains_loaded"), 16)
            link(V.tensor_scalar(gn[:, 0:64], gn[:, 0:64], math.sqrt(D), None, ALU.mult))
            link(V.tensor_scalar(gn[:, G_AK:G_AK + 1], gn[:, G_AK:G_AK + 1], math.sqrt(ADK), None, ALU.mult))
            link(V.tensor_scalar(gn[:, G_AQ:G_AQ + 1], gn[:, G_AQ:G_AQ + 1], math.sqrt(ADK) * ADK ** -0.5, None, ALU.mult))
            link(V.tensor_scalar(gn[:, G_BKV:G_BKV + 2], gn[:, G_BKV:G_BKV + 2], math.sqrt(BDC), None, ALU.mult))
            link(V.tensor_scalar(gn[:, G_BQ:G_BQ + 2], gn[:, G_BQ:G_BQ + 2], math.sqrt(BDC) * BDC ** -0.5, None, ALU.mult))
            link(V.tensor_scalar(gn[:, G_SUB:G_SUB + 1], gn[:, G_SUB:G_SUB + 1], math.sqrt(ADV) * (1.0 - LAM0), None, ALU.mult))
            link(V.tensor_scalar(gn[:, G_QN:G_QN + 4], gn[:, G_QN:G_QN + 4], math.sqrt(256), None, ALU.mult))
            link(V.tensor_scalar(gn[:, G_KVN:G_KVN + 2], gn[:, G_KVN:G_KVN + 2], math.sqrt(128), None, ALU.mult))
            for j in range(2):
                a, b = G_LAM + 2 * j * ADK, G_LAM + (2 * j + 1) * ADK
                ins = V.tensor_tensor_reduce(lprod[:], gn[:, a:a + ADK], gn[:, b:b + ADK], 1.0, 0.0,
                                             ALU.mult, ALU.add, lamb[:, j:j + 1])
                if j == 0:
                    link(ins)
            ins.then_inc(S("lam_sums_ready"), 1)
            dve.wait_ge(S("lam_exp_ready"), 1)
            link(V.scalar_tensor_tensor(lamb[:, 4:5], lamb[:, 3:4], -LAM0, lamb[:, 2:3], ALU.add, ALU.subtract))
            dve.wait_ge(S("input_saved"), 8)
            norm(0)
            dve.wait_ge(S("bias_psum"), 1)
            dve.wait_ge(S("consts_loaded"), 16)
            V.tensor_tensor(btab[:, :], bank[7][0:8, :], cst[0:8, C_OM:C_OM + ROW], ALU.add).then_inc(S("bias_rows_ready"), 1)
            ffn(0)
            residual(0, 0, 0.5)
            dve_total = 8
            norm(1)
            for t in range(8):
                inv_rms(rstd[:, t % 2, :])
                V.scalar_tensor_tensor(uT[:, t, :], uT[:, t, :], gain(G_AQ if t < 4 else G_AK), rstd[:, t % 2, :],
                                       ALU.mult, ALU.mult).then_inc(S("norm1_done"), 1)
            dve.wait_ge(S("norm1_done"), 8)
            inv_rms(rstd[:, 0, :])
            for t in range(2):
                V.scalar_tensor_tensor(uT[:, 12 + t, :], uT[:, 12 + t, :], gain(G_BKV + t), rstd[:, 0, :],
                                       ALU.mult, ALU.mult).then_inc(S("normc_done"), 1)
            for h in range(BH):
                inv_rms(rstd[:, (h + 1) % 2, :])
                for t in range(2):
                    V.scalar_tensor_tensor(qlT[:, 2 * h + t, :], qlT[:, 2 * h + t, :], gain(G_BQ + t),
                                           rstd[:, (h + 1) % 2, :], ALU.mult, ALU.mult).then_inc(S("normq_done"), 1)
            dve.wait_ge(S("normq_done"), 8)
            for i in range(3):
                q0, nq, L = qcols(i)
                s = score[0:nq, 0:L]
                for h in range(IH):
                    n = IH * i + h
                    dve.wait_ge(S("relu_ready"), n + 1)
                    prev = cst[0:nq, C_CM + P * (2 - i):C_CM + P * (2 - i) + L] if h == 0 else s
                    V.scalar_tensor_tensor(s, rel[0:nq, n % 4, 0:L], iw[0:nq, i, h:h + 1], prev, ALU.mult, ALU.add
                                           ).then_inc(S("score_added"), 1)
                    dve.wait_ge(S("score_added"), n + 1)
                for r in range(TOPK // 8):
                    link(V.max(top8[0:nq, :], s))
                    link(V.match_replace(s, top8[0:nq, :], s, TAKEN))
                V.tensor_scalar(selb[0:nq, i, 0:L], s, 0.5 * TAKEN, NEG, ALU.is_gt, ALU.mult).then_inc(S("selected"), 1)
                dve.wait_ge(S("selected"), i + 1)
            dve.wait_ge(S("G_loaded"), 16 * 8)
            steps(SEG_A, maxes, weights)
            for h in range(AH):
                inv_rms(rstd[:, h % 2, :])
                V.scalar_tensor_tensor(mixT[:, h, :], mixT[:, h, :], gain(G_SUB), rstd[:, h % 2, :],
                                       ALU.mult, ALU.mult).then_inc(S("subln_done"), 1)
            steps(SEG_B, maxes, weights)
            residual(1, 1, 1.0)
            norm(2)
            ffn(1)
            residual(2, 2, 0.5)

            for l in range(LAYERS):
                norm(3 + 2 * l)
                base = U1 + U2 * l
                ck, sk = (cst[64:96, C_COS + j * T2:C_COS + (j + 1) * T2] for j in (2, 3))
                dve.wait_ge(S("proj_ready"), base + 5)
                V.tensor_tensor(rt1[64:96, 0, :], bank[(base + 3) % 8][64:96, 0:T2], ck, ALU.mult).then_inc(S("rotary_read"), 1)
                V.tensor_tensor(rt2[64:96, 0, :], bank[(base + 4) % 8][64:96, 0:T2], sk, ALU.mult).then_inc(S("rotary_read"), 1)
                dve.wait_ge(S("rotary_read"), 2 * (l + 1))
                V.tensor_tensor(kcat[64:96, :, :], spread(rt1[64:96, 0:1, :], 1, MH), spread(rt2[64:96, 0:1, :], 1, MH),
                                ALU.add).then_inc(S("k_rope_saved"), 1)
                dve.wait_ge(S("k_rope_saved"), l + 1)
                inv_rms(rstd[:, 0, 0:T2], T2)
                for t in range(2):
                    V.scalar_tensor_tensor(cq[:, t, :], cq[:, t, :], gain(G_QN + 2 * l + t), rstd[:, 0, 0:T2],
                                           ALU.mult, ALU.mult).then_inc(S("lat_ready"), 1)
                inv_rms(rstd[:, 1, 0:T2], T2)
                V.scalar_tensor_tensor(ckv[:, 0, :], ckv[:, 0, :], gain(G_KVN + l), rstd[:, 1, 0:T2],
                                       ALU.mult, ALU.mult).then_inc(S("lat_ready"), 1)
                cqt, sqt = (spread(cst[64:96, C_COS + j * T2:C_COS + (j + 1) * T2].rearrange("p (a n) -> p a n", a=1), 1, 2)
                            for j in (0, 1))
                for n in range(4):
                    dve.wait_ge(S("q_up_ready"), 4 * l + n + 1)
                    b0 = bank[2 * (n % 2)][64:96, :].rearrange("p (h n) -> p h n", h=2)
                    b1 = bank[2 * (n % 2) + 1][64:96, :].rearrange("p (h n) -> p h n", h=2)
                    link(V.tensor_tensor(rt1[64:96, :, :], b0, cqt, ALU.mult))
                    link(V.tensor_tensor(rt2[64:96, :, :], b1, sqt, ALU.mult))
                    V.tensor_tensor(qcat[64:96, 2 * n:2 * n + 2, :], rt1[64:96, :, :], rt2[64:96, :, :], ALU.add
                                    ).then_inc(S("q_rope_saved"), 1)
                    dve.wait_ge(S("q_rope_saved"), 4 * l + n + 1)
                steps(SEG_M[l], maxes, weights)
                nm = cst[:, C_NM:C_NM + 384]
                for h in range(SH):
                    dve.wait_ge(S("z_ready"), SH * l + h + 1)
                    dve.wait_ge(S("aT_saved"), SEG_M[l][1])
                    dve.wait_ge(S("o_ready"), SEG_M[l][1])
                    link(V.scalar_tensor_tensor(zm[:, h, :], bank[h][:, 0:384], 0.125, nm, ALU.mult, ALU.add))
                    V.scalar_tensor_tensor(ln[:, h, :], zm[:, h, :], -1.0, zm[:, h, :], ALU.mult, ALU.min
                                           ).then_inc(S("nabs_ready"), 1)
                for h in range(SH):
                    dve.wait_ge(S("ln_ready"), SH * l + h + 1)
                    V.scalar_tensor_tensor(ln[:, h, :], zm[:, h, :], 0.0, ln[:, h, :], ALU.max, ALU.add
                                           ).then_inc(S("softplus_ready"), 1)
                for h in range(SH):
                    dve.wait_ge(S("later_ready"), SH * l + h + 1)
                    V.tensor_tensor(zm[:, h, :], zm[:, h, :], bank[h][:, 0:384], ALU.subtract
                                    ).then_inc(S("stick_log_ready"), 1)
                residual(3 + l if l == 0 else 4, 3, 1.0)
                norm(4 + 2 * l)
                dve.wait_ge(S("router_ready"), l + 1)
                bias = spread(gn[:, G_RB + 36 * l:G_RB + 36 * l + 36].rearrange("p (a n) -> p a n", a=1), 1, 2)
                link(V.tensor_tensor(rl[:, :, :], bank[0][:, 0:72].rearrange("p (t n) -> p t n", t=2), bias, ALU.add))
                gl = rl[:, :, 0:4]
                gmax = small[:, 0:2]
                bc = lambda v, n: spread(v.rearrange("p (t a) -> p t a", a=1), 2, n)
                v4 = lambda o: small[:, o:o + 8].rearrange("p (t g) -> p t g", t=2)
                link(V.tensor_reduce(gmax, gl, AX_X, ALU.max))
                V.tensor_tensor(v4(8), gl, bc(gmax, 4), ALU.subtract).then_inc(S("router_shifted"), 1)
                dve.wait_ge(S("router_shifted"), l + 1)

                fo = lambda n: spread(cst[:, C_FO:C_FO + n].rearrange("p (a n) -> p a n", a=1), 1, 2)

                def first_of(out, vals, top, n, tmp, tmp1):
                    link(V.tensor_tensor(out, vals, bc(top, n), ALU.is_equal))
                    link(V.tensor_tensor(tmp, out, fo(n), ALU.mult))
                    link(V.tensor_reduce(tmp1, tmp, AX_X, ALU.max))
                    link(V.tensor_tensor(out, tmp, bc(tmp1, n), ALU.is_equal))

                goh = v4(24)
                first_of(goh, gl, gmax, 4, v4(32), small[:, 2:4])
                el = rl[:, :, 4:36].rearrange("p t (g e) -> p t g e", g=4)
                tt = t48.rearrange("p t (g e) -> p t g e", g=4)
                goh8 = spread(goh.rearrange("p t (g a) -> p t g a", a=1), 3, 8)
                for t in range(2):
                    link(V.tensor_tensor(tt[:, t], el[:, t], goh8[:, t], ALU.mult))
                link(V.tensor_reduce(e8[:, :, :], t48.rearrange("p t (g e) -> p t e g", g=4), AX_X, ALU.add))
                v8 = lambda o: small[:, o:o + 16].rearrange("p (t g) -> p t g", t=2)
                o1, o2, tmp8, rest = v8(48), v8(64), v8(80), v8(96)
                l1, l2 = small[:, 4:6], small[:, 6:8]
                link(V.tensor_reduce(l1, e8[:, :, :], AX_X, ALU.max))
                first_of(o1, e8[:, :, :], l1, 8, tmp8, small[:, 42:44])
                link(V.scalar_tensor_tensor(rest, o1, NEG, e8[:, :, :], ALU.mult, ALU.add))
                link(V.tensor_reduce(l2, rest, AX_X, ALU.max))
                first_of(o2, rest, l2, 8, tmp8, small[:, 42:44])
                V.tensor_tensor(small[:, 40:42], l2, l1, ALU.subtract).then_inc(S("router_gap"), 1)
                dve.wait_ge(S("router_exp1"), l + 1)
                dve.wait_ge(S("router_gap"), l + 1)
                psel, den = small[:, 112:114], small[:, 114:116]
                link(V.tensor_reduce(psel, v4(16), AX_X, ALU.add))
                dve.wait_ge(S("router_exp2"), l + 1)
                e2 = small[:, 44:46]
                link(V.scalar_tensor_tensor(den, e2, 1.0, psel, ALU.add, ALU.mult))
                w1, w2 = small[:, 116:118], small[:, 118:120]
                link(V.reciprocal(w1, den))
                link(V.tensor_tensor(w2, w1, e2, ALU.mult))
                link(V.tensor_tensor(v8(80), o1, o2, ALU.add))
                for t in range(2):
                    ins = V.tensor_tensor(sel[:, t, :].rearrange("p (g e) -> p g e", g=4), goh8[:, t],
                                          spread(v8(80)[:, t:t + 1, :], 1, 4), ALU.mult)
                    if t == 0:
                        link(ins)
                ins.then_inc(S("sel_ready"), 1)
                dve.wait_ge(S("sel_ready"), l + 1)
                link(V.tensor_tensor(o1, o1, bc(w1, 8), ALU.mult))
                link(V.tensor_tensor(o2, o2, bc(w2, 8), ALU.mult))
                link(V.tensor_tensor(o1, o1, o2, ALU.add))
                for t in range(2):
                    inner = spread(o1[:, t:t + 1, :], 1, 4)
                    ins = V.tensor_tensor(comb[:, t, :].rearrange("p (g e) -> p g e", g=4), goh8[:, t], inner, ALU.mult)
                    if t == 0:
                        link(ins)
                ins.then_inc(S("comb_ready"), 1)

                dve.wait_ge(S("comb_ready"), l + 1)
                dve.wait_ge(S("places_psum"), l + 1)
                link(V.scalar_tensor_tensor(posm[:, :, :], bank[1][:, 0:2 * NE].rearrange("p (t e) -> p t e", t=2), 1.0,
                                            sel[:, :, :], ALU.add, ALU.mult))
                link(V.tensor_scalar(posm[:, :, :], posm[:, :, :], -1.0, None, ALU.add))
                link(V.tensor_reduce(load[:, :], bank[1][:, 2 * NE:3 * NE], AX_X, ALU.max))
                V.tensor_copy(load_i[:, :], load[:, :]).then_inc(S("load_known"), 1)
                for b in range(4):
                    half = slice(512 * (b % 2), 512 * (b % 2) + 512)
                    dve.wait_ge(S("x_hi_ready"), 4 * l + b + 1)
                    V.tensor_tensor(x_lo[:, b // 2, half], bank[2 + b][:, :], x_hi[:, b // 2, half].bitcast(F32),
                                    ALU.subtract).then_inc(S("x_lo_ready"), 1)

                def hidden(e, p, first):
                    dve.wait_ge(S(f"moe_silu_ready{l}"), e + 1)
                    dve.wait_ge(S("moe_up_ready"), e + (NE * l + 1))
                    V.tensor_tensor(um[:, :], silm[:, p, :], bank[5 + 2 * p][:, :], ALU.mult
                                    ).then_inc(S(f"moe_product{l}"), 1)
                    dve.wait_ge(S(f"moe_product{l}"), e + 1)
                    if not first:
                        dve.wait_ge(S("moe_down_used"), e + (NE * l - 1))
                    c = spread(comb_bc[:, bass.ds(e, 1), :], 1, 2)
                    V.tensor_tensor(hm[:, p, :].rearrange("p (f n) -> p f n", f=2), um.rearrange("p (f n) -> p f n", f=2),
                                    c, ALU.mult).then_inc(S(f"moe_hid_ready{l}"), 1)
                    dve.wait_ge(S(f"moe_hid_ready{l}"), e + 1)

                def pair_cols(v, s):
                    v = v[:, :, bass.ds(s * 2, 2)].rearrange("p t (e a) -> p t e a", a=1)
                    return spread(v, 3, CAP)

                def by_expert(v):
                    return v.rearrange("p t (e c) -> p t e c", e=2)

                def make_slots(s, p, first=False):
                    if not first:
                        dve.wait_ge(S(f"slots_turned{l}"), s - 1)
                    io = cst[:, C_IO:C_IO + CAP].rearrange("p (a b c) -> p a b c", a=1, b=1)
                    V.tensor_tensor(by_expert(slots[:, p, :, :]), spread(spread(io, 1, 2), 2, 2), pair_cols(posm, s),
                                    ALU.is_equal).then_inc(S(f"slots_ready{l}"), 1)

                def weigh_slots(s, p, first=False):
                    if not first:
                        dve.wait_ge(S(f"slots_turned{l}"), s)
                    dve.wait_ge(S(f"slots_ready{l}"), s + 1)
                    V.tensor_tensor(by_expert(slotw[:, :, :]), by_expert(slots[:, p, :, :].bitcast(F32)),
                                    pair_cols(comb, s), ALU.mult).then_inc(S(f"slotw_ready{l}"), 1)

                def low(s):
                    dve.wait_ge(S(f"o_hi_ready{l}"), s + 1)
                    for half in range(2):
                        c = slice(512 * half, 512 * half + 512)
                        ins = V.scalar_tensor_tensor(o_lo[:, c], bank[4 + half][:, :], wslot[:, 0:1],
                                                     o_hi[:, c].bitcast(F32), ALU.mult, ALU.subtract)
                    ins.then_inc(S(f"o_lo_ready{l}"), 1)

                def product(s, first=False):
                    dve.wait_ge(S(f"silu_pair_ready{l}"), s + 1)
                    dve.wait_ge(S("moe_up_ready"), s * 2 + (NE * l + 2))
                    if not first:
                        dve.wait_ge(S("moe_down_used"), s * 2 + NE * l)
                    V.tensor_tensor(hs[:, :], sl[:, :], bank[6][:, 256:512], ALU.mult).then_inc(S(f"hs_ready{l}"), 1)

                def save_gathered(s):
                    dve.wait_ge(S(f"gathered{l}"), s * 2 + 2)
                    V.tensor_copy(xg[:, 4:8, :], bank[5].rearrange("p (k n) -> p k n", k=4)
                                  ).then_inc(S(f"xg_high_ready{l}"), 1)

                dve.wait_ge(S("load_known"), l + 1)
                with dve.If(dve.value_load(load_i[0:1, 0:1]) > CAP):
                    dve.wait_ge(S(f"comb_loaded{l}"), 16)
                    hidden(0, 0, True)
                    hidden(1, 1, True)
                    with dve.Fori(1, PAIRS) as i:
                        for p in range(2):
                            hidden(i * 2 + p, p, False)
                with dve.Else():
                    make_slots(0, 0, True)
                    make_slots(1, 1, True)
                    weigh_slots(0, 0, True)
                    save_gathered(0)
                    product(0, True)
                    save_gathered(1)

                    def step(s, p):
                        make_slots(s + 2, p)
                        weigh_slots(s + 1, 1 - p)
                        low(s)
                        product(s + 1)
                        save_gathered(s + 2)

                    with dve.Fori(0, PAIRS // 2 - 1) as i:
                        for p in range(2):
                            step(i * 2 + p, p)
                    weigh_slots(PAIRS - 1, 1)
                    low(PAIRS - 2)
                    product(PAIRS - 1)
                    low(PAIRS - 1)
                dve.wait_ge(S("experts_done"), l + 1)
                for d in range(KT):
                    h = hT[:, d, NMETA:T1]
                    V.tensor_tensor(h, bank[d // 2][:, T2 * (d % 2):T2 * (d % 2) + T2], h, ALU.add
                                    ).then_inc(S("residual_ready"), 1)
            norm(7)


def _chunks(w):
    n = w.shape[1]
    return w.reshape(KT, P, n // 256, 256).transpose(2, 1, 0, 3).reshape(n // 256, P, CH)


def _row_chunks(w):
    n = w.shape[0]
    return w.reshape(n // 256, 2, P, D).transpose(0, 2, 1, 3).reshape(n // 256, P, CH)


def _pad_cols(w, n):
    return np.concatenate([w, np.zeros((w.shape[0], n - w.shape[1]), w.dtype)], axis=1)


def _pairs(a, b):
    return np.stack([a, b], axis=1).reshape(-1, P, CH)


def _layout(i):
    col = lambda v: np.ascontiguousarray(v.reshape(-1, P).T)
    parts = []
    for f in ("ffn1", "ffn2"):
        gu = _pairs(_chunks(i[f + "_w_gate"][0]), _chunks(i[f + "_w_up"][0]))
        parts.append([gu, _row_chunks(i[f + "_w_down"][0])])
    w_in = i["w_in"][0]
    first_in = np.concatenate([w_in[:, 0:2816], _pad_cols(w_in[:, 2816:2888], 256)], axis=1)
    stream = parts[0] + [_chunks(first_in), _row_chunks(i["w_out"][0])] + parts[1]
    small2 = []
    for l in range(LAYERS):
        w = i["w_in_2"][l]
        w = np.concatenate([w[:, 0:256], _pad_cols(w[:, 256:416], 256), w[:, 416:1440]], axis=1)
        stream += [_chunks(w), _row_chunks(i["w_out_2"][l])]
        g, u, d = (i[k][l].reshape(NE, -1, i[k].shape[-1]) for k in ("w_gate_2", "w_up_2", "w_down_2"))
        g, u = (a.reshape(NE, KT, P, 256).transpose(0, 2, 1, 3).reshape(NE, P, CH) for a in (g, u))
        d = d.reshape(NE, 2, P, D).transpose(0, 2, 1, 3).reshape(NE, P, CH)
        stream.append(np.stack([g[0::2], u[0::2], g[1::2], u[1::2], d[0::2], d[1::2]], axis=1).reshape(3 * NE, P, CH))
        wp = np.zeros((P, 2, P), np.float32)
        for t in range(2):
            for j in range(2):
                wp[64 * j:64 * j + 64, t, 64 * j:64 * j + 64] = i["pool_w_2"][l][2 * t + j]
        rt = np.concatenate([i["w_group_2"][l], i["w_expert_2"][l]], axis=1)
        small2.append(np.concatenate([
            i["w_uq_2"][l].reshape(2, P, 768).transpose(1, 0, 2).reshape(P, -1),
            i["w_ukv_2"][l].reshape(P, -1),
            wp.reshape(P, -1),
            rt.reshape(KT, P, 36).transpose(1, 0, 2).reshape(P, -1)], axis=1))
    norms = [i["ffn1_norm"][0], i["mix_norm"][0], i["ffn2_norm"][0]]
    for l in range(LAYERS):
        norms += [i["norm1_g_2"][l], i["norm2_g_2"][l]]
    norms.append(i["final_g_2"])
    twice = lambda v: np.concatenate([v, v]).reshape(P, 1)
    rows = [i[f"a_lambda_{k}"][0] for k in ("q1", "k1", "q2", "k2")]
    for l in range(LAYERS):
        rows += [i["b_group_2"][l], i["b_expert_2"][l]]
    gains = [col(v) for v in norms] + [twice(i["a_q_norm"][0]), twice(i["a_k_norm"][0]), col(i["b_kv_norm"][0]),
                                       col(i["b_q_norm"][0]), col(i["a_subln"][0])]
    gains += [col(i["q_norm_g_2"][l]) for l in range(LAYERS)] + [col(i["kv_norm_g_2"][l]) for l in range(LAYERS)]
    gains += [col(i["pool_scale_2"][l]) for l in range(LAYERS)]
    gains.append(np.broadcast_to(np.concatenate(rows)[None], (P, 4 * ADK + LAYERS * 36)))
    gains.append(np.broadcast_to(np.array([w * EPS for w in EPS_AT], np.float32), (P, len(EPS_AT))))
    return {
        "stream": np.concatenate(stream),
        "gains": np.concatenate(gains, axis=1),
        "consts": constants(),
        "x_tok": np.concatenate([i["meta_tokens"], i["x"][0]]),
        "rel_bias": i["rel_bias"],
        "wuk": i["b_w_uk"][0].transpose(1, 0, 2),
        "wuv": i["b_w_uv"][0].reshape(4, 2, P, P).transpose(2, 0, 1, 3),
        "small2": np.stack(small2),
    }


def kernel(**inputs):
    import concourse.bacc as bacc
    from concourse.bass_utils import run_bass_kernel_spmd

    nc = bacc.Bacc("TRN2", target_bir_lowering=False, num_devices=1)
    arrays, args = {}, []
    for name, a in _layout({k: np.asarray(v) for k, v in inputs.items()}).items():
        a = np.ascontiguousarray(a)
        arrays[f"in_{name}"] = a
        args.append(nc.dram_tensor(f"in_{name}", a.shape, mybir.dt.from_np(a.dtype), kind="ExternalInput").ap())
    out = nc.dram_tensor("out", (1, SEQ, D), F32, kind="ExternalOutput").ap()
    build(nc, *args, out)
    r = run_bass_kernel_spmd(nc, [arrays], core_ids=[0])
    return r.results[0]["out"]
```

```python
from contextlib import ExitStack
import math

import numpy as np

import concourse.bass as bass
from concourse import mybir

F32 = mybir.dt.float32
F32R = mybir.dt.float32r
I32 = mybir.dt.int32
BF16 = mybir.dt.bfloat16
ALU = mybir.AluOpType
ACT = mybir.ActivationFunctionType
AX_X = mybir.AxisListType.X

P = 128
D = 1024
KT = D // P
NMETA, SEQ = 16, 256
T1 = NMETA + SEQ
T2 = SEQ
D_FF = 2816
FT = D_FF // P
FC = FT // 2
CH = KT * 256
AH, ADK, ADV = 4, 64, 128
BH, BDC = 4, 256
IH, TOPK = 8, 64
BLOCKS1 = [(0, 128), (128, 128), (256, T1 - 256)]
BLOCKS2 = [(0, 128), (128, 128)]
MH = 8
SH = 4
NE = 32
LAYERS = 2
CAP = 64
PAIRS = NE // 2
NEG = -1e30
TAKEN = -3e38
EPS = 1e-6
LAM0 = 0.8 - 0.6 * math.exp(0.0)
GX = 384
ROW = 512
NS = 6
NS2 = 12
AR = 17850

G_NORM = 0
G_AQ, G_AK, G_BKV, G_BQ, G_SUB = 64, 65, 66, 68, 70
G_QN, G_KVN, G_PS = 71, 75, 77
G_LAM = 81
G_RB = G_LAM + 4 * ADK
G_EPS = G_RB + LAYERS * 36
EPS_AT = {1024: 0, 64: 1, 256: 2, 128: 3}
G_ALL = G_EPS + len(EPS_AT)

C_ID, C_ONE, C_BD, C_UP = 0, 128, 256, 384
C_CM = 512
C_M2 = C_CM + GX
C_NM = C_M2 + 256
C_COS = C_NM + 384
C_IC = C_COS + 4 * T2
C_FO = C_IC + 2 * T2
C_IO = C_FO + 32
C_BE = C_IO + CAP
C_ALL = C_BE + P
C_OH = 0
C_OM = ROW

def spread(ap, axis, n):
    shape = list(ap.shape)
    shape[axis] = n
    return ap.broadcast_to(shape)


def constants():
    c = np.zeros((P, C_ALL), np.float32)
    p = np.arange(P)
    c[:, C_ID:C_ID + P] = np.eye(P)
    c[:, C_ONE:C_ONE + P] = 1.0
    c[:, C_BD:C_BD + P] = (p[:, None] // 64) == (p[None, :] // 64)
    c[:, C_UP:C_UP + P] = p[:, None] >= p[None, :]
    x = np.arange(GX)
    c[:, C_CM:C_CM + GX] = np.where(p[:, None] + 256 - x[None, :] >= 0, 0.0, NEG)
    c[:64, C_M2 + 192:C_M2 + 256] = NEG
    q = np.arange(T2)
    c[:, C_NM:C_NM + T2] = np.where(p[:, None] < q[None, :], 0.0, NEG)
    c[:, C_NM + T2:C_NM + 384] = np.where(p[:, None] < p[None, :], 0.0, NEG)
    inv = (np.float32(10000.0) ** (-np.arange(0, 32, 2, dtype=np.float32) / np.float32(32))).astype(np.float32)
    ang = np.arange(T2, dtype=np.float32)[:, None] * inv[None, :]
    cos, sin = np.cos(ang).T, np.sin(ang).T
    cos2, sin2 = np.concatenate([cos, cos]), np.concatenate([-sin, sin])
    s = 96.0 ** -0.5
    for j, t in enumerate((cos2 * s, sin2 * s, cos2, sin2)):
        c[64:96, C_COS + j * T2:C_COS + (j + 1) * T2] = t
    for g, w in enumerate((2, 4, 8, 16)):
        r = slice(64 * (g % 2), 64 * (g % 2) + 64)
        c[r, C_IC + (g // 2) * T2:C_IC + (g // 2 + 1) * T2] = 1.0 / np.minimum(q + 1.0, w)
    c[:, C_FO:C_FO + 32] = 32 - np.arange(32)
    n = 383 - np.arange(ROW)
    nf = np.maximum(n, 1).astype(np.float32)
    large = 16 + (np.log(nf / np.float32(16)) / np.float32(math.log(8)) * np.float32(16)).astype(np.int32)
    bucket = np.where(np.maximum(n, 0) < 16, np.maximum(n, 0), np.minimum(large, 31))
    b = np.zeros((32, 2 * ROW), np.float32)
    b[:, C_OH:C_OH + ROW] = np.arange(32)[:, None] == bucket[None, :]
    b[:, C_OM:C_OM + ROW] = np.where(n >= 0, 0.0, NEG)
    c[:, C_IO:C_IO + CAP] = np.arange(CAP)
    c[:, C_BE:C_BE + P] = p[:, None] < p[None, :]
    return c, b


def build(nc, stream, gains, consts, bias_consts, x_tok, rel_bias, wuk, wuv, small2, out):
    with ExitStack() as ctx:
        sems = {}

        def S(name):
            if name not in sems:
                sems[name] = ctx.enter_context(nc.semaphore(name))
            return sems[name]

        def sb(name, shape, dt=F32):
            return ctx.enter_context(nc.sbuf_tensor(name, shape, dt))

        ring = sb("ring", [P, NS, CH])
        hT = sb("hT", [P, KT, T1])
        xn = sb("xn", [P, KT, T1])
        sq = sb("sq", [P, 10, T1])
        root = sb("root", [P, 2, T1])
        rstd = sb("rstd", [P, 2, T1])
        mixT = sb("mixT", [P, KT, T1])
        G = sb("G", [P, 8, GX])
        cst = sb("cst", [P, C_ALL])
        gn = sb("gn", [P, G_ALL])
        w_uk = sb("w_uk", [P, 4, 256])
        w_uv = sb("w_uv", [P, 4, 2, P])
        SM = 1536 + 1024 + 256 + 288
        sm = sb("sm", [P, SM])
        w_uq = sm[:, 0:1536].rearrange("p (k n) -> p k n", k=2)
        w_ukv = sm[:, 1536:2560].rearrange("p (h n) -> p h n", h=MH)
        w_pool = sm[:, 2560:2816].rearrange("p (t n) -> p t n", t=2)
        w_rt = sm[:, 2816:3104].rearrange("p (k n) -> p k n", k=KT)
        rb = sb("rb", [32, 8])
        zb = sb("zb", [P, 512], BF16)
        wslot = sb("wslot", [P, 1])
        load = sb("load", [P, 1])
        load_i = sb("load_i", [P, 1], I32)
        mx = sb("mx", [P, 2, 2])
        nmx = sb("nmx", [P, 2, 2])
        sums = sb("sums", [P, 2, 2])
        rs = sb("rs", [P, 2, 2])
        top8 = sb("top8", [P, 8])
        lamb = sb("lamb", [P, 8])
        lprod = sb("lprod", [P, ADK])
        arena_space = nc.sbuf_tensor("arena", [P, AR], F32)
        arena = arena_space.__enter__()
        arena_space.__exit__(None, None, None)
        with ExitStack() as ffn_space:
            fr = lambda name, shape: ffn_space.enter_context(nc.sbuf_tensor(name, shape, F32R))
            w_hi = fr("w_hi", [P, 2, CH])
            w_lo = fr("w_lo", [P, 2, CH])
            r_hi = fr("r_hi", [P, KT, T1])
            r_lo = fr("r_lo", [P, KT, T1])
        FR = 4 * CH + 2 * KT * T1
        x_hi = sb("x_hi", [P, 2, D], F32R)
        x_lo = sb("x_lo", [P, 2, D], F32R)
        slots = sb("slots", [P, 2, 2, P], F32R)
        slotsT = sb("slotsT", [P, T2], F32R)
        o_hi = sb("o_hi", [P, D], F32R)
        o_lo = sb("o_lo", [P, D], F32R)

        at = {}

        def carve(name, off, *shape):
            n = int(np.prod(shape))
            at[name] = off + n
            assert off + n <= AR, (name, off + n)
            v = arena[:, off:off + n]
            if len(shape) == 2:
                v = v.rearrange("p (a b) -> p a b", a=shape[0])
            if len(shape) == 3:
                v = v.rearrange("p (a b c) -> p a b c", a=shape[0], b=shape[1])
            return v

        xtok = carve("xtok", 0, 3, D)
        hid_a = carve("hid_a", FR, FT - KT, T1)
        sil = carve("sil", at["hid_a"], 2, T1)

        def hid(i, n=1):
            return hid_a[:, i:i + n, :] if i < FT - KT else xn[:, i - (FT - KT):i - (FT - KT) + n, :]

        uT = carve("uT", 0, 18, T1)
        va = carve("va", at["uT"], 3, 512)
        ikT = carve("ikT", at["va"], T1)
        iw = carve("iw", at["ikT"], 3, IH)
        qlT = carve("qlT", at["iw"], 8, T1)
        ctok = carve("ctok", at["qlT"], 3, BDC)
        selb = carve("selb", at["ctok"], 3, T1)
        olT = carve("olT", at["selb"], 8, T1)
        W0 = at["olT"]
        s_sb = carve("s_sb", W0, 2, 2, 272)
        a_sb = carve("a_sb", at["s_sb"], 2, 272)
        aT = carve("aT", at["a_sb"], 2, 384)
        gb = carve("gb", at["aT"], 2, 272)
        score = carve("score", W0, 272)
        rel = carve("rel", W0 + 272, 4, 272)
        qcat = carve("qcat", 0, MH, T2)
        kcat = carve("kcat", at["qcat"], MH, T2)
        vm = carve("vm", at["kcat"], 2, 512)
        qbT = carve("qbT", at["vm"], 2, T2)
        kbT = carve("kbT", at["qbT"], 2, T2)
        vb = carve("vb", at["kbT"], 2, T2)
        cq = carve("cq", at["vb"], 2, T2)
        ckv = carve("ckv", at["cq"], 1, T2)
        wuqs = carve("wuqs", at["ckv"], 2, MH, 32)
        wkrs = carve("wkrs", at["wuqs"], KT, 32)
        rt1 = carve("rt1", at["wkrs"], 2, T2)
        rt2 = carve("rt2", at["rt1"], 2, T2)
        PO = at["rt2"]
        upad = carve("upad", PO, 2, 272)
        ps2 = carve("ps2", at["upad"], 2, 272)
        ps4 = carve("ps4", at["ps2"], 2, 272)
        pd = carve("pd", at["ps4"], 2, T2)
        assert at["pd"] <= W0, (at["pd"], W0)
        zm = carve("zm", W0, SH, 384)
        ln = carve("ln", at["zm"], SH, 384)
        comb_bc = carve("comb_bc", 0, NE, T2)
        silm = carve("silm", at["comb_bc"], 2, 512)
        um = carve("um", at["silm"], 512)
        hm = carve("hm", at["um"], 2, 512)
        rl = carve("rl", at["hm"], 2, 36)
        comb = carve("comb", at["rl"], 2, NE)
        combT = carve("combT", at["comb"], T2)
        e8 = carve("e8", at["combT"], 2, 8)
        t48 = carve("t48", at["e8"], 2, NE)
        small = carve("small", at["t48"], 160)
        sel = carve("sel", at["small"], 2, NE)
        posm = carve("posm", at["sel"], 2, NE)
        XF = 6912
        xg = carve("xg", XF, KT, P)
        hs = carve("hs", at["xg"], 256)
        sl = carve("sl", at["hs"], 256)
        slotw = carve("slotw", at["sl"], 2, P)
        hp = carve("hp", at["slotw"], 256)
        assert at["hp"] <= at["comb_bc"] + 2560
        otok = carve("otok", 0, 2, D)
        mix_flat = mixT.rearrange("p a b -> p (a b)")
        btab = mix_flat[0:8, 0:ROW]
        bcst = mix_flat[0:32, ROW:3 * ROW]
        assert AR - 3 * CH >= at["posm"]
        flat = lambda v: v.rearrange("p a b -> p (a b)")[:, 0:CH]
        slot_at = [ring[:, j, :] for j in range(NS)]
        slot_at += [flat(G), flat(mixT), flat(sq)] + [arena[:, AR - (j + 1) * CH:AR - j * CH] for j in range(3)]

        bank = [ctx.enter_context(nc.psum_tensor(f"bank{i}", [P, 512], F32)) for i in range(8)]
        bias_rows = nc.dram_tensor("bias_rows", (8, ROW), F32).ap()
        bias_skew = nc.dram_tensor("bias_skew", (P, 8 * ROW), F32).ap()
        comb_dram = nc.dram_tensor("comb_dram", (LAYERS, NE, T2), F32).ap()

        ident, ones = cst[:, C_ID:C_ID + P], cst[:, C_ONE:C_ONE + P]
        bd64, upper = cst[:, C_BD:C_BD + P], cst[:, C_UP:C_UP + P]

        def gain(c):
            return gn[:, c:c + 1]

        span = [(0, T1)] * 3 + [(NMETA, T2)] * 5

        PAIR_ORDER = [("moe_gate_ready", 0), ("moe_gate_ready", 1), ("moe_up_ready", 0), ("moe_up_ready", 1),
                      ("moe_down_used", 0), ("moe_down_used", 1)]

        freed = []
        used_at = [0, 0]
        X_LO = [0, 4]
        used = 0
        units = 0
        MOE_AT = []

        def plan_ffn(f, k):
            nonlocal used
            used_at[f] = used
            used += FC - 1
            for q in range(3 * FC):
                freed.append(("w_lo_ready", 3 * FC * f + q + 1))

        def plan_down(k, n):
            nonlocal used
            for c in range(n - 1):
                used += 1
                freed.append(("down_used", used))
            freed.append(("y_ready", 8 * (k + 1)))

        def plan_proj(per_chunk):
            nonlocal units
            for n in per_chunk:
                units += n
                freed.append(("proj_ready", units))

        A_FFN1 = len(freed)
        plan_ffn(0, 0)
        A_IN1 = len(freed)
        PER1 = [2, 2, 2, 2, 3, 3, 2, 2, 2, 2, 2, 2]
        plan_proj(PER1)
        A_OUT1 = len(freed)
        plan_down(1, 4)
        A_FFN2 = len(freed)
        plan_ffn(1, 2)
        A_IN2, A_OUT2 = [], []
        PER2 = [2, 3, 2, 2, 1, 2]
        for l in range(LAYERS):
            A_IN2.append(len(freed))
            plan_proj(PER2)
            A_OUT2.append(len(freed))
            plan_down(3 + l, 4)
            MOE_AT.append(len(freed))
            for s in range(PAIRS):
                for j, (name, e) in enumerate(PAIR_ORDER):
                    freed.append((name, NE * l + 2 * s + e + 1))
        NCHUNK = len(freed)
        U1, U2 = sum(PER1), sum(PER2)
        SAVED2 = U2 - 2

        slot_of, loads_of, wait_of = [], [], []
        last = [None] * NS2
        count = [0] * NS2
        turn = 0
        for n in range(NCHUNK):
            l = next((l for l in range(LAYERS) if MOE_AT[l] <= n < MOE_AT[l] + 3 * NE), None)
            if l is None:
                j = turn % NS
                turn += 1
            else:
                j = (n - MOE_AT[l]) % NS2
                turn = 0
            waits = [last[j]] if last[j] else []
            if l is not None and j >= NS and n - MOE_AT[l] < NS2:
                waits = [("sumsq_ready", 5 + 2 * l)]
            slot_of.append(j)
            count[j] += 1
            loads_of.append(count[j])
            wait_of.append(waits)
            last[j] = freed[n]

        def up_part(w, q):
            return w[:, q % 2, :].rearrange("p (k n) -> p k n", k=KT)

        def down_part(w, q):
            return w[:, q % 2, :].rearrange("p (f n) -> p f n", f=2)

        def part_free(eng, f, q):
            if q < 2:
                return
            c = (q - 2) // 2
            if q - 2 < 2 * FC:
                eng.wait_ge(S(("gate_ready", "up_ready")[q % 2]), FT * f + 2 * c + 2)
            else:
                eng.wait_ge(S("down_used"), used_at[f] + q - 2 - 2 * FC + 1)

        def chunk(n):
            return slot_at[slot_of[n]]

        def up_view(n):
            return chunk(n).rearrange("p (k n) -> p k n", k=KT)

        def down_view(n):
            return chunk(n).rearrange("p (f n) -> p f n", f=2)

        def slot_sem(n):
            return S(f"slot{slot_of[n]}_loaded")

        def loaded(eng, n):
            eng.wait_ge(slot_sem(n), 16 * loads_of[n])

        units_all = []

        def seg(make):
            at0 = len(units_all)
            units_all.extend(make)
            return at0, len(units_all)

        def block_bias(h, i, nq, L):
            x0 = P * (2 - i)
            return G[0:nq, h, x0:x0 + L]

        def unit_a(i, h):
            q0, nq = BLOCKS1[i]
            L = q0 + nq
            return dict(
                maps=2, nq=nq, L=L, q0=q0, kind="a", h=h, i=i,
                score=[[(uT[64 * m:64 * m + 64, h, q0:q0 + nq], uT[64 * m:64 * m + 64, 4 + h, 0:L])] for m in range(2)],
                bias=block_bias(h, i, nq, L),
                v=[lambda k, nk: va[0:nk, k, P * h:P * h + P]], base=0, M=P,
                out=mixT[:, h, q0:q0 + nq])

        def unit_b(i, h):
            q0, nq = BLOCKS1[i]
            L = q0 + nq
            return dict(
                maps=1, nq=nq, L=L, q0=q0, kind="b", h=h, i=i,
                score=[[(qlT[:, 2 * h + c, q0:q0 + nq], uT[:, 12 + c, 0:L]) for c in range(2)]],
                bias=None,
                v=[lambda k, nk, c=c: ctok[0:nk, k, P * c:P * c + P] for c in range(2)], base=0, M=P,
                out=olT[:, 2 * h:2 * h + 2, q0:q0 + nq])

        def unit_m(i, h):
            q0, nq = BLOCKS2[i]
            L = q0 + nq
            b = 64 * (h % 2)
            return dict(
                maps=1, nq=nq, L=L, q0=q0, kind="m", h=h, i=i,
                score=[[(qcat[0:96, h, q0:q0 + nq], kcat[0:96, h, 0:L])]],
                bias=cst[:, C_M2 + P * (1 - i):C_M2 + 256],
                v=[lambda k, nk: vm[0:nk, k, 64 * h:64 * h + 64]], base=b, M=64,
                out=mixT[b:b + 64, h // 2, q0:q0 + nq])

        SEG_A = seg([unit_a(i, h) for i in range(3) for h in range(AH)])
        SEG_B = seg([unit_b(i, h) for i in range(3) for h in range(BH)])
        SEG_M = [seg([unit_m(i, h) for i in range(2) for h in range(MH)]) for l in range(LAYERS)]

        def key_tiles(u):
            return [(k, min(P, u["L"] - P * k)) for k in range((u["L"] + P - 1) // P)]

        def steps(segment, *stages):
            a, b = segment
            for s in range(a, b + len(stages) - 1):
                for j, stage in enumerate(stages):
                    if a <= s - j < b:
                        stage(s - j)

        def qcols(i):
            q0, nq = BLOCKS1[i]
            return q0, nq, q0 + nq

        block = ctx.enter_context(nc.Block())

        @block.sync
        def _(sp):
            def load(n):
                for name, v in wait_of[n]:
                    sp.wait_ge(S(name), v)
                sp.dma_start(chunk(n), stream[n]).then_inc(slot_sem(n), 16)

            sp.wait_ge(S("consts_loaded"), 16)
            sp.wait_ge(S("x_loaded"), 32)
            n = 0
            for l in range(LAYERS):
                while n < MOE_AT[l] + NS2:
                    load(n)
                    n += 1
                with sp.Fori(1, NE // 4) as i:
                    for j in range(NS2):
                        m = MOE_AT[l] + j
                        name, e = PAIR_ORDER[j % 6]
                        sp.wait_ge(S(name), i * 4 + (NE * l - 4 + 2 * (j // 6) + e + 1))
                        sp.dma_start(chunk(m), stream[bass.ds(i * NS2 + m, 1)].rearrange("a p n -> p (a n)")
                                     ).then_inc(slot_sem(m), 16)
                n = MOE_AT[l] + 3 * NE
            for t in range(2):
                sp.wait_ge(S("out_ready"), 4 * (t + 1))
                sp.dma_start(out[0, P * t:P * t + P, :], otok[:, t, :]).then_inc(S("out_written"), 16)
            sp.wait_ge(S("out_written"), 32)

        @block.gpsimd
        def _(pool):
            n_chain = 0

            def link(ins):
                nonlocal n_chain
                n_chain += 1
                ins.then_inc(S("pool_chain"), 1)
                pool.wait_ge(S("pool_chain"), n_chain)

            nc.gpsimd.memset(zb[:], 0.0).then_inc(S("zeros_ready"), 1)
            pool.wait_ge(S("bias_rows_ready"), 1)
            pool.dma_start(bias_rows, btab[:, :]).then_inc(S("bias_rows_written"), 16)
            pool.wait_ge(S("bias_rows_written"), 16)
            src = spread(bias_rows.rearrange("(a h) n -> a (h n)", a=1), 0, P)
            pool.dma_start(bias_skew, src).then_inc(S("bias_skew_written"), 16)
            pool.wait_ge(S("bias_skew_written"), 16)
            for h in range(8):
                src = bass.AP(bias_skew.tensor, 127 + ROW * h, [[8 * ROW - 1, P], [1, GX]])
                pool.dma_start(G[:, h, :], src).then_inc(S("G_loaded"), 16)

            for g in range(*SEG_B):
                u = units_all[g]
                pool.wait_ge(S("G_loaded"), 16 * 8)
                pool.wait_ge(S("selected"), u["i"] + 1)
                if g - SEG_B[0] >= 2:
                    pool.wait_ge(S("scores_taken"), g - 1)
                else:
                    pool.wait_ge(S("subln_done"), AH)
                nc.gpsimd.tensor_tensor(gb[0:u["nq"], g % 2, 0:u["L"]], block_bias(4 + u["h"], u["i"], u["nq"], u["L"]),
                                        selb[0:u["nq"], u["i"], 0:u["L"]], ALU.add).then_inc(S("bias_ready"), 1)

            for l in range(LAYERS):
                pool.wait_ge(S("small2_loaded"), 16 * (l + 1))
                if l == 0:
                    pool.wait_ge(S("residual_ready"), 8 * 3)
                else:
                    pool.wait_ge(S("residual_ready"), 8 * 5)
                wq = w_uq.rearrange("p k (h n) -> p k h n", h=MH)
                for k in range(2):
                    link(nc.gpsimd.tensor_copy(wuqs[:, k, :, 0:16], wq[:, k, :, 80:96]))
                    link(nc.gpsimd.tensor_copy(wuqs[:, k, :, 16:32], wq[:, k, :, 64:80]))
                loaded(pool, A_IN2[l] + 1)
                wk = up_view(A_IN2[l] + 1)
                link(nc.gpsimd.tensor_copy(wkrs[:, :, 0:16], wk[:, :, 144:160]))
                nc.gpsimd.tensor_copy(wkrs[:, :, 16:32], wk[:, :, 128:144]).then_inc(S("swapped_ready"), 1)
                nc.gpsimd.memset(upad[:, :, 0:16], 0.0).then_inc(S("pad_ready"), 1)
                pool.wait_ge(S("pad_ready"), l + 1)
                pool.wait_ge(S("proj_saved"), U1 + SAVED2 * (l + 1))
                link(nc.gpsimd.tensor_tensor(ps2[:, :, 1:272], upad[:, :, 1:272], upad[:, :, 0:271], ALU.add))
                link(nc.gpsimd.tensor_tensor(ps4[:, :, 3:272], ps2[:, :, 3:272], ps2[:, :, 1:270], ALU.add))
                ic = cst[:, C_IC:C_IC + 2 * T2].rearrange("p (t n) -> p t n", t=2)
                link(nc.gpsimd.tensor_tensor(pd[0:64, 0, :], ps2[0:64, 0, 16:272], ic[0:64, 0, :], ALU.mult))
                link(nc.gpsimd.tensor_tensor(pd[64:128, 0, :], ps4[64:128, 0, 16:272], ic[64:128, 0, :], ALU.mult))
                link(nc.gpsimd.tensor_tensor(ps2[:, 1, 7:272], ps4[:, 1, 7:272], ps4[:, 1, 3:268], ALU.add))
                link(nc.gpsimd.tensor_tensor(pd[0:64, 1, :], ps2[0:64, 1, 16:272], ic[0:64, 1, :], ALU.mult))
                link(nc.gpsimd.tensor_tensor(ps4[:, 1, 15:272], ps2[:, 1, 15:272], ps2[:, 1, 7:264], ALU.add))
                link(nc.gpsimd.tensor_tensor(pd[64:128, 1, :], ps4[64:128, 1, 16:272], ic[64:128, 1, :], ALU.mult))
                nc.gpsimd.tensor_tensor(pd[:, :, :], pd[:, :, :], upad[:, :, 16:272], ALU.subtract
                                        ).then_inc(S("pool_d_ready"), 1)
                pool.wait_ge(S("load_known"), l + 1)
                with pool.If(pool.value_load(load_i[0:1, 0:1]) > CAP):
                    pool.wait_ge(S(f"combT_ready{l}"), 1)
                    pool.dma_start(comb_dram[l], combT[0:NE, :]).then_inc(S(f"comb_written{l}"), 16)
                    pool.wait_ge(S(f"comb_written{l}"), 16)
                    src = spread(comb_dram[l].rearrange("(a e) n -> a (e n)", a=1), 0, P)
                    pool.dma_start(comb_bc.rearrange("p e n -> p (e n)"), src).then_inc(S(f"comb_loaded{l}"), 16)
                    pool.wait_ge(S(f"comb_loaded{l}"), 16)
            pool.wait_ge(S("G_loaded"), 16 * 8)

        @block.scalar
        def _(act):
            n_chain = 0

            def link(ins):
                nonlocal n_chain
                n_chain += 1
                ins.then_inc(S("act_chain"), 1)
                act.wait_ge(S("act_chain"), n_chain)

            copy = nc.scalar.activation

            act.dma_start(cst[:], consts).then_inc(S("consts_loaded"), 16)
            act.dma_start(xtok[:, 0:2, :], x_tok[0:256].rearrange("(t p) n -> p t n", p=P)).then_inc(S("x_loaded"), 16)
            act.dma_start(xtok[0:16, 2, :], x_tok[256:272]).then_inc(S("x_loaded"), 16)
            act.dma_start(gn[:], gains).then_inc(S("gains_loaded"), 16)
            act.dma_start(rb[:], rel_bias).then_inc(S("rb_loaded"), 16)
            act.dma_start(bcst, bias_consts).then_inc(S("rb_loaded"), 16)
            act.dma_start(w_uk[:], wuk).then_inc(S("wuk_loaded"), 16)
            act.dma_start(w_uv[:], wuv).then_inc(S("wuv_loaded"), 16)
            act.dma_start(sm[:], small2[0]).then_inc(S("small2_loaded"), 16)

            for d in range(KT):
                act.wait_ge(S("xT_ready"), d + 1)
                copy(hT[:, d, :], bank[d][:, 0:T1], ACT.Copy).then_inc(S("input_saved"), 1)
            act.wait_ge(S("lam_sums_ready"), 1)
            copy(lamb[:, 2:4], lamb[:, 0:2], ACT.Exp).then_inc(S("lam_exp_ready"), 1)

            n_root = 0

            def take_root(src, width, ready, v):
                nonlocal n_root
                act.wait_ge(S(ready), v)
                if n_root >= 2:
                    act.wait_ge(S("root_used"), n_root - 1)
                nc.scalar.activation(root[:, n_root % 2, 0:src.shape[1]], src, ACT.Sqrt, bias=gain(G_EPS + EPS_AT[width])
                                     ).then_inc(S("root_ready"), 1)
                n_root += 1

            def squares(n):
                off, T = span[n]
                for half in range(2):
                    if n == 0:
                        act.wait_ge(S("input_saved"), 4 * (half + 1))
                    else:
                        act.wait_ge(S("residual_ready"), 8 * (n - 1) + 4 * (half + 1))
                    copy(sq[:, 4 * half:4 * half + 4, 0:T], hT[:, 4 * half:4 * half + 4, off:off + T], ACT.Square
                         ).then_inc(S("squares_ready"), 1)
                if n == 0:
                    act.wait_ge(S("gains_loaded"), 16)
                if n in (0, 2):
                    split_w(n // 2, 0)
                    split_w(n // 2, 1)
                take_root(bank[0][:, 0:T], D, "sumsq_ready", n + 1)

            def split_w(f, q):
                loaded(act, (A_FFN1, A_FFN2)[f] + q)
                part_free(act, f, q)
                copy(w_hi[:, q % 2, :], chunk((A_FFN1, A_FFN2)[f] + q), ACT.Copy).then_inc(S("w_hi_ready"), 1)

            def split_x(f):
                for j in range(4):
                    act.wait_ge(S("xn_ready"), KT * 2 * f + 2 * j + 2)
                    copy(r_hi[:, 2 * j:2 * j + 2, :], xn[:, 2 * j:2 * j + 2, :], ACT.Copy).then_inc(S("x_hi_ready"), 1)

            def split_hid(f, c):
                act.wait_ge(S("hid_ready"), FT * f + 2 * c + 2)
                act.wait_ge(S("up_ready"), FT * (f + 1))
                if c >= 4:
                    act.wait_ge(S("down_used"), used_at[f] + c - 3)
                j = 2 * (c % 4)
                copy(r_hi[:, j:j + 2, :], hid(2 * c, 2), ACT.Copy).then_inc(S("hid_hi_ready"), 1)

            def ffn(f):
                split_x(f)
                for c in range(FC):
                    for i in (2 * c, 2 * c + 1):
                        g = FT * f + i
                        act.wait_ge(S("gate_ready"), g + 1)
                        if i >= 2:
                            act.wait_ge(S("hid_ready"), g - 1)
                        copy(sil[:, i % 2, :], bank[2 * (i % 4)][:, 0:T1], ACT.Silu).then_inc(S("silu_ready"), 1)
                    split_w(f, 2 * c + 2)
                    if c == FC - 1:
                        split_hid(f, 0)
                    split_w(f, 2 * c + 3)
                split_hid(f, 1)
                for c in range(FC - 2):
                    split_w(f, 2 * FC + c + 2)
                    split_hid(f, c + 2)

            def save(u, *ops):
                act.wait_ge(S("proj_ready"), u + 1)
                for op in ops[:-1]:
                    link(op())
                ops[-1]().then_inc(S("proj_saved"), 1)

            def exps(g):
                u = units_all[g]
                act.wait_ge(S("max_ready"), g + 1)
                for m in range(u["maps"]):
                    s = s_sb[0:u["nq"], g % 2, m, 0:u["L"]]
                    ins = nc.scalar.activation(s, s, ACT.Exp, bias=nmx[0:u["nq"], g % 2, m:m + 1],
                                               accum_out=sums[0:u["nq"], g % 2, m:m + 1])
                ins.then_inc(S("exps_ready"), 1)

            def save_T(g):
                u = units_all[g]
                act.wait_ge(S("aT_ready"), g + 1)
                if g >= 2:
                    act.wait_ge(S("o_ready"), g - 1)
                kts = key_tiles(u)
                nq = u["nq"]
                full = [k for k, nk in kts if nk == P]
                ops = []
                if full:
                    w = nq * len(full)
                    ops.append((aT[:, g % 2, 0:w], bank[4 + g % 2][:, 0:w]))
                if kts[-1][1] < P:
                    k, nk = kts[-1]
                    ops.append((aT[0:nk, g % 2, nq * k:nq * k + nq], bank[4 + g % 2][0:nk, nq * k:nq * k + nq]))
                for o, i in ops[:-1]:
                    link(copy(o, i, ACT.Copy))
                copy(ops[-1][0], ops[-1][1], ACT.Copy).then_inc(S("aT_saved"), 1)

            def save_o(g):
                u = units_all[g]
                act.wait_ge(S("o_ready"), g + 1)
                b, M, nq = u["base"], u["M"], u["nq"]
                src = bank[6 + g % 2][b:b + M, 0:nq * len(u["v"])]
                if len(u["v"]) == 2:
                    src = src.rearrange("p (c n) -> p c n", c=2)
                if u["kind"] == "a":
                    link(copy(u["out"], src, ACT.Copy))
                    copy(sq[:, u["h"], u["q0"]:u["q0"] + nq], src, ACT.Square).then_inc(S("o_saved"), 1)
                else:
                    copy(u["out"], src, ACT.Copy).then_inc(S("o_saved"), 1)

            squares(0)
            ffn(0)
            squares(1)
            act.wait_ge(S("bias_rows_written"), 16)
            u = 0
            for t in range(8):
                save(u, lambda: copy(uT[:, t, :], bank[u % 8][:, 0:T1], ACT.Copy),
                     lambda: copy(sq[:, t, :], bank[u % 8][:, 0:T1], ACT.Square))
                u += 1
            for c in range(2):
                for t, (q0, nq) in enumerate(BLOCKS1):
                    save(u, lambda: copy(va[0:nq, t, 256 * c:256 * c + 256], bank[u % 8][0:nq, 0:256], ACT.Copy))
                    u += 1
            for t in range(4):
                save(u, lambda: copy(uT[:, 8 + t, :], bank[u % 8][:, 0:T1], ACT.Copy))
                u += 1
            for t in range(2):
                save(u, lambda: copy(uT[:, 12 + t, :], bank[u % 8][:, 0:T1], ACT.Copy),
                     lambda: copy(sq[:, 8 + t, :], bank[u % 8][:, 0:T1], ACT.Square))
                u += 1
            for t in range(4):
                save(u, lambda: copy(uT[:, 14 + t, :], bank[u % 8][:, 0:T1], ACT.Copy))
                u += 1
            save(u, lambda: copy(ikT[:, :], bank[u % 8][:, 0:T1], ACT.Copy))
            u += 1
            iwb = bank[u % 8][:, 0:24].rearrange("p (t n) -> p t n", t=3)
            save(u, lambda: nc.scalar.activation(iw[:, 0:2, :], iwb[:, 0:2, :], ACT.Copy, scale=IH ** -0.5),
                 lambda: nc.scalar.activation(iw[0:16, 2, :], iwb[0:16, 2, :], ACT.Copy, scale=IH ** -0.5))
            for t in range(8):
                take_root(bank[t][:, 0:T1], ADK, "norm1_psum", t + 1)
            take_root(bank[0][:, 0:T1], BDC, "normc_psum", 1)
            for t in range(8):
                act.wait_ge(S("qlat_ready"), t + 1)
                link(copy(qlT[:, t, :], bank[t][:, 0:T1], ACT.Copy))
                copy(sq[:, t, :], bank[t][:, 0:T1], ACT.Square).then_inc(S("qlat_saved"), 1)
            for h in range(BH):
                take_root(bank[h][:, 0:T1], BDC, "normq_psum", h + 1)
            for t, (q0, nq) in enumerate(BLOCKS1):
                act.wait_ge(S("ctok_ready"), t + 1)
                copy(ctok[0:nq, t, :], bank[4 + t][0:nq, 0:BDC], ACT.Copy).then_inc(S("ctok_saved"), 1)
            for i in range(3):
                q0, nq, L = qcols(i)
                for h in range(IH):
                    n = IH * i + h
                    act.wait_ge(S("dots_ready"), n + 1)
                    if n >= 4:
                        act.wait_ge(S("score_added"), n - 3)
                    nc.scalar.activation(rel[0:nq, n % 4, 0:L], bank[n % 4][0:nq, 0:L], ACT.Relu, scale=0.125
                                         ).then_inc(S("relu_ready"), 1)
            steps(SEG_A, exps, save_T, save_o)
            for h in range(AH):
                take_root(bank[h][:, 0:T1], ADV, "subln_psum", h + 1)
            steps(SEG_B, exps, save_T, save_o)
            for h in range(BH):
                act.wait_ge(S("ob_ready"), h + 1)
                copy(mixT[:, 4 + h, :], bank[h][:, 0:T1], ACT.Copy).then_inc(S("ob_saved"), 1)
            squares(2)
            ffn(1)

            for l in range(LAYERS):
                squares(3 + 2 * l)
                u = U1 + U2 * l
                v = lambda b: bank[b % 8][:, 0:T2]
                for t in range(2):
                    save(u, lambda: copy(cq[:, t, :], v(u), ACT.Copy), lambda: copy(sq[:, t, 0:T2], v(u), ACT.Square))
                    u += 1
                save(u, lambda: copy(ckv[:, 0, :], v(u), ACT.Copy), lambda: copy(sq[:, 2, 0:T2], v(u), ACT.Square))
                u += 1
                u += 2
                for dst in (qbT, kbT):
                    for t in range(2):
                        save(u, lambda: copy(dst[:, t, :], v(u), ACT.Copy))
                        u += 1
                save(u, lambda: copy(vb.rearrange("p t n -> p (t n)"), bank[u % 8][:, :], ACT.Copy))
                u += 1
                act.wait_ge(S("pad_ready"), l + 1)
                for t in range(2):
                    save(u, lambda: copy(upad[:, t, 16:272], v(u), ACT.Copy))
                    u += 1
                take_root(bank[0][:, 0:T2], 256, "norm_lat_psum", 2 * l + 1)
                take_root(bank[1][:, 0:T2], 128, "norm_lat_psum", 2 * l + 2)
                for n in range(4):
                    act.wait_ge(S("q_up_ready"), 4 * l + n + 1)
                    nc.scalar.activation(qcat[0:64, 2 * n:2 * n + 2, :],
                                         bank[2 * (n % 2)][0:64, :].rearrange("p (h n) -> p h n", h=2),
                                         ACT.Copy, scale=96.0 ** -0.5).then_inc(S("q_nope_saved"), 1)
                for n in range(4):
                    act.wait_ge(S("k_up_ready"), 4 * l + n + 1)
                    copy(kcat[0:64, 2 * n:2 * n + 2, :], bank[4 + n % 2][0:64, :].rearrange("p (h n) -> p h n", h=2),
                         ACT.Copy).then_inc(S("k_nope_saved"), 1)
                for t in range(2):
                    act.wait_ge(S("v_up_ready"), 2 * l + t + 1)
                    copy(vm[:, t, :], bank[6 + t][:, :], ACT.Copy).then_inc(S("vm_saved"), 1)
                steps(SEG_M[l], exps, save_T, save_o)
                for h in range(SH):
                    act.wait_ge(S("nabs_ready"), SH * l + h + 1)
                    link(copy(ln[:, h, :], ln[:, h, :], ACT.Exp))
                for h in range(SH):
                    nc.scalar.activation(ln[:, h, :], ln[:, h, :], ACT.Ln, bias=1.0).then_inc(S("ln_ready"), 1)
                for h in range(SH):
                    act.wait_ge(S("stick_log_ready"), SH * l + h + 1)
                    copy(ln[:, h, :], zm[:, h, :], ACT.Exp).then_inc(S("stick_ready"), 1)
                for h in range(SH):
                    b = 64 * (h % 2)
                    act.wait_ge(S("stick_o_ready"), SH * l + h + 1)
                    copy(mixT[b:b + 64, 4 + h // 2, 0:T2], bank[4 + h][b:b + 64, 0:T2], ACT.Copy
                         ).then_inc(S("stick_saved"), 1)
                for t in range(2):
                    act.wait_ge(S("pool_y_ready"), l + 1)
                    nc.scalar.activation(mixT[:, 6 + t, 0:T2], bank[0][:, T2 * t:T2 * t + T2], ACT.Copy,
                                         scale=gain(G_PS + 2 * l + t)).then_inc(S("pool_saved"), 1)
                squares(4 + 2 * l)
                act.wait_ge(S("router_shifted"), l + 1)
                copy(small[:, 16:24], small[:, 8:16], ACT.Exp).then_inc(S("router_exp1"), 1)
                act.wait_ge(S("router_gap"), l + 1)
                copy(small[:, 44:46], small[:, 40:42], ACT.Exp).then_inc(S("router_exp2"), 1)
                if l + 1 < LAYERS:
                    act.wait_ge(S("router_ready"), l + 1)
                    act.dma_start(sm[:], small2[l + 1]).then_inc(S("small2_loaded"), 16)
                for b in range(4):
                    act.wait_ge(S("x_turned"), 4 * l + b + 1)
                    copy(x_hi[:, b // 2, 512 * (b % 2):512 * (b % 2) + 512], bank[2 + b][:, :], ACT.Copy
                         ).then_inc(S("x_hi_ready"), 1)

                def silu(e, p, first):
                    act.wait_ge(S("moe_gate_ready"), e + (NE * l + 1))
                    if not first:
                        act.wait_ge(S(f"moe_hid_ready{l}"), e - 1)
                    copy(silm[:, p, :], bank[4 + 2 * p][:, :], ACT.Silu).then_inc(S(f"moe_silu_ready{l}"), 1)

                def high(s):
                    act.wait_ge(S("moe_down_used"), s * 2 + (NE * l + 2))
                    act.wait_ge(S(f"slots_saved{l}"), s + 1)
                    for half in range(2):
                        ins = nc.scalar.activation(o_hi[:, 512 * half:512 * half + 512], bank[4 + half][:, :], ACT.Copy,
                                                   scale=wslot[:, 0:1])
                    ins.then_inc(S(f"o_hi_ready{l}"), 1)

                def silu_pair(s):
                    act.wait_ge(S("moe_up_ready"), s * 2 + (NE * l + 2))
                    copy(sl[:, :], bank[6][:, 0:256], ACT.Silu).then_inc(S(f"moe_silu_ready{l}"), 1)

                def save_slots(s):
                    act.wait_ge(S(f"slots_turned{l}"), s + 1)
                    copy(slotsT[:, :], bank[7][:, 0:T2], ACT.Copy)
                    copy(wslot[:, :], bank[7][:, T2:T2 + 1], ACT.Copy).then_inc(S(f"slots_saved{l}"), 1)

                def save_gathered(s):
                    act.wait_ge(S(f"gathered{l}"), s * 2 + 1)
                    copy(xg[:, 0:4, :], bank[4].rearrange("p (k n) -> p k n", k=4), ACT.Copy
                         ).then_inc(S(f"xg_low_ready{l}"), 1)

                def save_hidden(s):
                    act.wait_ge(S(f"hidden_turned{l}"), s + 1)
                    copy(hs[:, :], bank[6][:, 0:256], ACT.Copy).then_inc(S(f"moe_hid_ready{l}"), 1)

                act.wait_ge(S("load_known"), l + 1)
                with act.If(act.value_load(load_i[0:1, 0:1]) > CAP):
                    act.wait_ge(S(f"combT_psum{l}"), 1)
                    copy(combT[0:NE, :], bank[1][0:NE, 0:T2], ACT.Copy).then_inc(S(f"combT_ready{l}"), 1)
                    silu(0, 0, True)
                    silu(1, 1, True)
                    with act.Fori(1, PAIRS) as i:
                        for p in range(2):
                            silu(i * 2 + p, p, False)
                with act.Else():
                    save_gathered(0)
                    silu_pair(0)
                    save_gathered(1)
                    save_hidden(0)
                    save_slots(0)

                    def step(s):
                        high(s)
                        silu_pair(s + 1)
                        save_gathered(s + 2)
                        save_hidden(s + 1)
                        save_slots(s + 1)

                    with act.Fori(0, PAIRS // 2 - 1) as i:
                        for p in range(2):
                            step(i * 2 + p)
                    high(PAIRS - 2)
                    silu_pair(PAIRS - 1)
                    save_hidden(PAIRS - 1)
                    save_slots(PAIRS - 1)
                    high(PAIRS - 1)
            squares(7)
            for t in range(2):
                for j in range(4):
                    n = 4 * t + j
                    act.wait_ge(S("outT_ready"), n + 1)
                    copy(otok[:, t, 256 * j:256 * j + 256], bank[1 + n % 4][:, 0:256], ACT.Copy).then_inc(S("out_ready"), 1)

        @block.tensor
        def _(pe):
            mm = nc.tensor.matmul

            def token_sum(dst, lhs, tiles, T):
                for j, t in enumerate(tiles):
                    ins = mm(dst, lhs, sq[:, t, 0:T], start=(j == 0), stop=(j == len(tiles) - 1))
                return ins

            def norm(n):
                off, T = span[n]
                pe.wait_ge(S("squares_ready"), 2 * n + 1)
                for t in range(KT):
                    if t == 4:
                        pe.wait_ge(S("squares_ready"), 2 * n + 2)
                    ins = mm(bank[0][:, 0:T], ones, sq[:, t, 0:T], start=(t == 0), stop=(t == KT - 1))
                ins.then_inc(S("sumsq_ready"), 1)

            def ffn(f, at, n):
                for c in range(FC):
                    for j, sig in enumerate(("gate_ready", "up_ready")):
                        q = 2 * c + j
                        pe.wait_ge(S("w_lo_ready"), 3 * FC * f + q + 1)
                        for i in (2 * c, 2 * c + 1):
                            if i >= 4:
                                pe.wait_ge(S("hid_ready"), FT * f + i - 3)
                            ft = i % 2
                            for k in range(KT):
                                if i == 0 and j == 0 and k % 2 == 0:
                                    pe.wait_ge(S("x_lo_ready"), X_LO[f] + k // 2 + 1)
                                ins = split_mm(bank[2 * (i % 4) + j][:, 0:T1], up_part(w_hi, q)[:, k, P * ft:P * ft + P],
                                               up_part(w_lo, q)[:, k, P * ft:P * ft + P], k, k == 0, k == KT - 1)
                            ins.then_inc(S(sig), 1)
                pe.wait_ge(S("hid_ready"), FT * (f + 1))
                for c in range(FC):
                    q = 2 * FC + c
                    pe.wait_ge(S("w_lo_ready"), 3 * FC * f + q + 1)
                    pe.wait_ge(S("hid_lo_ready"), FC * f + c + 1)
                    for h in range(2):
                        for d in range(KT):
                            last = c == FC - 1 and h == 1
                            ins = split_mm(bank[d][:, 0:T1], down_part(w_hi, q)[:, h, P * d:P * d + P],
                                           down_part(w_lo, q)[:, h, P * d:P * d + P], 2 * (c % 4) + h, c == 0 and h == 0, last)
                            if last:
                                ins.then_inc(S("y_ready"), 1)
                    if c < FC - 1:
                        ins.then_inc(S("down_used"), 1)

            def split_mm(dst, hi, lo, k, first, last):
                mm(dst, hi, r_hi[:, k, :], start=first, stop=False)
                mm(dst, hi, r_lo[:, k, :], start=False, stop=False)
                return mm(dst, lo, r_hi[:, k, :], start=False, stop=last)

            def down(at, chunks, rhs, T, ready):
                for name, v in ready:
                    pe.wait_ge(S(name), v)
                for c in range(chunks):
                    loaded(pe, at + c)
                    w = down_view(at + c)
                    for f in range(2):
                        for d in range(KT):
                            first, last = c == 0 and f == 0, c == chunks - 1 and f == 1
                            ins = mm(bank[d][:, 0:T], w[:, f, P * d:P * d + P], rhs[:, 2 * c + f, 0:T],
                                     start=first, stop=last)
                            if last:
                                ins.then_inc(S("y_ready"), 1)
                    if c < chunks - 1:
                        ins.then_inc(S("down_used"), 1)

            def bank_free(u, base):
                held = u - base - 8
                if held >= 0 and base < U1:
                    pe.wait_ge(S("proj_saved"), held + 1)
                elif 0 <= held < 3:
                    pe.wait_ge(S("proj_saved"), U1 + SAVED2 * ((base - U1) // U2) + held + 1)
                elif held == 3:
                    pe.wait_ge(S("rotary_read"), 2 * ((base - U1) // U2) + 1)

            def feature_unit(u, base, at, c0, T, n=None):
                bank_free(u, base)
                w = up_view(at)
                loaded(pe, at)
                for k in range(KT):
                    if n is not None:
                        pe.wait_ge(S("xn_ready"), KT * n + k + 1)
                    ins = mm(bank[u % 8][:, 0:T], w[:, k, c0:c0 + P], xn[:, k, 0:T], start=(k == 0), stop=(k == KT - 1))
                ins.then_inc(S("proj_ready"), 1)

            def scores(g):
                u = units_all[g]
                if g >= 2:
                    pe.wait_ge(S("scores_taken"), g - 1)
                for m in range(u["maps"]):
                    parts = u["score"][m]
                    for j, (lhs, rhs) in enumerate(parts):
                        ins = mm(bank[2 * (g % 2) + m][0:u["nq"], 0:u["L"]], lhs, rhs,
                                 start=(j == 0), stop=(j == len(parts) - 1))
                ins.then_inc(S("scores_ready"), 1)

            def turn(g):
                u = units_all[g]
                pe.wait_ge(S("probs_ready"), g + 1)
                if g >= 2:
                    pe.wait_ge(S("aT_saved"), g - 1)
                nq = u["nq"]
                for k, nk in key_tiles(u):
                    ins = nc.tensor.transpose(bank[4 + g % 2][0:nk, nq * k:nq * k + nq],
                                              a_sb[0:nq, g % 2, P * k:P * k + nk], ident[0:nq, 0:nq])
                ins.then_inc(S("aT_ready"), 1)

            def pv(g):
                u = units_all[g]
                pe.wait_ge(S("aT_saved"), g + 1)
                if g >= 2:
                    pe.wait_ge(S("o_saved"), g - 1)
                nq, b, M = u["nq"], u["base"], u["M"]
                kts = key_tiles(u)
                for c, v in enumerate(u["v"]):
                    for k, nk in kts:
                        ins = mm(bank[6 + g % 2][b:b + M, nq * c:nq * c + nq], v(k, nk), aT[0:nk, g % 2, nq * k:nq * k + nq],
                                 start=(k == 0), stop=(k == len(kts) - 1))
                ins.then_inc(S("o_ready"), 1)

            pe.wait_ge(S("consts_loaded"), 16)
            pe.wait_ge(S("x_loaded"), 32)
            for d in range(KT):
                for t, (q0, nq) in enumerate(BLOCKS1):
                    ins = nc.tensor.transpose(bank[d][:, q0:q0 + nq], xtok[0:nq, t, P * d:P * d + P], ident[0:nq, 0:nq])
                ins.then_inc(S("xT_ready"), 1)
            pe.wait_ge(S("input_saved"), 8)
            pe.wait_ge(S("rb_loaded"), 32)
            mm(bank[7][0:8, :], rb[:, :], bcst[:, C_OH:C_OH + ROW], start=True, stop=True).then_inc(S("bias_psum"), 1)
            norm(0)
            pe.wait_ge(S("bias_rows_ready"), 1)
            ffn(0, A_FFN1, 0)
            norm(1)

            u = 0
            for t in range(8):
                feature_unit(u, 0, A_IN1 + t // 2, P * (t % 2), T1, n=1 if t == 0 else None)
                u += 1
            for c in range(2):
                at_ = A_IN1 + 4 + c
                for t, (q0, nq) in enumerate(BLOCKS1):
                    bank_free(u, 0)
                    loaded(pe, at_)
                    for k in range(KT):
                        ins = mm(bank[u % 8][0:nq, 0:256], xn[:, k, q0:q0 + nq], up_view(at_)[:, k, :],
                                 start=(k == 0), stop=(k == KT - 1))
                    ins.then_inc(S("proj_ready"), 1)
                    u += 1
            for t in range(10):
                feature_unit(u, 0, A_IN1 + 6 + t // 2, P * (t % 2), T1)
                u += 1
            w = up_view(A_IN1 + 11)
            loaded(pe, A_IN1 + 11)
            bank_free(u, 0)
            for half in range(2):
                for k in range(KT):
                    ins = mm(bank[u % 8][64 * half:64 * half + 64, 0:T1], w[:, k, 0:64], xn[:, k, :],
                             start=(k == 0), stop=(k == KT - 1))
            ins.then_inc(S("proj_ready"), 1)
            u += 1
            bank_free(u, 0)
            for t, (q0, nq) in enumerate(BLOCKS1):
                for k in range(KT):
                    ins = mm(bank[u % 8][0:nq, 8 * t:8 * t + 8], xn[:, k, q0:q0 + nq], w[:, k, 64:72],
                             start=(k == 0), stop=(k == KT - 1))
            ins.then_inc(S("proj_ready"), 1)
            pe.wait_ge(S("proj_saved"), U1)
            for t in range(8):
                mm(bank[t][:, 0:T1], bd64, sq[:, t, :], start=True, stop=True).then_inc(S("norm1_psum"), 1)
            pe.wait_ge(S("norm1_done"), 1)
            token_sum(bank[0][:, 0:T1], ones, (8, 9), T1).then_inc(S("normc_psum"), 1)
            pe.wait_ge(S("wuk_loaded"), 16)
            pe.wait_ge(S("normc_done"), 2)
            pe.wait_ge(S("norm1_done"), 8)
            for t in range(8):
                mm(bank[t][:, 0:T1], w_uk[:, t // 2, P * (t % 2):P * (t % 2) + P], uT[:, 8 + t // 2, :],
                   start=True, stop=True).then_inc(S("qlat_ready"), 1)
            pe.wait_ge(S("qlat_saved"), 8)
            for h in range(BH):
                token_sum(bank[h][:, 0:T1], ones, (2 * h, 2 * h + 1), T1).then_inc(S("normq_psum"), 1)
            for t, (q0, nq) in enumerate(BLOCKS1):
                for c in range(2):
                    ins = nc.tensor.transpose(bank[4 + t][0:nq, P * c:P * c + P], uT[:, 12 + c, q0:q0 + nq], ident)
                ins.then_inc(S("ctok_ready"), 1)
            pe.wait_ge(S("normq_done"), 8)
            for i in range(3):
                q0, nq, L = qcols(i)
                for h in range(IH):
                    n, b = IH * i + h, 64 * (h % 2)
                    if n >= 4:
                        pe.wait_ge(S("relu_ready"), n - 3)
                    mm(bank[n % 4][0:nq, 0:L], uT[b:b + 64, 14 + h // 2, q0:q0 + nq], ikT[b:b + 64, 0:L],
                       start=True, stop=True).then_inc(S("dots_ready"), 1)
            pe.wait_ge(S("relu_ready"), 24)
            pe.wait_ge(S("ctok_saved"), 3)
            steps(SEG_A, scores, turn, pv)
            pe.wait_ge(S("o_saved"), SEG_A[1])
            for h in range(AH):
                mm(bank[h][:, 0:T1], ones, sq[:, h, :], start=True, stop=True).then_inc(S("subln_psum"), 1)
            pe.wait_ge(S("subln_done"), AH)
            steps(SEG_B, scores, turn, pv)
            pe.wait_ge(S("o_saved"), SEG_B[1])
            pe.wait_ge(S("wuv_loaded"), 16)
            for h in range(BH):
                for c in range(2):
                    ins = mm(bank[h][:, 0:T1], w_uv[:, h, c, :], olT[:, 2 * h + c, :], start=(c == 0), stop=(c == 1))
                ins.then_inc(S("ob_ready"), 1)
            down(A_OUT1, 4, mixT, T1, [("ob_saved", BH), ("subln_done", AH)])
            norm(2)
            ffn(1, A_FFN2, 2)

            for l in range(LAYERS):
                n1 = 3 + 2 * l
                norm(n1)
                base = U1 + U2 * l
                u = base
                a = A_IN2[l]
                pe.wait_ge(S("xn_ready"), KT * n1 + 1)
                feature_unit(u, base, a, 0, T2, n=n1)
                feature_unit(u + 1, base, a, P, T2)
                feature_unit(u + 2, base, a + 1, 0, T2)
                pe.wait_ge(S("swapped_ready"), l + 1)
                for j in range(2):
                    bank_free(u + 3 + j, base)
                    for k in range(KT):
                        lhs = wkrs[:, k, :] if j else up_view(a + 1)[:, k, P:P + 32]
                        ins = mm(bank[(u + 3 + j) % 8][64:96, 0:T2], lhs, xn[:, k, 0:T2], start=(k == 0), stop=(k == KT - 1))
                    ins.then_inc(S("proj_ready"), 1)
                u += 5
                for t in range(4):
                    feature_unit(u, base, a + 2 + t // 2, P * (t % 2), T2)
                    u += 1
                bank_free(u, base)
                loaded(pe, a + 4)
                for t in range(2):
                    for k in range(KT):
                        ins = mm(bank[u % 8][:, T2 * t:T2 * t + T2], xn[:, k, P * t:P * t + P], up_view(a + 4)[:, k, :],
                                 start=(k == 0), stop=(k == KT - 1))
                ins.then_inc(S("proj_ready"), 1)
                u += 1
                for t in range(2):
                    feature_unit(u, base, a + 5, P * t, T2)
                    u += 1
                pe.wait_ge(S("proj_saved"), U1 + SAVED2 * (l + 1))
                pe.wait_ge(S("rotary_read"), 2 * (l + 1))
                token_sum(bank[0][:, 0:T2], ones, (0, 1), T2).then_inc(S("norm_lat_psum"), 1)
                mm(bank[1][:, 0:T2], ones, sq[:, 2, 0:T2], start=True, stop=True).then_inc(S("norm_lat_psum"), 1)
                pe.wait_ge(S("lat_ready"), 3 * (l + 1))
                for n in range(4):
                    if n >= 2:
                        pe.wait_ge(S("q_nope_saved"), 4 * l + n - 1)
                        pe.wait_ge(S("q_rope_saved"), 4 * l + n - 1)
                    b0, b1 = bank[2 * (n % 2)], bank[2 * (n % 2) + 1]
                    for j in range(2):
                        h = 2 * n + j
                        for k in range(2):
                            mm(b0[0:96, T2 * j:T2 * j + T2], w_uq[:, k, 96 * h:96 * h + 96], cq[:, k, :],
                               start=(k == 0), stop=(k == 1))
                        for k in range(2):
                            ins = mm(b1[64:96, T2 * j:T2 * j + T2], wuqs[:, k, h, :], cq[:, k, :],
                                     start=(k == 0), stop=(k == 1))
                    ins.then_inc(S("q_up_ready"), 1)
                for n in range(4):
                    if n >= 2:
                        pe.wait_ge(S("k_nope_saved"), 4 * l + n - 1)
                    for j in range(2):
                        ins = mm(bank[4 + n % 2][0:64, T2 * j:T2 * j + T2], w_ukv[:, 2 * n + j, 0:64], ckv[:, 0, :],
                                 start=True, stop=True)
                    ins.then_inc(S("k_up_ready"), 1)
                for t in range(2):
                    mm(bank[6 + t][:, :], ckv[:, 0, P * t:P * t + P], w_ukv[:, :, 64:128],
                       start=True, stop=True).then_inc(S("v_up_ready"), 1)
                pe.wait_ge(S("q_nope_saved"), 4 * (l + 1))
                pe.wait_ge(S("q_rope_saved"), 4 * (l + 1))
                pe.wait_ge(S("k_nope_saved"), 4 * (l + 1))
                pe.wait_ge(S("k_rope_saved"), l + 1)
                pe.wait_ge(S("vm_saved"), 2 * (l + 1))
                steps(SEG_M[l], scores, turn, pv)
                pe.wait_ge(S("o_saved"), SEG_M[l][1])
                for h in range(SH):
                    b, t = 64 * (h % 2), h // 2
                    mm(bank[h][:, 0:T2], kbT[b:b + 64, t, 0:P], qbT[b:b + 64, t, :], start=True, stop=True)
                    mm(bank[h][:, T2:384], kbT[b:b + 64, t, P:T2], qbT[b:b + 64, t, P:T2],
                       start=True, stop=True).then_inc(S("z_ready"), 1)
                for h in range(SH):
                    pe.wait_ge(S("softplus_ready"), SH * l + h + 1)
                    mm(bank[h][:, T2:384], upper, ln[:, h, T2:384], start=True, stop=True)
                    mm(bank[h][:, 0:T2], upper, ln[:, h, 0:T2], start=True, stop=True)
                    mm(bank[h][:, P:T2], ones, ln[:, h, T2:384], start=False, stop=True,
                       skip_group_check=True).then_inc(S("later_ready"), 1)
                for h in range(SH):
                    b = 64 * (h % 2)
                    pe.wait_ge(S("stick_ready"), SH * l + h + 1)
                    mm(bank[4 + h][b:b + 64, 0:T2], vb[:, 0, 64 * h:64 * h + 64], ln[:, h, 0:T2], start=True, stop=True)
                    mm(bank[4 + h][b:b + 64, P:T2], vb[:, 1, 64 * h:64 * h + 64], ln[:, h, T2:384], start=False, stop=True,
                       skip_group_check=True).then_inc(S("stick_o_ready"), 1)
                pe.wait_ge(S("pool_d_ready"), l + 1)
                for t in range(2):
                    ins = mm(bank[0][:, T2 * t:T2 * t + T2], w_pool[:, t, :], pd[:, t, :], start=True, stop=True)
                ins.then_inc(S("pool_y_ready"), 1)
                down(A_OUT2[l], 4, mixT, T2, [("stick_saved", SH * (l + 1)), ("pool_saved", 2 * (l + 1))])
                n2 = 4 + 2 * l
                norm(n2)
                pe.wait_ge(S("xn_ready"), KT * (n2 + 1))
                for t in range(2):
                    for k in range(KT):
                        ins = mm(bank[0][:, 36 * t:36 * t + 36], xn[:, k, P * t:P * t + P], w_rt[:, k, :],
                                 start=(k == 0), stop=(k == KT - 1))
                ins.then_inc(S("router_ready"), 1)
                for b in range(4):
                    for k in range(4):
                        f = 4 * (b % 2) + k
                        ins = nc.tensor.transpose(bank[2 + b][:, P * k:P * k + P],
                                                  xn[:, f, P * (b // 2):P * (b // 2) + P], ident)
                    ins.then_inc(S("x_turned"), 1)
                pe.wait_ge(S("sel_ready"), l + 1)
                before = cst[:, C_BE:C_BE + P]
                mm(bank[1][:, 0:NE], before, sel[:, 0, :], start=True, stop=True)
                mm(bank[1][:, NE:2 * NE], before, sel[:, 1, :], start=True, stop=False)
                mm(bank[1][:, NE:2 * NE], ones, sel[:, 0, :], start=False, stop=True)
                mm(bank[1][:, 2 * NE:3 * NE], ones, sel[:, 0, :], start=True, stop=False)
                mm(bank[1][:, 2 * NE:3 * NE], ones, sel[:, 1, :], start=False, stop=True).then_inc(S("places_psum"), 1)
                pe.wait_ge(S("comb_ready"), l + 1)
                pe.wait_ge(S("x_lo_ready"), 4 * (l + 3))
                pe.wait_ge(S("load_known"), l + 1)
                pe.wait_ge(S("zeros_ready"), 1)

                def zero_sum():
                    for b in range(4):
                        mm(bank[b][:, :], zb[:, 0:P], zb[:, :], start=True, stop=True)

                at_ = MOE_AT[l]

                def chunk_loaded(n, lap):
                    pe.wait_ge(slot_sem(n), lap * 16 + 16 * loads_of[n])

                def gate_up(e, q, lap, first=False):
                    p = q % 2
                    for j, sig in enumerate(("moe_gate_ready", "moe_up_ready")):
                        n = at_ + 6 * (q // 2) + 2 * j + p
                        chunk_loaded(n, lap)
                        if not first and j == 0:
                            pe.wait_ge(S(f"moe_hid_ready{l}"), e - 1)
                        for f in range(2):
                            for k in range(KT):
                                ins = mm(bank[4 + 2 * p + j][:, T2 * f:T2 * f + T2], up_view(n)[:, k, P * f:P * f + P],
                                         xn[:, k, 0:T2], start=(k == 0), stop=(k == KT - 1))
                        ins.then_inc(S(sig), 1)

                def expert_down(e, q, lap):
                    p = q % 2
                    n = at_ + 6 * (q // 2) + 4 + p
                    chunk_loaded(n, lap)
                    pe.wait_ge(S(f"moe_hid_ready{l}"), e + 1)
                    for f in range(2):
                        for d in range(KT):
                            ins = mm(bank[d // 2][:, T2 * (d % 2):T2 * (d % 2) + T2], down_view(n)[:, f, P * d:P * d + P],
                                     hm[:, p, T2 * f:T2 * f + T2], start=False, stop=True, skip_group_check=True)
                    ins.then_inc(S("moe_down_used"), 1)

                def gather(s, p, first=False):
                    pe.wait_ge(S(f"slots_ready{l}"), s + 1)
                    if not first:
                        pe.wait_ge(S(f"o_lo_ready{l}"), s - 1)
                    for half in range(2):
                        for kk in range(4):
                            k = 4 * half + kk
                            for j, x in enumerate((x_hi, x_lo)):
                                for t in range(2):
                                    ins = mm(bank[4 + half][:, P * kk:P * kk + P], x[:, t, P * k:P * k + P],
                                             slots[:, p, t, :], start=(j == 0 and t == 0), stop=(j == 1 and t == 1))
                        ins.then_inc(S(f"gathered{l}"), 1)

                def gate_up_pair(s, p, lap, first=False):
                    pe.wait_ge(S(f"xg_low_ready{l}"), s + 1)
                    pe.wait_ge(S(f"xg_high_ready{l}"), s + 1)
                    if not first:
                        pe.wait_ge(S(f"moe_hid_ready{l}"), s)
                    for j, sig in enumerate(("moe_gate_ready", "moe_up_ready")):
                        for e in range(2):
                            chunk_loaded(at_ + 6 * p + 2 * j + e, lap)
                        for k in range(KT):
                            for e in range(2):
                                ins = mm(bank[6][64 * e:64 * e + 64, 256 * j:256 * j + 256],
                                         xg[:, k, CAP * e:CAP * e + CAP], up_view(at_ + 6 * p + 2 * j + e)[:, k, :],
                                         start=(k == 0), stop=(k == KT - 1))
                                if k == KT - 1:
                                    ins.then_inc(S(sig), 1)

                def turn_hidden(s):
                    pe.wait_ge(S(f"moe_product{l}"), s + 1)
                    for f in range(2):
                        ins = nc.tensor.transpose(bank[6][:, P * f:P * f + P], hp[:, P * f:P * f + P], ident)
                    ins.then_inc(S(f"hidden_turned{l}"), 1)

                def turn_slots(s, p, first=False):
                    pe.wait_ge(S(f"slotw_ready{l}"), s + 1)
                    if not first:
                        pe.wait_ge(S(f"slots_saved{l}"), s)
                    for t in range(2):
                        nc.tensor.transpose(bank[7][:, P * t:P * t + P], slots[:, p, t, :].bitcast(F32), ident)
                    for t in range(2):
                        ins = mm(bank[7][:, T2:T2 + 2], slotw[:, t, :], ones[:, 0:2], start=(t == 0), stop=(t == 1))
                    ins.then_inc(S(f"slots_turned{l}"), 1)

                def down_pair(s, p, lap, last=False):
                    pe.wait_ge(S(f"moe_hid_ready{l}"), s + 1)
                    pe.wait_ge(S(f"xg_low_ready{l}"), s + (1 if last else 2))
                    pe.wait_ge(S(f"xg_high_ready{l}"), s + (1 if last else 2))
                    for e in range(2):
                        chunk_loaded(at_ + 6 * p + 4 + e, lap)
                    for half in range(2):
                        for f in range(2):
                            for e in range(2):
                                c = P * f + CAP * e
                                ins = mm(bank[4 + half][64 * e:64 * e + 64, :], hs[:, c:c + CAP],
                                         down_view(at_ + 6 * p + 4 + e)[:, f, 512 * half:512 * half + 512],
                                         start=(f == 0), stop=(f == 1))
                                if half == 1 and f == 1:
                                    ins.then_inc(S("moe_down_used"), 1)

                def scatter(s):
                    pe.wait_ge(S(f"o_hi_ready{l}"), s + 1)
                    pe.wait_ge(S(f"o_lo_ready{l}"), s + 1)
                    pe.wait_ge(S(f"slots_saved{l}"), s + 1)
                    for d in range(KT):
                        for o in (o_hi, o_lo):
                            ins = mm(bank[d // 2][:, T2 * (d % 2):T2 * (d % 2) + T2], o[:, P * d:P * d + P],
                                     slotsT[:, :], start=False, stop=True, skip_group_check=True)
                    return ins

                with pe.If(pe.value_load(load_i[0:1, 0:1]) > CAP):
                    for t in range(2):
                        ins = nc.tensor.transpose(bank[1][0:NE, P * t:P * t + P], comb[:, t, :], ident)
                    ins.then_inc(S(f"combT_psum{l}"), 1)
                    pe.wait_ge(S(f"combT_ready{l}"), 1)
                    zero_sum()
                    gate_up(0, 0, 0, first=True)
                    for e in range(4):
                        gate_up(e + 1, (e + 1) % 4, (e + 1) // 4, first=e == 0)
                        expert_down(e, e, 0)
                    with pe.Fori(1, NE // 4 - 1) as i:
                        for q in range(4):
                            gate_up(i * 4 + (q + 1), (q + 1) % 4, i + (q + 1) // 4)
                            expert_down(i * 4 + q, q, i)
                    for e in range(NE - 4, NE):
                        if e < NE - 1:
                            gate_up(e + 1, (e + 1) % 4, NE // 4 - 1)
                        expert_down(e, e % 4, NE // 4 - 1)
                with pe.Else():
                    zero_sum()
                    gather(0, 0, True)
                    gate_up_pair(0, 0, 0, True)
                    gather(1, 1, True)
                    turn_hidden(0)
                    turn_slots(0, 0, True)
                    with pe.Fori(0, PAIRS // 2 - 1) as i:
                        for p in range(2):
                            s = i * 2 + p
                            down_pair(s, p, i)
                            gate_up_pair(s + 1, 1 - p, i + p)
                            scatter(s)
                            gather(s + 2, p)
                            turn_hidden(s + 1)
                            turn_slots(s + 1, 1 - p)
                    down_pair(PAIRS - 2, 0, PAIRS // 2 - 1)
                    gate_up_pair(PAIRS - 1, 1, PAIRS // 2 - 1)
                    scatter(PAIRS - 2)
                    turn_hidden(PAIRS - 1)
                    turn_slots(PAIRS - 1, 1)
                    down_pair(PAIRS - 1, 1, PAIRS // 2 - 1, last=True)
                    scatter(PAIRS - 1)
                mm(bank[4][:, :], zb[:, 0:P], zb[:, :], start=True, stop=True).then_inc(S("experts_done"), 1)
            norm(7)
            pe.wait_ge(S("xn_ready"), 64)
            for t in range(2):
                for j in range(4):
                    n = 4 * t + j
                    if n >= 4:
                        pe.wait_ge(S("out_ready"), n - 3)
                    for c in range(2):
                        ins = nc.tensor.transpose(bank[1 + n % 4][:, P * c:P * c + P], xn[:, 2 * j + c, P * t:P * t + P], ident)
                    ins.then_inc(S("outT_ready"), 1)

        @block.vector
        def _(dve):
            n_chain = 0
            V = nc.vector

            def link(ins):
                nonlocal n_chain
                n_chain += 1
                ins.then_inc(S("dve_chain"), 1)
                dve.wait_ge(S("dve_chain"), n_chain)

            n_root = 0

            def inv_rms(dst, T=T1):
                nonlocal n_root
                dve.wait_ge(S("root_ready"), n_root + 1)
                V.reciprocal(dst, root[:, n_root % 2, 0:T]).then_inc(S("root_used"), 1)
                n_root += 1
                dve.wait_ge(S("root_used"), n_root)

            def norm(n):
                off, T = span[n]
                if n in (0, 2):
                    split_w(n // 2, 0)
                inv_rms(rstd[:, 0, 0:T], T)
                for k in range(KT):
                    V.scalar_tensor_tensor(xn[:, k, 0:T], hT[:, k, off:off + T], gain(G_NORM + KT * n + k), rstd[:, 0, 0:T],
                                           ALU.mult, ALU.mult).then_inc(S("xn_ready"), 1)

            def split_w(f, q):
                dve.wait_ge(S("w_hi_ready"), 3 * FC * f + q + 1)
                part_free(dve, f, q)
                V.tensor_tensor(w_lo[:, q % 2, :], chunk((A_FFN1, A_FFN2)[f] + q), w_hi[:, q % 2, :].bitcast(F32),
                                ALU.subtract).then_inc(S("w_lo_ready"), 1)

            def split_x(f):
                for j in range(4):
                    dve.wait_ge(S("x_hi_ready"), X_LO[f] + j + 1)
                    t = slice(2 * j, 2 * j + 2)
                    V.tensor_tensor(r_lo[:, t, :], xn[:, t, :], r_hi[:, t, :].bitcast(F32), ALU.subtract
                                    ).then_inc(S("x_lo_ready"), 1)

            def split_hid(f, c):
                dve.wait_ge(S("hid_hi_ready"), FC * f + c + 1)
                if c >= 4:
                    dve.wait_ge(S("down_used"), used_at[f] + c - 3)
                j = 2 * (c % 4)
                V.tensor_tensor(r_lo[:, j:j + 2, :], hid(2 * c, 2), r_hi[:, j:j + 2, :].bitcast(F32), ALU.subtract
                                ).then_inc(S("hid_lo_ready"), 1)

            def ffn(f):
                split_x(f)
                split_w(f, 1)
                for c in range(FC):
                    split_w(f, 2 * c + 2)
                    for i in (2 * c, 2 * c + 1):
                        g = FT * f + i
                        dve.wait_ge(S("silu_ready"), g + 1)
                        dve.wait_ge(S("up_ready"), g + 1)
                        V.tensor_tensor(hid(i)[:, 0, :], sil[:, i % 2, :], bank[2 * (i % 4) + 1][:, 0:T1], ALU.mult
                                        ).then_inc(S("hid_ready"), 1)
                    if c == FC - 1:
                        split_hid(f, 0)
                    split_w(f, 2 * c + 3)
                split_hid(f, 1)
                for c in range(FC - 2):
                    split_w(f, 2 * FC + c + 2)
                    split_hid(f, c + 2)

            def residual(k, r, factor):
                off, T = span[r]
                for d in range(KT):
                    dve.wait_ge(S("y_ready"), 8 * k + d + 1)
                    h = hT[:, d, 0 if T == T1 else off:T1]
                    V.scalar_tensor_tensor(h, bank[d][:, 0:T], factor, h, ALU.mult, ALU.add
                                           ).then_inc(S("residual_ready"), 1)

            def maxes(g):
                u = units_all[g]
                dve.wait_ge(S("scores_ready"), g + 1)
                nq, L = u["nq"], u["L"]
                bias = u["bias"]
                if u["kind"] == "b":
                    dve.wait_ge(S("bias_ready"), g - SEG_B[0] + 1)
                    bias = gb[0:nq, g % 2, 0:L]
                for m in range(u["maps"]):
                    ins = V.tensor_tensor_reduce(s_sb[0:nq, g % 2, m, 0:L], bank[2 * (g % 2) + m][0:nq, 0:L], bias,
                                                 1.0, -3.4e38, ALU.add, ALU.max, mx[0:nq, g % 2, m:m + 1])
                    if m < u["maps"] - 1:
                        link(ins)
                ins.then_inc(S("scores_taken"), 1)
                dve.wait_ge(S("scores_taken"), g + 1)
                V.tensor_scalar(nmx[0:nq, g % 2, 0:u["maps"]], mx[0:nq, g % 2, 0:u["maps"]], -1.0, None, ALU.mult
                                ).then_inc(S("max_ready"), 1)

            def weights(g):
                u = units_all[g]
                dve.wait_ge(S("exps_ready"), g + 1)
                nq, L = u["nq"], u["L"]
                if g >= 2:
                    dve.wait_ge(S("aT_ready"), g - 1)
                r = rs[0:nq, g % 2, 0:u["maps"]]
                link(V.reciprocal(r, sums[0:nq, g % 2, 0:u["maps"]]))
                a = a_sb[0:nq, g % 2, 0:L]
                if u["kind"] == "a":
                    link(V.tensor_scalar(rs[0:nq, g % 2, 1:2], rs[0:nq, g % 2, 1:2], lamb[0:nq, 4:5], None, ALU.mult))
                    link(V.tensor_scalar(a, s_sb[0:nq, g % 2, 0, 0:L], rs[0:nq, g % 2, 0:1], None, ALU.mult))
                    ins = V.scalar_tensor_tensor(a, s_sb[0:nq, g % 2, 1, 0:L], rs[0:nq, g % 2, 1:2], a, ALU.mult, ALU.add)
                else:
                    ins = V.tensor_scalar(a, s_sb[0:nq, g % 2, 0, 0:L], rs[0:nq, g % 2, 0:1], None, ALU.mult)
                ins.then_inc(S("probs_ready"), 1)
                dve.wait_ge(S("probs_ready"), g + 1)

            dve.wait_ge(S("gains_loaded"), 16)
            link(V.tensor_scalar(gn[:, 0:64], gn[:, 0:64], math.sqrt(D), None, ALU.mult))
            link(V.tensor_scalar(gn[:, G_AK:G_AK + 1], gn[:, G_AK:G_AK + 1], math.sqrt(ADK), None, ALU.mult))
            link(V.tensor_scalar(gn[:, G_AQ:G_AQ + 1], gn[:, G_AQ:G_AQ + 1], math.sqrt(ADK) * ADK ** -0.5, None, ALU.mult))
            link(V.tensor_scalar(gn[:, G_BKV:G_BKV + 2], gn[:, G_BKV:G_BKV + 2], math.sqrt(BDC), None, ALU.mult))
            link(V.tensor_scalar(gn[:, G_BQ:G_BQ + 2], gn[:, G_BQ:G_BQ + 2], math.sqrt(BDC) * BDC ** -0.5, None, ALU.mult))
            link(V.tensor_scalar(gn[:, G_SUB:G_SUB + 1], gn[:, G_SUB:G_SUB + 1], math.sqrt(ADV) * (1.0 - LAM0), None, ALU.mult))
            link(V.tensor_scalar(gn[:, G_QN:G_QN + 4], gn[:, G_QN:G_QN + 4], math.sqrt(256), None, ALU.mult))
            link(V.tensor_scalar(gn[:, G_KVN:G_KVN + 2], gn[:, G_KVN:G_KVN + 2], math.sqrt(128), None, ALU.mult))
            for j in range(2):
                a, b = G_LAM + 2 * j * ADK, G_LAM + (2 * j + 1) * ADK
                ins = V.tensor_tensor_reduce(lprod[:], gn[:, a:a + ADK], gn[:, b:b + ADK], 1.0, 0.0,
                                             ALU.mult, ALU.add, lamb[:, j:j + 1])
                if j == 0:
                    link(ins)
            ins.then_inc(S("lam_sums_ready"), 1)
            dve.wait_ge(S("lam_exp_ready"), 1)
            link(V.scalar_tensor_tensor(lamb[:, 4:5], lamb[:, 3:4], -LAM0, lamb[:, 2:3], ALU.add, ALU.subtract))
            dve.wait_ge(S("input_saved"), 8)
            dve.wait_ge(S("bias_psum"), 1)
            dve.wait_ge(S("rb_loaded"), 32)
            V.tensor_tensor(btab[:, :], bank[7][0:8, :], bcst[0:8, C_OM:C_OM + ROW], ALU.add).then_inc(S("bias_rows_ready"), 1)
            norm(0)
            ffn(0)
            residual(0, 0, 0.5)
            norm(1)
            for t in range(8):
                inv_rms(rstd[:, t % 2, :])
                V.scalar_tensor_tensor(uT[:, t, :], uT[:, t, :], gain(G_AQ if t < 4 else G_AK), rstd[:, t % 2, :],
                                       ALU.mult, ALU.mult).then_inc(S("norm1_done"), 1)
            dve.wait_ge(S("norm1_done"), 8)
            inv_rms(rstd[:, 0, :])
            for t in range(2):
                V.scalar_tensor_tensor(uT[:, 12 + t, :], uT[:, 12 + t, :], gain(G_BKV + t), rstd[:, 0, :],
                                       ALU.mult, ALU.mult).then_inc(S("normc_done"), 1)
            for h in range(BH):
                inv_rms(rstd[:, (h + 1) % 2, :])
                for t in range(2):
                    V.scalar_tensor_tensor(qlT[:, 2 * h + t, :], qlT[:, 2 * h + t, :], gain(G_BQ + t),
                                           rstd[:, (h + 1) % 2, :], ALU.mult, ALU.mult).then_inc(S("normq_done"), 1)
            dve.wait_ge(S("normq_done"), 8)
            for i in range(3):
                q0, nq, L = qcols(i)
                s = score[0:nq, 0:L]
                for h in range(IH):
                    n = IH * i + h
                    dve.wait_ge(S("relu_ready"), n + 1)
                    prev = cst[0:nq, C_CM + P * (2 - i):C_CM + P * (2 - i) + L] if h == 0 else s
                    V.scalar_tensor_tensor(s, rel[0:nq, n % 4, 0:L], iw[0:nq, i, h:h + 1], prev, ALU.mult, ALU.add
                                           ).then_inc(S("score_added"), 1)
                    dve.wait_ge(S("score_added"), n + 1)
                for r in range(TOPK // 8):
                    link(V.max(top8[0:nq, :], s))
                    link(V.match_replace(s, top8[0:nq, :], s, TAKEN))
                V.tensor_scalar(selb[0:nq, i, 0:L], s, 0.5 * TAKEN, NEG, ALU.is_gt, ALU.mult).then_inc(S("selected"), 1)
                dve.wait_ge(S("selected"), i + 1)
            dve.wait_ge(S("G_loaded"), 16 * 8)
            steps(SEG_A, maxes, weights)
            for h in range(AH):
                inv_rms(rstd[:, h % 2, :])
                V.scalar_tensor_tensor(mixT[:, h, :], mixT[:, h, :], gain(G_SUB), rstd[:, h % 2, :],
                                       ALU.mult, ALU.mult).then_inc(S("subln_done"), 1)
            steps(SEG_B, maxes, weights)
            residual(1, 1, 1.0)
            norm(2)
            ffn(1)
            residual(2, 2, 0.5)

            for l in range(LAYERS):
                norm(3 + 2 * l)
                base = U1 + U2 * l
                ck, sk = (cst[64:96, C_COS + j * T2:C_COS + (j + 1) * T2] for j in (2, 3))
                dve.wait_ge(S("proj_ready"), base + 5)
                V.tensor_tensor(rt1[64:96, 0, :], bank[(base + 3) % 8][64:96, 0:T2], ck, ALU.mult).then_inc(S("rotary_read"), 1)
                V.tensor_tensor(rt2[64:96, 0, :], bank[(base + 4) % 8][64:96, 0:T2], sk, ALU.mult).then_inc(S("rotary_read"), 1)
                dve.wait_ge(S("rotary_read"), 2 * (l + 1))
                V.tensor_tensor(kcat[64:96, :, :], spread(rt1[64:96, 0:1, :], 1, MH), spread(rt2[64:96, 0:1, :], 1, MH),
                                ALU.add).then_inc(S("k_rope_saved"), 1)
                dve.wait_ge(S("k_rope_saved"), l + 1)
                inv_rms(rstd[:, 0, 0:T2], T2)
                for t in range(2):
                    V.scalar_tensor_tensor(cq[:, t, :], cq[:, t, :], gain(G_QN + 2 * l + t), rstd[:, 0, 0:T2],
                                           ALU.mult, ALU.mult).then_inc(S("lat_ready"), 1)
                inv_rms(rstd[:, 1, 0:T2], T2)
                V.scalar_tensor_tensor(ckv[:, 0, :], ckv[:, 0, :], gain(G_KVN + l), rstd[:, 1, 0:T2],
                                       ALU.mult, ALU.mult).then_inc(S("lat_ready"), 1)
                cqt, sqt = (spread(cst[64:96, C_COS + j * T2:C_COS + (j + 1) * T2].rearrange("p (a n) -> p a n", a=1), 1, 2)
                            for j in (0, 1))
                for n in range(4):
                    dve.wait_ge(S("q_up_ready"), 4 * l + n + 1)
                    b0 = bank[2 * (n % 2)][64:96, :].rearrange("p (h n) -> p h n", h=2)
                    b1 = bank[2 * (n % 2) + 1][64:96, :].rearrange("p (h n) -> p h n", h=2)
                    link(V.tensor_tensor(rt1[64:96, :, :], b0, cqt, ALU.mult))
                    link(V.tensor_tensor(rt2[64:96, :, :], b1, sqt, ALU.mult))
                    V.tensor_tensor(qcat[64:96, 2 * n:2 * n + 2, :], rt1[64:96, :, :], rt2[64:96, :, :], ALU.add
                                    ).then_inc(S("q_rope_saved"), 1)
                    dve.wait_ge(S("q_rope_saved"), 4 * l + n + 1)
                steps(SEG_M[l], maxes, weights)
                nm = cst[:, C_NM:C_NM + 384]
                for h in range(SH):
                    dve.wait_ge(S("z_ready"), SH * l + h + 1)
                    dve.wait_ge(S("aT_saved"), SEG_M[l][1])
                    dve.wait_ge(S("o_ready"), SEG_M[l][1])
                    link(V.scalar_tensor_tensor(zm[:, h, :], bank[h][:, 0:384], 0.125, nm, ALU.mult, ALU.add))
                    V.scalar_tensor_tensor(ln[:, h, :], zm[:, h, :], -1.0, zm[:, h, :], ALU.mult, ALU.min
                                           ).then_inc(S("nabs_ready"), 1)
                for h in range(SH):
                    dve.wait_ge(S("ln_ready"), SH * l + h + 1)
                    V.scalar_tensor_tensor(ln[:, h, :], zm[:, h, :], 0.0, ln[:, h, :], ALU.max, ALU.add
                                           ).then_inc(S("softplus_ready"), 1)
                for h in range(SH):
                    dve.wait_ge(S("later_ready"), SH * l + h + 1)
                    V.tensor_tensor(zm[:, h, :], zm[:, h, :], bank[h][:, 0:384], ALU.subtract
                                    ).then_inc(S("stick_log_ready"), 1)
                residual(3 + l if l == 0 else 4, 3, 1.0)
                norm(4 + 2 * l)
                dve.wait_ge(S("router_ready"), l + 1)
                bias = spread(gn[:, G_RB + 36 * l:G_RB + 36 * l + 36].rearrange("p (a n) -> p a n", a=1), 1, 2)
                link(V.tensor_tensor(rl[:, :, :], bank[0][:, 0:72].rearrange("p (t n) -> p t n", t=2), bias, ALU.add))
                gl = rl[:, :, 0:4]
                gmax = small[:, 0:2]
                bc = lambda v, n: spread(v.rearrange("p (t a) -> p t a", a=1), 2, n)
                v4 = lambda o: small[:, o:o + 8].rearrange("p (t g) -> p t g", t=2)
                link(V.tensor_reduce(gmax, gl, AX_X, ALU.max))
                V.tensor_tensor(v4(8), gl, bc(gmax, 4), ALU.subtract).then_inc(S("router_shifted"), 1)
                dve.wait_ge(S("router_shifted"), l + 1)

                fo = lambda n: spread(cst[:, C_FO:C_FO + n].rearrange("p (a n) -> p a n", a=1), 1, 2)

                def first_of(out, vals, top, n, tmp, tmp1):
                    link(V.tensor_tensor(out, vals, bc(top, n), ALU.is_equal))
                    link(V.tensor_tensor(tmp, out, fo(n), ALU.mult))
                    link(V.tensor_reduce(tmp1, tmp, AX_X, ALU.max))
                    link(V.tensor_tensor(out, tmp, bc(tmp1, n), ALU.is_equal))

                goh = v4(24)
                first_of(goh, gl, gmax, 4, v4(32), small[:, 2:4])
                el = rl[:, :, 4:36].rearrange("p t (g e) -> p t g e", g=4)
                tt = t48.rearrange("p t (g e) -> p t g e", g=4)
                goh8 = spread(goh.rearrange("p t (g a) -> p t g a", a=1), 3, 8)
                for t in range(2):
                    link(V.tensor_tensor(tt[:, t], el[:, t], goh8[:, t], ALU.mult))
                link(V.tensor_reduce(e8[:, :, :], t48.rearrange("p t (g e) -> p t e g", g=4), AX_X, ALU.add))
                v8 = lambda o: small[:, o:o + 16].rearrange("p (t g) -> p t g", t=2)
                o1, o2, tmp8, rest = v8(48), v8(64), v8(80), v8(96)
                l1, l2 = small[:, 4:6], small[:, 6:8]
                link(V.tensor_reduce(l1, e8[:, :, :], AX_X, ALU.max))
                first_of(o1, e8[:, :, :], l1, 8, tmp8, small[:, 42:44])
                link(V.scalar_tensor_tensor(rest, o1, NEG, e8[:, :, :], ALU.mult, ALU.add))
                link(V.tensor_reduce(l2, rest, AX_X, ALU.max))
                first_of(o2, rest, l2, 8, tmp8, small[:, 42:44])
                V.tensor_tensor(small[:, 40:42], l2, l1, ALU.subtract).then_inc(S("router_gap"), 1)
                dve.wait_ge(S("router_exp1"), l + 1)
                dve.wait_ge(S("router_gap"), l + 1)
                psel, den = small[:, 112:114], small[:, 114:116]
                link(V.tensor_reduce(psel, v4(16), AX_X, ALU.add))
                dve.wait_ge(S("router_exp2"), l + 1)
                e2 = small[:, 44:46]
                link(V.scalar_tensor_tensor(den, e2, 1.0, psel, ALU.add, ALU.mult))
                w1, w2 = small[:, 116:118], small[:, 118:120]
                link(V.reciprocal(w1, den))
                link(V.tensor_tensor(w2, w1, e2, ALU.mult))
                link(V.tensor_tensor(v8(80), o1, o2, ALU.add))
                for t in range(2):
                    ins = V.tensor_tensor(sel[:, t, :].rearrange("p (g e) -> p g e", g=4), goh8[:, t],
                                          spread(v8(80)[:, t:t + 1, :], 1, 4), ALU.mult)
                    if t == 0:
                        link(ins)
                ins.then_inc(S("sel_ready"), 1)
                dve.wait_ge(S("sel_ready"), l + 1)
                link(V.tensor_tensor(o1, o1, bc(w1, 8), ALU.mult))
                link(V.tensor_tensor(o2, o2, bc(w2, 8), ALU.mult))
                link(V.tensor_tensor(o1, o1, o2, ALU.add))
                for t in range(2):
                    inner = spread(o1[:, t:t + 1, :], 1, 4)
                    ins = V.tensor_tensor(comb[:, t, :].rearrange("p (g e) -> p g e", g=4), goh8[:, t], inner, ALU.mult)
                    if t == 0:
                        link(ins)
                ins.then_inc(S("comb_ready"), 1)

                dve.wait_ge(S("comb_ready"), l + 1)
                dve.wait_ge(S("places_psum"), l + 1)
                link(V.scalar_tensor_tensor(posm[:, :, :], bank[1][:, 0:2 * NE].rearrange("p (t e) -> p t e", t=2), 1.0,
                                            sel[:, :, :], ALU.add, ALU.mult))
                link(V.tensor_scalar(posm[:, :, :], posm[:, :, :], -1.0, None, ALU.add))
                link(V.tensor_reduce(load[:, :], bank[1][:, 2 * NE:3 * NE], AX_X, ALU.max))
                V.tensor_copy(load_i[:, :], load[:, :]).then_inc(S("load_known"), 1)
                for b in range(4):
                    half = slice(512 * (b % 2), 512 * (b % 2) + 512)
                    dve.wait_ge(S("x_hi_ready"), 4 * (l + 2) + b + 1)
                    V.tensor_tensor(x_lo[:, b // 2, half], bank[2 + b][:, :], x_hi[:, b // 2, half].bitcast(F32),
                                    ALU.subtract).then_inc(S("x_lo_ready"), 1)

                def hidden(e, p, first):
                    dve.wait_ge(S(f"moe_silu_ready{l}"), e + 1)
                    dve.wait_ge(S("moe_up_ready"), e + (NE * l + 1))
                    V.tensor_tensor(um[:, :], silm[:, p, :], bank[5 + 2 * p][:, :], ALU.mult
                                    ).then_inc(S(f"moe_product{l}"), 1)
                    dve.wait_ge(S(f"moe_product{l}"), e + 1)
                    if not first:
                        dve.wait_ge(S("moe_down_used"), e + (NE * l - 1))
                    c = spread(comb_bc[:, bass.ds(e, 1), :], 1, 2)
                    V.tensor_tensor(hm[:, p, :].rearrange("p (f n) -> p f n", f=2), um.rearrange("p (f n) -> p f n", f=2),
                                    c, ALU.mult).then_inc(S(f"moe_hid_ready{l}"), 1)
                    dve.wait_ge(S(f"moe_hid_ready{l}"), e + 1)

                def pair_cols(v, s):
                    v = v[:, :, bass.ds(s * 2, 2)].rearrange("p t (e a) -> p t e a", a=1)
                    return spread(v, 3, CAP)

                def by_expert(v):
                    return v.rearrange("p t (e c) -> p t e c", e=2)

                def make_slots(s, p, first=False):
                    if not first:
                        dve.wait_ge(S(f"slots_turned{l}"), s - 1)
                    io = cst[:, C_IO:C_IO + CAP].rearrange("p (a b c) -> p a b c", a=1, b=1)
                    V.tensor_tensor(by_expert(slots[:, p, :, :]), spread(spread(io, 1, 2), 2, 2), pair_cols(posm, s),
                                    ALU.is_equal).then_inc(S(f"slots_ready{l}"), 1)

                def weigh_slots(s, p, first=False):
                    if not first:
                        dve.wait_ge(S(f"slots_turned{l}"), s)
                    dve.wait_ge(S(f"slots_ready{l}"), s + 1)
                    V.tensor_tensor(by_expert(slotw[:, :, :]), by_expert(slots[:, p, :, :].bitcast(F32)),
                                    pair_cols(comb, s), ALU.mult).then_inc(S(f"slotw_ready{l}"), 1)

                def low(s):
                    dve.wait_ge(S(f"o_hi_ready{l}"), s + 1)
                    for half in range(2):
                        c = slice(512 * half, 512 * half + 512)
                        ins = V.scalar_tensor_tensor(o_lo[:, c], bank[4 + half][:, :], wslot[:, 0:1],
                                                     o_hi[:, c].bitcast(F32), ALU.mult, ALU.subtract)
                    ins.then_inc(S(f"o_lo_ready{l}"), 1)

                def product(s, first=False):
                    dve.wait_ge(S(f"moe_silu_ready{l}"), s + 1)
                    dve.wait_ge(S("moe_up_ready"), s * 2 + (NE * l + 2))
                    if not first:
                        dve.wait_ge(S(f"hidden_turned{l}"), s)
                    V.tensor_tensor(hp[:, :], sl[:, :], bank[6][:, 256:512], ALU.mult
                                    ).then_inc(S(f"moe_product{l}"), 1)

                def save_gathered(s):
                    dve.wait_ge(S(f"gathered{l}"), s * 2 + 2)
                    V.tensor_copy(xg[:, 4:8, :], bank[5].rearrange("p (k n) -> p k n", k=4)
                                  ).then_inc(S(f"xg_high_ready{l}"), 1)

                dve.wait_ge(S("load_known"), l + 1)
                with dve.If(dve.value_load(load_i[0:1, 0:1]) > CAP):
                    dve.wait_ge(S(f"comb_loaded{l}"), 16)
                    hidden(0, 0, True)
                    hidden(1, 1, True)
                    with dve.Fori(1, PAIRS) as i:
                        for p in range(2):
                            hidden(i * 2 + p, p, False)
                with dve.Else():
                    make_slots(0, 0, True)
                    make_slots(1, 1, True)
                    weigh_slots(0, 0, True)
                    save_gathered(0)
                    product(0, True)
                    save_gathered(1)

                    def step(s, p):
                        make_slots(s + 2, p)
                        weigh_slots(s + 1, 1 - p)
                        low(s)
                        product(s + 1)
                        save_gathered(s + 2)

                    with dve.Fori(0, PAIRS // 2 - 1) as i:
                        for p in range(2):
                            step(i * 2 + p, p)
                    weigh_slots(PAIRS - 1, 1)
                    low(PAIRS - 2)
                    product(PAIRS - 1)
                    low(PAIRS - 1)
                dve.wait_ge(S("experts_done"), l + 1)
                for d in range(KT):
                    h = hT[:, d, NMETA:T1]
                    V.tensor_tensor(h, bank[d // 2][:, T2 * (d % 2):T2 * (d % 2) + T2], h, ALU.add
                                    ).then_inc(S("residual_ready"), 1)
            norm(7)


def _chunks(w):
    n = w.shape[1]
    return w.reshape(KT, P, n // 256, 256).transpose(2, 1, 0, 3).reshape(n // 256, P, CH)


def _row_chunks(w):
    n = w.shape[0]
    return w.reshape(n // 256, 2, P, D).transpose(0, 2, 1, 3).reshape(n // 256, P, CH)


def _pad_cols(w, n):
    return np.concatenate([w, np.zeros((w.shape[0], n - w.shape[1]), w.dtype)], axis=1)


def _pairs(a, b):
    return np.stack([a, b], axis=1).reshape(-1, P, CH)


def _layout(i):
    col = lambda v: np.ascontiguousarray(v.reshape(-1, P).T)
    parts = []
    for f in ("ffn1", "ffn2"):
        gu = _pairs(_chunks(i[f + "_w_gate"][0]), _chunks(i[f + "_w_up"][0]))
        parts.append([gu, _row_chunks(i[f + "_w_down"][0])])
    w_in = i["w_in"][0]
    first_in = np.concatenate([w_in[:, 0:2816], _pad_cols(w_in[:, 2816:2888], 256)], axis=1)
    stream = parts[0] + [_chunks(first_in), _row_chunks(i["w_out"][0])] + parts[1]
    small2 = []
    for l in range(LAYERS):
        w = i["w_in_2"][l]
        w = np.concatenate([w[:, 0:256], _pad_cols(w[:, 256:416], 256), w[:, 416:1440]], axis=1)
        stream += [_chunks(w), _row_chunks(i["w_out_2"][l])]
        g, u, d = (i[k][l].reshape(NE, -1, i[k].shape[-1]) for k in ("w_gate_2", "w_up_2", "w_down_2"))
        g, u = (a.reshape(NE, KT, P, 256).transpose(0, 2, 1, 3).reshape(NE, P, CH) for a in (g, u))
        d = d.reshape(NE, 2, P, D).transpose(0, 2, 1, 3).reshape(NE, P, CH)
        stream.append(np.stack([g[0::2], g[1::2], u[0::2], u[1::2], d[0::2], d[1::2]], axis=1).reshape(3 * NE, P, CH))
        wp = np.zeros((P, 2, P), np.float32)
        for t in range(2):
            for j in range(2):
                wp[64 * j:64 * j + 64, t, 64 * j:64 * j + 64] = i["pool_w_2"][l][2 * t + j]
        rt = np.concatenate([i["w_group_2"][l], i["w_expert_2"][l]], axis=1)
        small2.append(np.concatenate([
            i["w_uq_2"][l].reshape(2, P, 768).transpose(1, 0, 2).reshape(P, -1),
            i["w_ukv_2"][l].reshape(P, -1),
            wp.reshape(P, -1),
            rt.reshape(KT, P, 36).transpose(1, 0, 2).reshape(P, -1)], axis=1))
    norms = [i["ffn1_norm"][0], i["mix_norm"][0], i["ffn2_norm"][0]]
    for l in range(LAYERS):
        norms += [i["norm1_g_2"][l], i["norm2_g_2"][l]]
    norms.append(i["final_g_2"])
    twice = lambda v: np.concatenate([v, v]).reshape(P, 1)
    rows = [i[f"a_lambda_{k}"][0] for k in ("q1", "k1", "q2", "k2")]
    for l in range(LAYERS):
        rows += [i["b_group_2"][l], i["b_expert_2"][l]]
    gains = [col(v) for v in norms] + [twice(i["a_q_norm"][0]), twice(i["a_k_norm"][0]), col(i["b_kv_norm"][0]),
                                       col(i["b_q_norm"][0]), col(i["a_subln"][0])]
    gains += [col(i["q_norm_g_2"][l]) for l in range(LAYERS)] + [col(i["kv_norm_g_2"][l]) for l in range(LAYERS)]
    gains += [col(i["pool_scale_2"][l]) for l in range(LAYERS)]
    gains.append(np.broadcast_to(np.concatenate(rows)[None], (P, 4 * ADK + LAYERS * 36)))
    gains.append(np.broadcast_to(np.array([w * EPS for w in EPS_AT], np.float32), (P, len(EPS_AT))))
    return {
        "stream": np.concatenate(stream),
        "gains": np.concatenate(gains, axis=1),
        "consts": constants()[0],
        "bias_consts": constants()[1],
        "x_tok": np.concatenate([i["meta_tokens"], i["x"][0]]),
        "rel_bias": i["rel_bias"],
        "wuk": i["b_w_uk"][0].transpose(1, 0, 2),
        "wuv": i["b_w_uv"][0].reshape(4, 2, P, P).transpose(2, 0, 1, 3),
        "small2": np.stack(small2),
    }


def kernel(**inputs):
    import concourse.bacc as bacc
    from concourse.bass_utils import run_bass_kernel_spmd

    nc = bacc.Bacc("TRN2", target_bir_lowering=False, num_devices=1)
    arrays, args = {}, []
    for name, a in _layout({k: np.asarray(v) for k, v in inputs.items()}).items():
        a = np.ascontiguousarray(a)
        arrays[f"in_{name}"] = a
        args.append(nc.dram_tensor(f"in_{name}", a.shape, mybir.dt.from_np(a.dtype), kind="ExternalInput").ap())
    out = nc.dram_tensor("out", (1, SEQ, D), F32, kind="ExternalOutput").ap()
    build(nc, *args, out)
    r = run_bass_kernel_spmd(nc, [arrays], core_ids=[0])
    return r.results[0]["out"]
```
